# Optimizing a Trainium2 kernel written in Bass

```python
import math
import jax
import jax.numpy as jnp
from jax import lax
import numpy as np

D_MODEL = 1024
BATCH = 1
SEQ = 512
DEPTH = 2

PLE_DIM = 256
D_FF = 2816
ROPE_THETA = 10000.0
EPS = 1e-6
NEG = -1e30
Q_BLOCK = 128

S5_WIDTH = 512
S5_GROUP = 16
S5_GROUPS = S5_WIDTH // S5_GROUP
S5_STATE = 64

NSA_HEADS = 8
NSA_KV_HEADS = 2
NSA_GQA = NSA_HEADS // NSA_KV_HEADS
NSA_HEAD_DIM = 64
CMP_LEN = 32
CMP_STRIDE = 16
SEL_BLOCK = 64
SEL_TOP = 16
WINDOW = 512
FORCE_BONUS = 1000.0
NSA_Q = NSA_HEADS * NSA_HEAD_DIM
NSA_KV = NSA_KV_HEADS * NSA_HEAD_DIM
EVEN_SIZES = (S5_WIDTH, NSA_Q, NSA_KV, NSA_KV, NSA_KV, NSA_KV, NSA_KV, NSA_KV, 3 * NSA_HEADS)
EVEN_IN = sum(EVEN_SIZES)
EVEN_MIX = S5_WIDTH + NSA_Q

MLA_HEADS = 16
MLA_LATENT = 256
MLA_ROPE = 32
MLA_V_DIM = 64
IDX_HEADS = 8
IDX_DIM = 64
DSA_TOP = 256
ODD_SIZES = (MLA_HEADS * MLA_LATENT, MLA_HEADS * MLA_ROPE, MLA_LATENT, MLA_ROPE, IDX_HEADS * IDX_DIM, IDX_DIM, IDX_HEADS)
ODD_IN = sum(ODD_SIZES)
ODD_MIX = MLA_HEADS * MLA_V_DIM

kernel_name = "hybrid_s5_nsa_dsa_macaron_trunk"

def rms_norm(t, g):
    tf = t.astype(jnp.float32)
    y = tf * lax.rsqrt(jnp.mean(tf * tf, axis=-1, keepdims=True) + EPS)
    return (y * g.astype(jnp.float32)).astype(t.dtype)

def rope(t, pos):
    half = t.shape[-1] // 2
    inv = ROPE_THETA ** (-jnp.arange(half, dtype=jnp.float32) / half)
    ang = pos.astype(jnp.float32)[:, None] * inv[None, :]
    cos = jnp.cos(ang)[:, None, :]
    sin = jnp.sin(ang)[:, None, :]
    tf = t.astype(jnp.float32)
    t1, t2 = tf[..., :half], tf[..., half:]
    return jnp.concatenate([t1 * cos - t2 * sin, t2 * cos + t1 * sin], axis=-1).astype(t.dtype)

def masked_softmax(s, mask):
    return jax.nn.softmax(jnp.where(mask, s.astype(jnp.float32), NEG), axis=-1)

def swiglu(t, w_in, w_out):
    g, u = jnp.split(t @ w_in, 2, axis=-1)
    return (jax.nn.silu(g) * u) @ w_out

def _split(z, sizes):
    cuts = [int(c) for c in np.cumsum(sizes)[:-1]]
    return jnp.split(z, cuts, axis=-1)

def _linear_recurrence(c1, c2):
    a1, b1 = c1
    a2, b2 = c2
    return a1 * a2, a2 * b1 + b2

def s5_mixer(u, a_re, a_im, b_re, b_im, c_re, c_im, log_dt, d_skip, w_glu):
    f32 = jnp.float32
    bsz, seq_len, _ = u.shape
    uf = u.astype(f32)
    ug = uf.reshape(bsz, seq_len, S5_GROUPS, S5_GROUP)
    lam = lax.complex(a_re.astype(f32), a_im.astype(f32))
    dt = jnp.exp(log_dt.astype(f32))[:, None]
    lam_bar = jnp.exp(lam * dt)
    b_bar = ((lam_bar - 1.0) / lam)[..., None] * lax.complex(b_re.astype(f32), b_im.astype(f32))
    bu = jnp.einsum('blgp,gnp->blgn', ug.astype(jnp.complex64), b_bar)
    a = jnp.broadcast_to(lam_bar, (1, seq_len) + lam_bar.shape)
    _, states = lax.associative_scan(_linear_recurrence, (a, bu), axis=1)
    y = (jnp.einsum('blgn,gpn->blgp', states.real, c_re.astype(f32))
         - jnp.einsum('blgn,gpn->blgp', states.imag, c_im.astype(f32)))
    y = y.reshape(bsz, seq_len, S5_WIDTH) + d_skip.astype(f32) * uf
    z = jax.nn.gelu(y)
    z = z * jax.nn.sigmoid(z @ w_glu.astype(f32))
    return z.astype(u.dtype)

def nsa_mixer(q, kc, vc, ks, vs, kw, vw, gates, pe_k, pe_v, wk1, wk2, wv1, wv2):
    bsz, seq_len = q.shape[0], q.shape[1]
    n_cmp = (seq_len - CMP_LEN) // CMP_STRIDE + 1
    n_sb = seq_len // SEL_BLOCK
    top_n = min(SEL_TOP, n_sb)
    n_sel = top_n * SEL_BLOCK
    scale = NSA_HEAD_DIM ** -0.5
    cidx = jnp.arange(n_cmp)[:, None] * CMP_STRIDE + jnp.arange(CMP_LEN)[None, :]

    def compress(t, pe, w1, w2):
        blk = t[:, cidx] + pe[:, None, :]
        blk = blk.transpose(0, 1, 3, 2, 4).reshape(bsz, n_cmp, NSA_KV_HEADS, CMP_LEN * NSA_HEAD_DIM)
        return jax.nn.gelu(blk @ w1) @ w2

    k_cmp = compress(kc, pe_k, wk1, wk2)
    v_cmp = compress(vc, pe_v, wv1, wv2)
    cmp_start = jnp.arange(n_cmp) * CMP_STRIDE
    cmp_last = cmp_start + CMP_LEN - 1
    sb_ids = jnp.arange(n_sb)
    sb_start = sb_ids * SEL_BLOCK
    overlap = ((cmp_start[:, None] < sb_start[None, :] + SEL_BLOCK)
               & (cmp_start[:, None] + CMP_LEN > sb_start[None, :])).astype(jnp.float32)
    k_sb = ks.reshape(bsz, n_sb, SEL_BLOCK, NSA_KV_HEADS, NSA_HEAD_DIM).transpose(0, 3, 1, 2, 4)
    v_sb = vs.reshape(bsz, n_sb, SEL_BLOCK, NSA_KV_HEADS, NSA_HEAD_DIM).transpose(0, 3, 1, 2, 4)
    kw_pad = jnp.pad(kw, ((0, 0), (WINDOW, 0), (0, 0), (0, 0)))
    vw_pad = jnp.pad(vw, ((0, 0), (WINDOW, 0), (0, 0), (0, 0)))
    qg = q.reshape(bsz, seq_len, NSA_KV_HEADS, NSA_GQA, NSA_HEAD_DIM)
    gg = gates.reshape(bsz, seq_len, NSA_KV_HEADS, NSA_GQA, 3)
    b_ix = jnp.arange(bsz)[:, None, None, None]
    h_ix = jnp.arange(NSA_KV_HEADS)[None, :, None, None]

    def block(i):
        s0 = i * Q_BLOCK
        t_pos = s0 + jnp.arange(Q_BLOCK)
        qb = lax.dynamic_slice_in_dim(qg, s0, Q_BLOCK, axis=1)
        gb = lax.dynamic_slice_in_dim(gg, s0, Q_BLOCK, axis=1)
        m_c = cmp_last[None, :] <= t_pos[:, None]
        p_c = masked_softmax(jnp.einsum('bqhgd,bchd->bhgqc', qb, k_cmp) * scale, m_c) * m_c
        o_c = jnp.einsum('bhgqc,bchd->bqhgd', p_c.astype(v_cmp.dtype), v_cmp)
        imp = jnp.einsum('bhgqc,cs->bhqs', p_c, overlap)
        cur = (t_pos // SEL_BLOCK)[:, None]
        forced = (sb_ids[None, :] == 0) | (sb_ids[None, :] == cur) | (sb_ids[None, :] == cur - 1)
        imp = imp + FORCE_BONUS * forced
        imp = jnp.where(sb_start[None, :] <= t_pos[:, None], imp, NEG)
        _, sel = lax.top_k(imp, top_n)
        k_sel = k_sb[b_ix, h_ix, sel].reshape(bsz, NSA_KV_HEADS, Q_BLOCK, n_sel, NSA_HEAD_DIM)
        v_sel = v_sb[b_ix, h_ix, sel].reshape(bsz, NSA_KV_HEADS, Q_BLOCK, n_sel, NSA_HEAD_DIM)
        k_pos = (sel[..., None] * SEL_BLOCK + jnp.arange(SEL_BLOCK)).reshape(bsz, NSA_KV_HEADS, Q_BLOCK, n_sel)
        m_s = (k_pos <= t_pos[None, None, :, None])[:, :, None]
        p_s = masked_softmax(jnp.einsum('bqhgd,bhqkd->bhgqk', qb, k_sel) * scale, m_s)
        o_s = jnp.einsum('bhgqk,bhqkd->bqhgd', p_s.astype(v_sel.dtype), v_sel)
        kwb = lax.dynamic_slice_in_dim(kw_pad, s0, WINDOW + Q_BLOCK, axis=1)
        vwb = lax.dynamic_slice_in_dim(vw_pad, s0, WINDOW + Q_BLOCK, axis=1)
        s_pos = s0 - WINDOW + jnp.arange(WINDOW + Q_BLOCK)
        diff = t_pos[:, None] - s_pos[None, :]
        m_w = (diff >= 0) & (diff < WINDOW) & (s_pos[None, :] >= 0)
        p_w = masked_softmax(jnp.einsum('bqhgd,bkhd->bhgqk', qb, kwb) * scale, m_w)
        o_w = jnp.einsum('bhgqk,bkhd->bqhgd', p_w.astype(vwb.dtype), vwb)
        return gb[..., 0:1] * o_c + gb[..., 1:2] * o_s + gb[..., 2:3] * o_w

    out = lax.map(block, jnp.arange(seq_len // Q_BLOCK))
    return out.transpose(1, 0, 2, 3, 4, 5).reshape(bsz, seq_len, NSA_Q)

def dsa_mixer(q_lat, q_rope, c_kv, k_rope, q_idx, k_idx, w_idx, w_uv):
    bsz, seq_len = q_lat.shape[0], q_lat.shape[1]
    top = min(DSA_TOP, seq_len // 4)
    scale = (MLA_LATENT + MLA_ROPE) ** -0.5
    idx_scale = IDX_DIM ** -0.5
    w_scale = IDX_HEADS ** -0.5
    key_pos = jnp.arange(seq_len)
    b_ix = jnp.arange(bsz)[:, None, None]

    def block(i):
        s0 = i * Q_BLOCK
        t_pos = s0 + jnp.arange(Q_BLOCK)
        qi = lax.dynamic_slice_in_dim(q_idx, s0, Q_BLOCK, axis=1)
        wi = lax.dynamic_slice_in_dim(w_idx, s0, Q_BLOCK, axis=1)
        dots = jax.nn.relu(jnp.einsum('bqhd,bsd->bqhs', qi, k_idx).astype(jnp.float32) * idx_scale)
        score = jnp.einsum('bqh,bqhs->bqs', wi.astype(jnp.float32) * w_scale, dots)
        score = jnp.where(key_pos[None, :] <= t_pos[:, None], score, NEG)
        _, sel = lax.top_k(score, top)
        ck = c_kv[b_ix, sel]
        kr = k_rope[b_ix, sel]
        m = (sel <= t_pos[None, :, None])[:, :, None, :]
        ql = lax.dynamic_slice_in_dim(q_lat, s0, Q_BLOCK, axis=1)
        qr = lax.dynamic_slice_in_dim(q_rope, s0, Q_BLOCK, axis=1)
        s = (jnp.einsum('bqhr,bqkr->bqhk', ql, ck) + jnp.einsum('bqhe,bqke->bqhk', qr, kr)) * scale
        p = masked_softmax(s, m)
        o = jnp.einsum('bqhk,bqkr->bqhr', p.astype(ck.dtype), ck)
        return jnp.einsum('bqhr,hrv->bqhv', o, w_uv)

    out = lax.map(block, jnp.arange(seq_len // Q_BLOCK))
    return out.transpose(1, 0, 2, 3, 4).reshape(bsz, seq_len, ODD_MIX)

def even_mixer(hn, pos, w_in, w_out, a_re, a_im, b_re, b_im, c_re, c_im, log_dt, d_skip, w_glu,
               pe_k, pe_v, wk1, wk2, wv1, wv2):
    bsz, seq_len, _ = hn.shape
    u, q, kc, vc, ks, vs, kw, vw, gt = _split(hn @ w_in, EVEN_SIZES)
    q = rope(q.reshape(bsz, seq_len, NSA_HEADS, NSA_HEAD_DIM), pos)
    kv_shape = (bsz, seq_len, NSA_KV_HEADS, NSA_HEAD_DIM)
    kc = rope(kc.reshape(kv_shape), pos)
    ks = rope(ks.reshape(kv_shape), pos)
    kw = rope(kw.reshape(kv_shape), pos)
    gates = jax.nn.sigmoid(gt.reshape(bsz, seq_len, NSA_HEADS, 3))
    a_out = s5_mixer(u, a_re, a_im, b_re, b_im, c_re, c_im, log_dt, d_skip, w_glu)
    b_out = nsa_mixer(q, kc, vc.reshape(kv_shape), ks, vs.reshape(kv_shape), kw, vw.reshape(kv_shape),
                      gates, pe_k, pe_v, wk1, wk2, wv1, wv2)
    return jnp.concatenate([a_out, b_out], axis=-1) @ w_out

def odd_mixer(hn, pos, w_in, kv_norm, w_uv, w_out):
    bsz, seq_len, _ = hn.shape
    q_lat, q_rope, c_kv, k_rope, q_idx, k_idx, w_idx = _split(hn @ w_in, ODD_SIZES)
    q_lat = q_lat.reshape(bsz, seq_len, MLA_HEADS, MLA_LATENT)
    q_rope = rope(q_rope.reshape(bsz, seq_len, MLA_HEADS, MLA_ROPE), pos)
    c_kv = rms_norm(c_kv, kv_norm)
    k_rope = rope(k_rope[:, :, None, :], pos)[:, :, 0, :]
    q_idx = rope(q_idx.reshape(bsz, seq_len, IDX_HEADS, IDX_DIM), pos)
    k_idx = rope(k_idx[:, :, None, :], pos)[:, :, 0, :]
    o = dsa_mixer(q_lat, q_rope, c_kv, k_rope, q_idx, k_idx, w_idx, w_uv)
    return o @ w_out

def setup_inputs(seed: int = 0) -> dict:
    key = jax.random.key(seed)
    ks = jax.random.split(key, 32)
    n_even = (DEPTH + 1) // 2
    n_odd = DEPTH // 2
    nrm = jax.random.normal
    f32 = jnp.float32

    def w(k, shape, fan_in):
        return nrm(k, shape, f32) * (fan_in ** -0.5)

    n_idx = jnp.arange(S5_STATE, dtype=f32)
    return {
        "x": nrm(ks[0], (BATCH, SEQ, D_MODEL), f32),
        "p": nrm(ks[1], (DEPTH, BATCH, SEQ, PLE_DIM), f32),
        "norm_g": 1.0 + 0.02 * nrm(ks[2], (DEPTH, 8, D_MODEL), f32),
        "ffn1_w_in": w(ks[3], (DEPTH, D_MODEL, 2 * D_FF), D_MODEL),
        "ffn1_w_out": w(ks[4], (DEPTH, D_FF, D_MODEL), D_FF),
        "ffn2_w_in": w(ks[5], (DEPTH, D_MODEL, 2 * D_FF), D_MODEL),
        "ffn2_w_out": w(ks[6], (DEPTH, D_FF, D_MODEL), D_FF),
        "ple_w_gate": w(ks[7], (DEPTH, D_MODEL, D_MODEL), D_MODEL),
        "ple_w_proj": w(ks[8], (DEPTH, PLE_DIM, D_MODEL), PLE_DIM),
        "ev_w_in": w(ks[9], (n_even, D_MODEL, EVEN_IN), D_MODEL),
        "ev_w_out": w(ks[10], (n_even, EVEN_MIX, D_MODEL), EVEN_MIX),
        "s5_a_re": -0.5 + 0.01 * nrm(ks[11], (n_even, S5_GROUPS, S5_STATE), f32),
        "s5_a_im": math.pi * n_idx + 0.01 * nrm(ks[12], (n_even, S5_GROUPS, S5_STATE), f32),
        "s5_b_re": w(ks[13], (n_even, S5_GROUPS, S5_STATE, S5_GROUP), 2 * S5_GROUP),
        "s5_b_im": w(ks[14], (n_even, S5_GROUPS, S5_STATE, S5_GROUP), 2 * S5_GROUP),
        "s5_c_re": w(ks[15], (n_even, S5_GROUPS, S5_GROUP, S5_STATE), 2 * S5_STATE),
        "s5_c_im": w(ks[16], (n_even, S5_GROUPS, S5_GROUP, S5_STATE), 2 * S5_STATE),
        "s5_log_dt": jax.random.uniform(ks[17], (n_even, S5_GROUPS), f32, math.log(1e-3), math.log(1e-1)),
        "s5_d": nrm(ks[18], (n_even, S5_WIDTH), f32),
        "s5_w_glu": w(ks[19], (n_even, S5_WIDTH, S5_WIDTH), S5_WIDTH),
        "nsa_pe_k": 0.1 * nrm(ks[20], (n_even, CMP_LEN, NSA_HEAD_DIM), f32),
        "nsa_pe_v": 0.1 * nrm(ks[21], (n_even, CMP_LEN, NSA_HEAD_DIM), f32),
        "nsa_wk1": w(ks[22], (n_even, CMP_LEN * NSA_HEAD_DIM, NSA_HEAD_DIM), CMP_LEN * NSA_HEAD_DIM),
        "nsa_wk2": w(ks[23], (n_even, NSA_HEAD_DIM, NSA_HEAD_DIM), NSA_HEAD_DIM),
        "nsa_wv1": w(ks[24], (n_even, CMP_LEN * NSA_HEAD_DIM, NSA_HEAD_DIM), CMP_LEN * NSA_HEAD_DIM),
        "nsa_wv2": w(ks[25], (n_even, NSA_HEAD_DIM, NSA_HEAD_DIM), NSA_HEAD_DIM),
        "od_w_in": w(ks[26], (n_odd, D_MODEL, ODD_IN), D_MODEL),
        "od_kv_norm": 1.0 + 0.02 * nrm(ks[27], (n_odd, MLA_LATENT), f32),
        "od_w_uv": w(ks[28], (n_odd, MLA_HEADS, MLA_LATENT, MLA_V_DIM), MLA_LATENT),
        "od_w_out": w(ks[29], (n_odd, ODD_MIX, D_MODEL), ODD_MIX),
    }

def reference(x, p, norm_g, ffn1_w_in, ffn1_w_out, ffn2_w_in, ffn2_w_out, ple_w_gate, ple_w_proj,
              ev_w_in, ev_w_out, s5_a_re, s5_a_im, s5_b_re, s5_b_im, s5_c_re, s5_c_im, s5_log_dt, s5_d, s5_w_glu,
              nsa_pe_k, nsa_pe_v, nsa_wk1, nsa_wk2, nsa_wv1, nsa_wv2,
              od_w_in, od_kv_norm, od_w_uv, od_w_out):
    seq_len = x.shape[1]
    pos = jnp.arange(seq_len)
    h = x
    for i in range(DEPTH):
        g = norm_g[i]
        j = i // 2
        h = h + 0.5 * rms_norm(swiglu(rms_norm(h, g[0]), ffn1_w_in[i], ffn1_w_out[i]), g[1])
        hn = rms_norm(h, g[2])
        if i % 2 == 0:
            mix = even_mixer(hn, pos, ev_w_in[j], ev_w_out[j], s5_a_re[j], s5_a_im[j], s5_b_re[j], s5_b_im[j],
                             s5_c_re[j], s5_c_im[j], s5_log_dt[j], s5_d[j], s5_w_glu[j],
                             nsa_pe_k[j], nsa_pe_v[j], nsa_wk1[j], nsa_wk2[j], nsa_wv1[j], nsa_wv2[j])
        else:
            mix = odd_mixer(hn, pos, od_w_in[j], od_kv_norm[j], od_w_uv[j], od_w_out[j])
        h = h + rms_norm(mix, g[3])
        h = h + 0.5 * rms_norm(swiglu(rms_norm(h, g[4]), ffn2_w_in[i], ffn2_w_out[i]), g[5])
        gate = jax.nn.sigmoid(rms_norm(h, g[6]) @ ple_w_gate[i])
        h = h + rms_norm((p[i] @ ple_w_proj[i]) * gate, g[7])
    return h


_drawn_inputs = setup_inputs


def setup_inputs(seed=0):
    import zlib

    import numpy as np

    out = dict(_drawn_inputs(seed))
    spreads = {}
    factors = {'s5_a_re': 64.0, 'nsa_pe_k': 3.523, 'od_kv_norm': 16.372}
    for name, (base, spread) in spreads.items():
        noise = np.random.default_rng([zlib.crc32(name.encode()), seed]).standard_normal(out[name].shape)
        drawn = base * np.exp(spread * noise) if base else spread * noise
        out[name] = jnp.asarray(drawn.astype(out[name].dtype))
    for name, factor in factors.items():
        out[name] = (out[name] * factor).astype(out[name].dtype)
    return out
```

```python
from contextlib import ExitStack, contextmanager

import numpy as np

import concourse.bass as bass
from concourse import mybir

F32 = mybir.dt.float32
BF16 = mybir.dt.bfloat16
ALU = mybir.AluOpType
ACT = mybir.ActivationFunctionType
AX = mybir.AxisListType

P = 128
T = 512
D = 1024
DC = D // P
FF = 2816
FC = FF // P
EPS = 1e-6
SLOTS = 4
SLOT = FC * P
BANKS = 4
TT = T // P
NEG = -1e30
HD = 64
STATES = 64
PAIRS = 16
GELU = 2 * (2 / np.pi) ** 0.5
POW = 9
TM = 2 * P + 24
LATENT = 256
HEADS = 16
IDX_HEADS = 8
TOP = T // 4
ROUNDS = TOP // 8
LOW = -3e38
DSA_SCALE = 288 ** -0.5
CMP = 31
CMP_STRIDE = 16
CMP_LEN = 32
MAGIC = 12582912.0
TWO_PI_HI = 6.28125
TWO_PI_LO = 2 * np.pi - 6.28125
PI_IN = 3.1415925

def plan_of():
    steps = []
    for layer in range(2):
        g = 8 * layer
        steps += [("norm_in", g), ("ffn", 2 * layer), ("norm_out", g + 1, 0.5),
                  ("norm_in", g + 2), ("even", 0) if layer == 0 else ("odd", 0), ("norm_out", g + 3, 1.0),
                  ("norm_in", g + 4), ("ffn", 2 * layer + 1), ("norm_out", g + 5, 0.5),
                  ("norm_in", g + 6), ("ple", layer), ("norm_out", g + 7, 1.0)]
    return steps


class Steps:

    def __init__(self, engine, semaphore, start=0):
        self.engine, self.semaphore, self.n, self.local = engine, semaphore, start, 0

    def by(self, instruction, k=1):
        instruction.then_inc(self.semaphore, k)
        self.n, self.local = self.n + k, self.local + k
        return self

    def past(self, k=1):
        self.n, self.local = self.n + k, self.local + k
        return self

    def wait(self, back=0):
        self.engine.wait_ge(self.semaphore, self.n - back)
        return self


@contextmanager
def looped(engine, trips, per):
    at = {s: s.n for s in per}
    with engine.Fori(0, trips) as i:
        for s, k in per.items():
            s.n, s.local = i * k + s.n, 0
        yield i
    for s, k in per.items():
        assert s.local == k, (s.semaphore, s.local, k)
        s.n = at[s] + trips * k


def streams_of(plan):
    out = []
    for step in plan:
        kind, n = step[0], step[1]
        if kind == "ffn":
            out += [("ffn_in", n * FC, FC, DC * 2 * P, 2), ("ffn_out", n * DC, DC, FC * P, 1)]
        elif kind == "even":
            out += [("even_in", 0, 6, DC * 2 * P, 2), ("even_tm", 0, 1, DC * TM, TT),
                    ("s5_glu", 0, 1, 4 * T, 4), ("even_out", 0, 4, DC * 2 * P, 2)]
        elif kind == "odd":
            out += [("odd_in", 0, 6, DC * 2 * P, 2), ("w_uv", 0, 1, 2 * D, 8),
                    ("q_lat", 0, HEADS, DC * 2 * P, 2), ("odd_out", 0, 4, DC * 2 * P, 2)]
        elif kind == "ple":
            out += [("ple_gate", n * DC // 2, DC // 2, DC * 2 * P, 2), ("ple_proj", n, 1, 2 * D, 8)]
    return out


def trunk(nc, ap):
    plan = plan_of()
    streams = streams_of(plan)
    with ExitStack() as ctx:
        def sb(name, shape, dt=F32):
            return ctx.enter_context(nc.sbuf_tensor(name, shape, dt))

        def sem(name):
            return ctx.enter_context(nc.semaphore(name))

        h = sb("h", [P, DC, T])
        hn = sb("hn", [P, DC, T])
        y = sb("y", [P, DC, T])
        hid = sb("hid", [P, FC, T])
        ring = sb("ring", [P, SLOTS, SLOT])
        sq = sb("sq", [P, 4, T])
        ssum = sb("ssum", [P, T])
        std = sb("std", [P, T])
        rstd = sb("rstd", [P, T])
        tmp = sb("tmp", [P, 2, T])
        sg = sb("sg", [P, 2, T])
        gains = sb("gains", [P, 16, DC])
        ones = sb("ones", [P, P])
        eps = sb("eps", [P, 2])
        p_t = sb("p_t", [P, 2, T])

        cos64 = sb("cos64", [P, T])
        sin64 = sb("sin64", [P, T])
        turn64 = sb("turn64", [P, P])
        ident = sb("ident", [P, P])
        ident_b = sb("ident_b", [P, P], BF16)
        causal_b = sb("causal_b", [P, P], BF16)
        cos32 = sb("cos32", [P, T])
        sin32 = sb("sin32", [P, T])
        turn32 = sb("turn32", [P, P])
        kv_gain = sb("kv_gain", [P, 2])
        w_idx = sb("w_idx", [P, DC, IDX_HEADS])
        idx_w = sb("idx_w", [P, TT - 1, IDX_HEADS])
        top8 = sb("top8", [P, 8])
        count = sb("count", [P, 2])
        cmp_mask = sb("cmp_mask", [P, TT, P], BF16)
        row_valid = sb("row_valid", [P, TT])
        pe_t = sb("pe_t", [P, 2, CMP_LEN])
        w2 = sb("w2", [P, 2, P])
        gates = sb("gates", [P, TT, 24])
        k_cmp = sb("k_cmp", [P, P])
        v_cmp = sb("v_cmp", [P, P])
        cmp_h = sb("cmp_h", [P, 6, 32])
        probs = sb("probs", [P, 2, T])
        probs_t = sb("probs_t", [P, 2, T])
        stat = sb("stat", [P, 3, 24])
        s5_prm = sb("s5_prm", [P, 3, PAIRS])
        s5_d = sb("s5_d", [P, 5])
        s5_v = sb("s5_v", [P, 24, PAIRS])
        s5_pow = sb("s5_pow", [P, PAIRS, 19])
        s5_pow_cur = sb("s5_pow_cur", [P, 4, 19])
        b_cur = sb("b_cur", [P, 2, P])
        s5w = sb("s5w", [P, 8, T])

        y_flat = y[:, :, :].rearrange("p c t -> p (c t)")
        hn_flat = hn[:, :, :].rearrange("p c t -> p (c t)")
        q_t = [hid[:, 12 + j, :] for j in range(4)]
        kc_t, vc_t, ks_t, kw_t = (hid[:, c, :] for c in (16, 17, 18, 19))
        v_tm = hid[:, 20:22, :].rearrange("p a t -> p (a t)").rearrange("p (t n) -> p t n", t=TT)
        w1 = [y[:, :, :].rearrange("p c t -> p (c t)").rearrange("p (l m) -> p l m", m=P),
              hn[:, :, :].rearrange("p c t -> p (c t)").rearrange("p (l m) -> p l m", m=P)]
        blk = [sq[:, 2 * b:2 * b + 2, :].rearrange("p a t -> p (a t)")[:, 0:CMP_LEN * CMP].rearrange(
            "p (l c) -> p l c", c=CMP) for b in range(2)]
        rot_c, rot_s = s5w[:, 0, :], s5w[:, 1, :]
        zs = [s5w[:, 2, :], s5w[:, 3, :]]
        xs = [s5w[:, 4, :], s5w[:, 5, :]]
        wk = [s5w[:, 6, :], s5w[:, 7, :]]
        b_raw = s5w[:, 6:8, :]
        b_bar = s5w[:, 4:6, :]
        b_t = [std[:, :].rearrange("p (q n) -> p q n", q=4), rstd[:, :].rearrange("p (q n) -> p q n", q=4)]
        c_cur = p_t[:, :, :].rearrange("p c t -> p (c t)").rearrange("p (c j n) -> p c j n", c=2, j=4)
        u_cur = q_cur = ssum
        ya = sg[:, :, :]
        mixed = [hid[:, c, :] for c in (8, 9, 10, 11, 4, 5, 6, 7)]

        q_idx = [hid[:, 8 + c, :] for c in range(4)]
        q_rope = [hid[:, 12 + c, :] for c in range(4)]
        c_kv = [hid[:, 16, :], hid[:, 17, :]]
        k_rope, k_idx = hid[:, 18, :], hid[:, 19, :]
        sel_mask = hid[:, 20:22, :].rearrange("p a t -> p (a t)").bitcast(BF16).rearrange("p (t n) -> p t n", t=TT)
        v_h = y_flat.rearrange("p (t n) -> p t n", t=TT)
        q_lat = [s5w[:, 0:2, :], s5w[:, 2:4, :]]
        v_cur = s5w[:, 4:6, :].rearrange("p a t -> p (a t)").rearrange("p (t n) -> p t n", t=TT)
        score, found = s5w[:, 4, :], s5w[:, 5, :]
        relus = [s5w[:, 6, :], s5w[:, 7, :]]

        banks = ctx.enter_context(nc.psum_tensor("banks", [P, BANKS, T], F32))
        total = ctx.enter_context(nc.psum_tensor("total", [P, T], F32))

        xb = ctx.enter_context(nc.psum_tensor("xb", [P, 3, T], F32))
        scores = [xb[:, 0, :], xb[:, 1, :]]
        flipped = [xb[:, 2, :], total[:, :]]

        consts_in = sem("consts_in")
        x_in = sem("x_in")
        p_in = sem("p_in")
        unit_in = [sem(f"unit_in{s}") for s in range(SLOTS)]
        gemm_done = sem("gemm_done")
        bank_free = sem("bank_free")
        h_squared = sem("h_squared")
        y_squared = sem("y_squared")
        y_added = sem("y_added")
        total_step = sem("total_step")
        std_done = sem("std_done")
        hn_done = sem("hn_done")
        scaled_done = sem("scaled_done")
        h_done = sem("h_done")
        act_part = sem("act_part")
        out_stored = sem("out_stored")
        dve_step = sem("dve_step")
        act_step = sem("act_step")
        turned = sem("turned")
        roped = sem("roped")
        gates_done = sem("gates_done")
        w1_in = sem("w1_in")
        blk_done = sem("blk_done")
        pe_step = sem("pe_step")
        small_taken = sem("small_taken")
        small_act = sem("small_act")
        dve_asks = sem("dve_asks")
        cur_done = sem("cur_done")
        c_in = sem("c_in")
        bu_done = sem("bu_done")
        states_done = sem("states_done")
        pair_used = sem("pair_used")
        s5_y_taken = sem("s5_y_taken")
        q_done = sem("q_done")
        scores_done = sem("scores_done")
        max_done = sem("max_done")
        exp_done = sem("exp_done")
        probs_done = sem("probs_done")
        flip_done = sem("flip_done")
        flip_taken = sem("flip_taken")
        dots_done = sem("dots_done")
        relu_done = sem("relu_done")
        dots_used = sem("dots_used")
        sel_done = sem("sel_done")
        pv_done = sem("pv_done")
        o_taken = sem("o_taken")
        raised_first = {"pe": (flip_done, pv_done, scores_done, pair_used),
                        "act": (exp_done, flip_taken),
                        "dve": (states_done, s5_y_taken, o_taken)}

        def raise_first(engine, name):
            for semaphore in raised_first[name]:
                engine.sem_inc(semaphore, 1)

        block = ctx.enter_context(nc.Block())

        ODD_ROPED = [2, 3, 4, 5, 6, 7, 8, 9, 10, 11]
        NARROW = (2, 8, 9, 10, 11)
        EVEN_ROPED = [4, 5, 6, 7, 8, 10, 11]

        def dsa_items():
            return [(qt + 1, j, qt, 0) for j in range(4) for qt in range(TT)]

        def nsa_items():
            return [((1, qt + 1, qt + 1)[br], half, qt, br) for half in range(2) for qt in range(TT) for br in range(3)]

        CONSTS = [(gains[:, :, :], "gains"), (cos64[:, :], "cos64"), (sin64[:, :], "sin64"),
                  (turn64[:, :], "turn64"), (ident[:, :], "ident"), (sg[:, 0, 0:P], "causal"), (sg[:, 1, :], "cmp_mask"), (row_valid[:, :], "row_valid"),
                  (pe_t[:, :, :], "pe_t"), (w2[:, :, :], "w2"), (s5_prm[:, :, :], "s5_prm"),
                  (cos32[:, :], "cos32"), (sin32[:, :], "sin32"), (turn32[:, :], "turn32"),
                  (kv_gain[:, :], "kv_gain"), (w_idx[:, :, :], "w_idx"),
                  (s5_d[:, 0:4], "s5_d"), (b_raw, "s5_b")]

        @block.sync
        def _(sp):
            for buf, name in CONSTS:
                sp.dma_start(buf, ap[name]).then_inc(consts_in, 16)
            for c in range(DC):
                sp.dma_start(h[:, c, :], ap["x_t"][:, c, :]).then_inc(x_in, 16)
            unit = 0
            used_at = []

            def load(name, n, width, slot):
                sp.dma_start(ring[:, slot, 0:width], ap[name][n, :, :]).then_inc(unit_in[slot], 16)

            for name, first, count, width, outs in streams:
                done = used_at[-1] if used_at else 0
                used_at += [done + outs * (n + 1) for n in range(count)]
                if name == "ple_gate":
                    sp.wait_ge(gemm_done, used_at[unit - SLOTS])
                    sp.dma_start(p_t[:, :, :], ap["p_t"][0 if first == 0 else 1, :, :, :]).then_inc(p_in, 16)
                if name == "even_in":
                    sp.wait_ge(hn_done, 2 * DC)
                    sp.dma_start(y_flat, ap["w1"][0, :, :]).then_inc(w1_in, 16)
                if name == "s5_glu":
                    sp.wait_ge(gemm_done, used_at[unit - 1])
                    sp.dma_start(hn_flat, ap["w1"][1, :, :]).then_inc(w1_in, 16)
                    for q in range(4):
                        if q:
                            sp.wait_ge(pair_used, 4 * q + 1)
                        sp.dma_start(c_cur, ap["s5_c"][q, :, :, :, :]).then_inc(c_in, 16)
                trips = (count - SLOTS) // SLOTS if count >= 3 * SLOTS else 0
                n = 0
                while n < count:
                    if n == SLOTS and trips:
                        with sp.Fori(0, trips) as it:
                            for k in range(SLOTS):
                                sp.wait_ge(gemm_done, it * (outs * SLOTS) + (done + outs * (k + 1)))
                                load(name, it * SLOTS + (first + SLOTS + k), width, (unit + k) % SLOTS)
                        n += trips * SLOTS
                        unit += trips * SLOTS
                    else:
                        if unit >= SLOTS:
                            sp.wait_ge(gemm_done, used_at[unit - SLOTS])
                        load(name, first + n, width, unit % SLOTS)
                        n += 1
                        unit += 1
            ups = sum(DC for s in plan if s[0] == "norm_out")
            for c in range(DC):
                sp.wait_ge(h_done, ups - DC + c + 1)
                sp.dma_start(ap["out_t"][:, c, :], h[:, c, :]).then_inc(out_stored, 16)
            sp.wait_ge(out_stored, 16 * DC)

        @block.tensor
        def _(pe):
            raise_first(pe, "pe")
            gemm, totals = Steps(pe, gemm_done), Steps(pe, total_step)
            h_squares, added = Steps(pe, h_squared), Steps(pe, y_added)
            stds, hns = Steps(pe, std_done), Steps(pe, hn_done)
            added.past(4)
            unit = [0]
            out = [0]

            def product(bank, width, parts):
                pe.wait_ge(bank_free, gemm.n + 1)
                for n, (lhs, rhs) in enumerate(parts):
                    last = nc.tensor.matmul(banks[:, bank, 0:width], lhs, rhs, start=(n == 0),
                                            stop=(n == len(parts) - 1))
                gemm.by(last)

            def units(count, outs, use):
                first, bank = unit[0], out[0]
                trips = count // SLOTS if count >= 2 * SLOTS else 0
                if trips:
                    with looped(pe, trips, {gemm: outs * SLOTS}) as it:
                        for k in range(SLOTS):
                            slot = (first + k) % SLOTS
                            pe.wait_ge(unit_in[slot], it * 16 + 16 * ((first + k) // SLOTS + 1))
                            use(slot, (bank + outs * k) % BANKS)
                for n in range(trips * SLOTS, count):
                    u = first + n
                    pe.wait_ge(unit_in[u % SLOTS], 16 * (u // SLOTS + 1))
                    use(u % SLOTS, (bank + outs * n) % BANKS)
                unit[0] += count
                out[0] += count * outs

            def norm_in():
                if totals.n:
                    stds.past().wait()
                for c in range(DC):
                    h_squares.past().wait()
                    totals.by(nc.tensor.matmul(total[:, :], ones[:, :], sq[:, c % 4, :], start=(c == 0),
                                               stop=(c == DC - 1)))

            def norm_out():
                added.past(DC).wait()
                stds.past().wait()
                totals.by(nc.tensor.matmul(total[:, :], ones[:, :], ssum[:, :], start=True, stop=True))

            def dense(x, chunks, outs):
                def use(slot, bank):
                    w = ring[:, slot, 0:chunks * outs * P].rearrange("p (k n) -> p k n", k=chunks)
                    for o in range(outs):
                        product((bank + o) % BANKS, T,
                                [(w[:, k, o * P:(o + 1) * P], x[:, k, :]) for k in range(chunks)])
                return use

            def ffn():
                hns.past(DC).wait()
                units(FC, 2, dense(hn, DC, 2))
                pe.wait_ge(bank_free, gemm.n + BANKS)
                units(DC, 1, dense(hid, FC, 1))

            small, taken = Steps(pe, pe_step), Steps(pe, small_taken)
            turns, ropes = Steps(pe, turned), Steps(pe, roped)
            scored, exped, probd = Steps(pe, scores_done, 1), Steps(pe, exp_done, 1), Steps(pe, probs_done)
            flips, fliptaken, pvs, os_ = Steps(pe, flip_done, 1), Steps(pe, flip_taken, 1), Steps(pe, pv_done, 1), Steps(pe, o_taken, 1)
            curs, bus, states, pairs = Steps(pe, cur_done), Steps(pe, bu_done), Steps(pe, states_done, 1), Steps(pe, pair_used, 1)
            s5ys, qs = Steps(pe, s5_y_taken, 1), Steps(pe, q_done)

            def turn(k, turner):
                ropes_free = ropes.n + k - 1
                if ropes_free >= 1:
                    pe.wait_ge(roped, ropes_free)
                turns.by(nc.tensor.matmul(xb[:, k % 2, :], turner[:, :], tmp[:, k % 2, :], start=True, stop=True))

            def token_major(slot, bank, x, width):
                w = ring[:, slot, 0:DC * width].rearrange("p (k n) -> p k n", k=DC)
                for t in range(TT):
                    product((bank + t) % BANKS, width,
                            [(x[:, k, t * P:(t + 1) * P], w[:, k, :]) for k in range(DC)])

            def s5():
                pe.wait_ge(dve_asks, 3)
                for c in range(2):
                    for q in range(4):
                        last = nc.tensor.transpose(xb[:, c, q * P:(q + 1) * P], b_bar[:, c, q * P:(q + 1) * P], ident[:, :])
                small.by(last)
                taken.past().wait()
                with looped(pe, 4, {curs: 1, bus: 4, states: 4, pairs: 4, s5ys: 1}) as q:
                    curs.past().wait()
                    for j in range(4):
                        rows = slice(32 * j, 32 * j + 32)
                        states_before = states.n
                        pe.wait_ge(states_done, states_before)
                        for c in range(2):
                            last = nc.tensor.matmul(xb[:, c, :], b_cur[rows, c, :], u_cur[rows, :], start=True, stop=True,
                                                    tile_position=(32 * j, 0))
                        bus.by(last)
                        states.past().wait()
                        if j == 0:
                            pe.wait_ge(c_in, q * 16 + 16)
                            pe.wait_ge(s5_y_taken, s5ys.n)
                        for c in range(2):
                            last = nc.tensor.matmul(xb[:, 2, :], c_cur[:, c, j, :], xs[c], start=(j == 0 and c == 0),
                                                    stop=(j == 3 and c == 1))
                        pairs.by(last)
                    s5ys.past()

            def compress():
                for b in range(2):
                    pe.wait_ge(w1_in, 16 * (b + 1))
                    pe.wait_ge(blk_done, b + 1)
                    for l in range(CMP_LEN):
                        last = nc.tensor.matmul(xb[:, b, 0:CMP], w1[b][:, l, :], blk[b][:, l, :],
                                                start=(l == 0), stop=(l == CMP_LEN - 1))
                    small.by(last)
                pe.wait_ge(small_taken, 4)
                small.by(nc.tensor.matmul(xb[:, 2, 0:CMP], w2[:, 0, :], cmp_h[:, 4, 0:CMP], start=True, stop=True))
                pe.wait_ge(small_taken, 5)
                small.by(nc.tensor.matmul(total[0:CMP, 0:P], cmp_h[:, 5, 0:CMP], w2[:, 1, :], start=True, stop=True))
                pe.wait_ge(small_taken, 7)
                taken.past(6)

            def attention_item(n, items, score, value):
                if n < len(items):
                    pe.wait_ge(exp_done, exped.n - 1 if n else exped.n)
                    score(n)
                    exped.past()
                if 0 <= n - 1 < len(items):
                    m = n - 1
                    probd.past().wait()
                    pe.wait_ge(flip_taken, fliptaken.n)
                    w = items[m][0]
                    for b in range(w):
                        last = nc.tensor.transpose(flipped[m % 2][:, b * P:(b + 1) * P], probs[:, m % 2, b * P:(b + 1) * P],
                                                   ident[:, :])
                    flips.by(last)
                if 0 <= n - 2 < len(items):
                    m = n - 2
                    fliptaken.past().wait()
                    value(m)

            def nsa():
                items = nsa_items()
                with looped(pe, 4, {scored: 24, exped: 24, probd: 24, flips: 24, fliptaken: 24, pvs: 24,
                                    qs: 1, os_: 1}) as j:
                    qs.past().wait()

                    def score(n):
                        w, half, qt, br = items[n]
                        rows = slice(HD * half, HD * half + HD)
                        keys = (k_cmp[:, :], ks_t, kw_t)[br]
                        dst = scores[n % 2]
                        nc.tensor.matmul(dst[:, 0:w * P], q_cur[rows, qt * P:(qt + 1) * P], keys[rows, 0:w * P],
                                         start=True, stop=False, tile_position=(HD * half, 0))
                        mask = cmp_mask[:, qt, :] if br == 0 else causal_b[:, :]
                        scored.by(nc.tensor.matmul(dst[:, (w - 1) * P:w * P], ident_b[:, :], mask, start=False, stop=True))

                    def value(m):
                        w, half, qt, br = items[m]
                        cols = slice(HD * half, HD * half + HD)
                        if half == 0 and qt == 0 and br == 0:
                            pe.wait_ge(o_taken, os_.n)
                        for b in range(w):
                            v = v_cmp[:, cols] if br == 0 else v_tm[:, b, (br - 1) * P + cols.start:(br - 1) * P + cols.stop]
                            last = nc.tensor.matmul(banks[cols, 2, qt * P:(qt + 1) * P], v,
                                                    probs_t[:, m % 2, b * P:(b + 1) * P], start=(br == 0),
                                                    stop=(br == 2 and b == w - 1), tile_position=(0, HD * half))
                        pvs.by(last)

                    for n in range(len(items) + 2):
                        attention_item(n, items, score, value)
                    os_.past()
                os_.wait()

            def project(roped_chunks):
                seen = []
                for n in range(6):
                    u = unit[0] + n
                    pe.wait_ge(unit_in[u % SLOTS], 16 * (u // SLOTS + 1))
                    w = ring[:, u % SLOTS, 0:DC * 2 * P].rearrange("p (k n) -> p k n", k=DC)
                    for o in range(2):
                        c = 2 * n + o
                        product((out[0] + c) % BANKS, T,
                                [(w[:, k, o * P:(o + 1) * P], hn[:, k, :]) for k in range(DC)])
                        if seen:
                            pe.wait_ge(bank_free, gemm.n - 1 + BANKS)
                            r = seen.pop()
                            turn(roped_chunks.index(r), turn32 if roped_chunks is ODD_ROPED and r in NARROW else turn64)
                        if c in roped_chunks:
                            seen.append(c)
                unit[0] += 6
                out[0] += 12
                pe.wait_ge(bank_free, gemm.n + BANKS)
                r = seen.pop()
                turn(roped_chunks.index(r), turn32 if roped_chunks is ODD_ROPED and r in NARROW else turn64)
                ropes.past(len(roped_chunks))

            def odd():
                hns.past(DC).wait()
                project(ODD_ROPED)
                for t in range(TT - 1):
                    for k in range(DC):
                        last = nc.tensor.matmul(xb[:, 2, 8 * t:8 * t + 8], hn[:, k, (1 + t) * P:(2 + t) * P],
                                                w_idx[:, k, :], start=(k == 0), stop=(k == DC - 1))
                small.by(last)
                stds.past().wait()
                for c in range(2):
                    h_squares.past().wait()
                    totals.by(nc.tensor.matmul(total[:, :], ones[:, :], sq[:, c, :], start=(c == 0), stop=(c == 1)))
                ropes.wait()
                for n in range((TT - 1) * IDX_HEADS):
                    qt, i = 1 + n // IDX_HEADS, n % IDX_HEADS
                    rows = slice(HD * (i % 2), HD * (i % 2) + HD)
                    if n >= 2:
                        pe.wait_ge(relu_done, n - 1)
                    nc.tensor.matmul(scores[n % 2][:, 0:(qt + 1) * P], q_idx[i // 2][rows, qt * P:(qt + 1) * P],
                                     k_idx[rows, 0:(qt + 1) * P], start=True, stop=True,
                                     tile_position=(HD * (i % 2), 0)).then_inc(dots_done, 1)
                pe.wait_ge(small_taken, taken.n + 2)
                taken.past(2)

                def values(slot, bank):
                    w = ring[:, slot, 0:2 * D].rearrange("p (k n) -> p k n", k=2)
                    for t in range(TT):
                        for half in range(2):
                            product((bank + 2 * t + half) % BANKS, T,
                                    [(c_kv[c][:, t * P:(t + 1) * P], w[:, c, half * T:(half + 1) * T]) for c in range(2)])

                units(1, 8, values)
                pe.wait_ge(bank_free, gemm.n + BANKS)
                pe.wait_ge(sel_done, TT - 1)
                dsa()
                pe.wait_ge(bank_free, gemm.n + BANKS)
                units(4, 2, dense(hid, DC, 2))

            def dsa():
                items = dsa_items()
                first = unit[0]
                with looped(pe, 4, {scored: 16, exped: 16, probd: 16, flips: 16, fliptaken: 16, pvs: 16,
                                    qs: 1, os_: 2, gemm: 8}) as it:
                    def project_part(j, part):
                        slot = (first + j) % SLOTS
                        o, upper = part // 2, part % 2
                        if part == 0:
                            pe.wait_ge(unit_in[slot], it * 16 + 16 * ((first + j) // SLOTS + 1))
                        if not upper:
                            pe.wait_ge(bank_free, gemm.n + 1 + 2)
                        w = ring[:, slot, 0:DC * 2 * P].rearrange("p (k n) -> p k n", k=DC)
                        for k in range(4 * upper, 4 * upper + 4):
                            last = nc.tensor.matmul(banks[:, o, :], w[:, k, o * P:(o + 1) * P], hn[:, k, :],
                                                    start=(k == 0), stop=(k == DC - 1))
                        if upper:
                            gemm.by(last)

                    def score_of(n):
                        w, j, qt, _ = items[n]
                        dst = scores[n % 2][:, 0:w * P]
                        if n == 0:
                            pe.wait_ge(bank_free, gemm.n + BANKS)
                            qs.past().wait()
                        if qt == 0 and j:
                            pe.wait_ge(bank_free, gemm.n + BANKS)
                        for c in range(2):
                            nc.tensor.matmul(dst, q_lat[j % 2][:, c, qt * P:(qt + 1) * P], c_kv[c][:, 0:w * P],
                                             start=(c == 0), stop=False)
                        rows = slice(32 * j, 32 * j + 32)
                        nc.tensor.matmul(dst, q_cur[rows, qt * P:(qt + 1) * P], k_rope[rows, 0:w * P], start=False,
                                         stop=False, tile_position=(32 * j, 0))
                        if qt == 0:
                            scored.by(nc.tensor.matmul(dst[:, (w - 1) * P:w * P], ident_b[:, :], causal_b[:, :],
                                                       start=False, stop=True))
                        else:
                            scored.by(nc.tensor.matmul(dst, ident_b[:, :], sel_mask[:, qt - 1, 0:w * P],
                                                       start=False, stop=True))

                    def value(m):
                        w, j, qt, _ = items[m]
                        cols = slice(HD * (j % 2), HD * (j % 2) + HD)
                        if qt == 0 and j % 2 == 0:
                            pe.wait_ge(o_taken, os_.n - 1 if j else os_.n)
                            os_.past()
                        for b in range(w):
                            last = nc.tensor.matmul(banks[cols, 2 + j // 2, qt * P:(qt + 1) * P],
                                                    v_cur[:, b, HD * j:HD * j + HD], probs_t[:, m % 2, b * P:(b + 1) * P],
                                                    start=(b == 0), stop=(b == w - 1), tile_position=(0, HD * (j % 2)))
                        pvs.by(last)

                    for part in range(4):
                        project_part(0, part)
                    for n in range(len(items) + 2):
                        attention_item(n, items, score_of, value)
                        if n // 4 + 1 < 4:
                            project_part(n // 4 + 1, n % 4)
                unit[0] += HEADS
                out[0] += 2 * HEADS
                os_.wait()

            def even():
                hns.past(DC).wait()
                project(EVEN_ROPED)
                units(1, TT, lambda slot, bank: token_major(slot, bank, hn, TM))
                pe.wait_ge(bank_free, gemm.n + BANKS)
                ropes.wait()
                s5()
                compress()
                nsa()
                pe.wait_ge(s5_y_taken, 6)
                units(1, 4, dense(hid, 4, 4))
                pe.wait_ge(bank_free, gemm.n + BANKS)
                units(4, 2, dense_of(mixed, DC, 2))

            def dense_of(x, chunks, outs):
                def use(slot, bank):
                    w = ring[:, slot, 0:chunks * outs * P].rearrange("p (k n) -> p k n", k=chunks)
                    for o in range(outs):
                        product((bank + o) % BANKS, T, [(w[:, k, o * P:(o + 1) * P], x[k]) for k in range(chunks)])
                return use

            def ple(layer):
                hns.past(DC).wait()
                units(DC // 2, 2, dense(hn, DC, 2))
                pe.wait_ge(p_in, 16 * (layer + 1))
                units(1, DC, dense(p_t, 2, DC))

            pe.wait_ge(bank_free, BANKS)
            for step in plan:
                if step[0] == "norm_in":
                    norm_in()
                elif step[0] == "norm_out":
                    norm_out()
                elif step[0] == "ffn":
                    ffn()
                elif step[0] == "even":
                    even()
                elif step[0] == "odd":
                    odd()
                elif step[0] == "ple":
                    ple(step[1])

        @block.scalar
        def _(act):
            raise_first(act, "act")
            gemm, free = Steps(act, gemm_done), Steps(act, bank_free)
            h_squares, y_squares, added = Steps(act, h_squared), Steps(act, y_squared), Steps(act, y_added)
            totals, stds, hs = Steps(act, total_step), Steps(act, std_done), Steps(act, h_done)
            parts = Steps(act, act_part)
            free.past(BANKS)
            out = [0]

            def norm_in():
                for c in range(DC):
                    if h_squares.n < DC:
                        act.wait_ge(x_in, 16 * DC)
                    else:
                        hs.past().wait()
                    if c >= 4:
                        act.wait_ge(total_step, totals.n + c - 3)
                    h_squares.by(nc.scalar.activation(sq[:, c % 4, :], h[:, c, :], ACT.Square))
                totals.past(DC).wait()
                stds.by(nc.scalar.activation(std[:, :], total[:, :], ACT.Sqrt, bias=eps[:, 0:1], scale=1.0 / D))

            def norm_out(factor):
                totals.past().wait()
                col = 0 if factor == 1.0 else 1
                stds.by(nc.scalar.activation(std[:, :], total[:, :], ACT.Sqrt, bias=eps[:, col:col + 1],
                                             scale=1.0 / (D * factor * factor)))

            def square_ys(trips):
                with looped(act, trips, {gemm: 4, free: 4, y_squares: 4, added: 4}) as it:
                    for k in range(4):
                        gemm.past()
                        free.past().wait()
                        added.past().wait()
                        y_squares.by(nc.scalar.activation(sq[:, k, :], y[:, it * 4 + k, :], ACT.Square))
                out[0] += 4 * trips

            def ffn():
                bank = out[0]
                with looped(act, FC // 2, {gemm: 4, free: 4, parts: 2}) as it:
                    for k in range(2):
                        gemm.past().wait()
                        free.wait(2)
                        parts.by(nc.scalar.activation(sg[:, k, :], banks[:, (bank + 2 * k) % BANKS, :], ACT.Silu))
                        gemm.past()
                        free.past(2)
                out[0] += 2 * FC
                square_ys(2)

            small, asks = Steps(act, small_act), Steps(act, dve_asks)
            curs, pairs, qs, pvs = Steps(act, cur_done), Steps(act, pair_used, 1), Steps(act, q_done), Steps(act, pv_done, 1)
            maxed, exped, probd = Steps(act, max_done), Steps(act, exp_done, 1), Steps(act, probs_done)
            flips, fliptaken, own = Steps(act, flip_done, 1), Steps(act, flip_taken, 1), Steps(act, act_step)
            gated, s5ys, scored = Steps(act, gates_done), Steps(act, s5_y_taken, 1), Steps(act, scores_done, 1)

            def attention_item(n, items, scale):
                if n < len(items):
                    maxed.past().wait()
                    w = items[n][0]
                    act.wait_ge(flip_done, flips.n)
                    exped.by(nc.scalar.activation(probs[:, n % 2, 0:w * P], scores[n % 2][:, 0:w * P], ACT.Exp,
                                                  bias=stat[:, 0, n:n + 1], scale=scale, accum_out=stat[:, 1, n:n + 1]))
                if 0 <= n - 1 < len(items):
                    m = n - 1
                    w = items[m][0]
                    flips.past().wait()
                    act.wait_ge(pv_done, pvs.n)
                    fliptaken.by(nc.scalar.activation(probs_t[:, m % 2, 0:w * P], flipped[m % 2][:, 0:w * P], ACT.Copy))
                    if m >= 1:
                        pvs.past()

            def odd():
                gemm.past(12)
                for c in range(2):
                    free.past().wait()
                    h_squares.by(nc.scalar.activation(sq[:, c, :], c_kv[c], ACT.Square))
                free.past(10)
                totals.past(2).wait()
                stds.by(nc.scalar.activation(std[:, :], total[:, :], ACT.Sqrt, bias=eps[:, 0:1], scale=1.0 / LATENT))
                for n in range((TT - 1) * IDX_HEADS):
                    act.wait_ge(dots_done, n + 1)
                    if n >= 2:
                        act.wait_ge(dots_used, n - 1)
                    nc.scalar.activation(relus[n % 2][:, 0:(2 + n // IDX_HEADS) * P],
                                         scores[n % 2][:, 0:(2 + n // IDX_HEADS) * P], ACT.Relu,
                                         scale=HD ** -0.5).then_inc(relu_done, 1)
                gemm.past(8)
                free.past(8)
                act.wait_ge(sel_done, TT - 1)
                free.wait()
                items = dsa_items()
                start = scored.n
                with looped(act, 4, {maxed: 16, exped: 16, flips: 16, fliptaken: 16, pvs: 16, qs: 1, own: 1}) as it:
                    act.wait_ge(scores_done, it * 16 + start)
                    act.wait_ge(pv_done, pvs.n)
                    own.by(nc.scalar.activation(v_cur, v_h[:, :, bass.ds(it * 256, 256)], ACT.Copy))
                    qs.by(nc.scalar.activation(q_cur[:, :], hid[:, it + 12, :], ACT.Copy))
                    for n in range(len(items) + 1):
                        attention_item(n, items, DSA_SCALE)
                    pvs.past()
                gemm.past(2 * HEADS)
                free.past(2 * HEADS)
                out[0] += 20 + 2 * HEADS
                square_ys(2)

            def even():
                gemm.past(12)
                free.past(12)
                out[0] += 12
                for t in range(TT):
                    gemm.past().wait()
                    gated.by(nc.scalar.activation(gates[:, t, :], banks[:, (out[0] + t) % BANKS, 2 * P:TM], ACT.Sigmoid))
                    free.past()
                out[0] += TT
                asks.past().wait()
                small.by(nc.scalar.activation(s5_v[:, 0, :], s5_prm[:, 2, :], ACT.Exp))
                asks.past().wait()
                own.by(nc.scalar.activation(s5_v[:, 3, :], s5_v[:, 1, :], ACT.Exp))
                own.by(nc.scalar.activation(s5_v[:, 6, :], s5_v[:, 4, :], ACT.Sin))
                small.by(nc.scalar.activation(s5_v[:, 7, :], s5_v[:, 5, :], ACT.Sin))
                asks.past()
                act.wait_ge(small_taken, 1)
                act.wait_ge(dve_asks, 4)
                with looped(act, 4, {curs: 1, own: 3, s5ys: 1}) as q:
                    act.wait_ge(s5_y_taken, s5ys.n)
                    s5ys.past()
                    own.by(nc.scalar.activation(u_cur[:, :], hid[:, q + 8, :], ACT.Copy))
                    own.by(nc.scalar.activation(b_cur[:, 0, :], std[:, bass.ds(q * P, P)], ACT.Copy))
                    own.by(nc.scalar.activation(b_cur[:, 1, :], rstd[:, bass.ds(q * P, P)], ACT.Copy))
                    curs.by(nc.scalar.activation(s5_pow_cur[:, :, :], s5_pow[:, bass.ds(q * 4, 4), :], ACT.Copy))
                asks.past()
                for b in range(2):
                    asks.past().wait()
                    small.by(nc.scalar.activation(cmp_h[:, 2, 0:CMP], cmp_h[:, 1, 0:CMP], ACT.Sigmoid, scale=GELU))
                items = nsa_items()
                act.wait_ge(small_taken, 7)
                with looped(act, 4, {maxed: 24, exped: 24, flips: 24, fliptaken: 24, pvs: 24, qs: 1}) as j:
                    act.wait_ge(scores_done, j * 24 + 1)
                    qs.by(nc.scalar.activation(q_cur[:, :], hid[:, j + 12, :], ACT.Copy))
                    for n in range(len(items) + 1):
                        attention_item(n, items, HD ** -0.5)
                    pvs.past()
                scored.past(96)
                for c in range(4):
                    asks.past().wait()
                    small.by(nc.scalar.activation(sg[:, c % 2, :], s5w[:, c % 2, :], ACT.Sigmoid, scale=GELU))
                for c in range(4):
                    gemm.past().wait()
                    small.by(nc.scalar.activation(sg[:, c % 2, :], banks[:, (out[0] + c) % BANKS, :], ACT.Sigmoid))
                    free.past()
                    free.wait(0)
                out[0] += 4
                square_ys(2)

            def ple():
                gate = hid
                gemm.past(DC)
                for c in range(DC):
                    free.past().wait()
                    parts.by(nc.scalar.activation(gate[:, c, :], gate[:, c, :], ACT.Sigmoid))
                out[0] += DC
                square_ys(2)

            act.wait_ge(bank_free, BANKS)
            for step in plan:
                if step[0] == "norm_in":
                    norm_in()
                elif step[0] == "norm_out":
                    norm_out(step[2])
                elif step[0] == "ffn":
                    ffn()
                elif step[0] == "even":
                    even()
                elif step[0] == "odd":
                    odd()
                elif step[0] == "odd":
                    odd()
                elif step[0] == "ple":
                    ple()

        @block.vector
        def _(dve):
            raise_first(dve, "dve")
            gemm, free = Steps(dve, gemm_done), Steps(dve, bank_free)
            y_squares, added = Steps(dve, y_squared), Steps(dve, y_added)
            stds, hns, scaled, hs = Steps(dve, std_done), Steps(dve, hn_done), Steps(dve, scaled_done), Steps(dve, h_done)
            parts, own = Steps(dve, act_part), Steps(dve, dve_step)
            out = [0]
            last = [None]

            def did(instruction, steps=own, k=1):
                steps.by(instruction, k)
                last[0] = steps

            def settle():
                last[0].wait()

            def looped_dve(trips, per, tail):
                settle()
                last[0] = tail
                return looped(dve, trips, per)

            def root():
                stds.past().wait()
                settle()
                did(nc.vector.reciprocal(rstd[:, :], std[:, :]))
                settle()

            def norm_in(g):
                root()
                for c in range(DC):
                    did(nc.vector.scalar_tensor_tensor(hn[:, c, :], h[:, c, :], gains[:, g, c:c + 1], rstd[:, :],
                                                       ALU.mult, ALU.mult), hns)

            def norm_out(g):
                root()
                for c in range(DC):
                    if hs.n + c >= 2:
                        dve.wait_ge(h_done, hs.n + c - 1)
                    did(nc.vector.scalar_tensor_tensor(tmp[:, c % 2, :], y[:, c, :], gains[:, g, c:c + 1],
                                                       rstd[:, :], ALU.mult, ALU.mult), scaled)
                hs.past(DC)

            def take_y(trips, take):
                bank = out[0]
                settle()
                did(nc.vector.memset(ssum[:, :], 0.0))
                with looped_dve(trips, {gemm: 4, free: 4, y_squares: 4, added: 4}, added) as it:
                    for k in range(4):
                        gemm.past().wait()
                        settle()
                        take(it * 4 + k, (bank + k) % BANKS)
                        y_squares.past().wait()
                        settle()
                        did(nc.vector.tensor_tensor(ssum[:, :], ssum[:, :], sq[:, k, :], ALU.add), added)
                out[0] += 4 * trips

            def plain_y(c, bank):
                did(nc.vector.tensor_copy(y[:, c, :], banks[:, bank, :]), free)

            def ffn():
                bank = out[0]
                with looped_dve(FC // 2, {gemm: 4, free: 4, parts: 2}, free) as it:
                    for k in range(2):
                        gemm.past(2).wait()
                        parts.past().wait()
                        settle()
                        did(nc.vector.tensor_tensor(hid[:, it * 2 + k, :], sg[:, k, :],
                                                    banks[:, (bank + 2 * k + 1) % BANKS, :], ALU.mult), free, 2)
                out[0] += 2 * FC
                take_y(2, plain_y)

            turns, ropes = Steps(dve, turned), Steps(dve, roped)
            gated, blks, small_pe, taken = Steps(dve, gates_done), Steps(dve, blk_done), Steps(dve, pe_step), Steps(dve, small_taken)
            small, asks = Steps(dve, small_act), Steps(dve, dve_asks)
            bus, states, pairs, s5ys, curs = (Steps(dve, bu_done), Steps(dve, states_done, 1), Steps(dve, pair_used, 1),
                                              Steps(dve, s5_y_taken, 1), Steps(dve, cur_done))
            scored, maxed, exped, probd = (Steps(dve, scores_done, 1), Steps(dve, max_done), Steps(dve, exp_done, 1),
                                           Steps(dve, probs_done))
            pvs, os_ = Steps(dve, pv_done, 1), Steps(dve, o_taken, 1)
            dots, sels = Steps(dve, dots_used), Steps(dve, sel_done)

            def tt(dst, a, b, op, steps=own):
                settle()
                did(nc.vector.tensor_tensor(dst, a, b, op), steps)

            def ts(dst, a, s1, s2, op0, op1=None, steps=own):
                settle()
                if op1 is None:
                    did(nc.vector.tensor_scalar(dst, a, s1, None, op0), steps)
                else:
                    did(nc.vector.tensor_scalar(dst, a, s1, s2, op0, op1), steps)

            def rope_start(k, bank):
                settle()
                did(nc.vector.tensor_copy(tmp[:, k % 2, :], banks[:, bank, :]), free)

            def rope_end(k, dst, cos, sin):
                turns.past().wait()
                tt(sg[:, 0, :], tmp[:, k % 2, :], cos, ALU.mult)
                tt(sg[:, 1, :], xb[:, k % 2, :], sin, ALU.mult)
                tt(dst, sg[:, 0, :], sg[:, 1, :], ALU.add, ropes)

            def gelu_before(x, t, ask):
                tt(t, x, x, ALU.mult)
                ts(t, t, 0.044715, 1.0, ALU.mult, ALU.add)
                tt(t, t, x, ALU.mult, ask)

            def s5_scalars():
                v = lambda k: s5_v[:, k, :]
                a_re, a_im = s5_prm[:, 0, :], s5_prm[:, 1, :]
                settle()
                did(nc.vector.memset(s5_v[:, 20, :], 0.0), asks)
                small.past().wait()
                tt(v(1), a_re, v(0), ALU.mult)
                tt(v(2), a_im, v(0), ALU.mult)
                ts(v(8), v(2), 1 / (2 * np.pi), MAGIC, ALU.mult, ALU.add)
                ts(v(8), v(8), MAGIC, None, ALU.subtract)
                settle()
                did(nc.vector.scalar_tensor_tensor(v(9), v(8), -TWO_PI_HI, v(2), ALU.mult, ALU.add))
                settle()
                did(nc.vector.scalar_tensor_tensor(v(9), v(8), -TWO_PI_LO, v(9), ALU.mult, ALU.add))
                ts(v(4), v(9), PI_IN, -PI_IN, ALU.min, ALU.max)
                ts(v(5), v(4), -1.0, None, ALU.mult)
                tt(v(5), v(5), v(4), ALU.max)
                ts(v(5), v(5), -1.0, np.pi / 2, ALU.mult, ALU.add, asks)
                small.past().wait()
                for k in range(POW):
                    re, im = s5_pow[:, :, k], s5_pow[:, :, 9 + k]
                    if k == 0:
                        cr, ci = v(7), v(6)
                    else:
                        pr, pi = s5_pow[:, :, k - 1], s5_pow[:, :, 8 + k]
                        tt(v(10), pr, pr, ALU.mult)
                        tt(v(11), pi, pi, ALU.mult)
                        tt(v(12), v(10), v(11), ALU.subtract)
                        tt(v(13), pr, pi, ALU.mult)
                        ts(v(13), v(13), 2.0, None, ALU.mult)
                        cr, ci = v(12), v(13)
                    tt(v(10), cr, cr, ALU.mult)
                    tt(v(11), ci, ci, ALU.mult)
                    tt(v(10), v(10), v(11), ALU.add)
                    ts(v(10), v(10), -0.5, 1.5, ALU.mult, ALU.add)
                    tt(re, cr, v(10), ALU.mult)
                    tt(im, ci, v(10), ALU.mult)
                settle()
                did(nc.vector.tensor_copy(s5_pow[:, :, 18], v(3)))
                tt(v(14), v(3), v(7), ALU.mult)
                ts(v(14), v(14), 1.0, None, ALU.subtract)
                tt(v(15), v(3), v(6), ALU.mult)
                tt(v(16), a_re, a_re, ALU.mult)
                tt(v(17), a_im, a_im, ALU.mult)
                tt(v(16), v(16), v(17), ALU.add)
                settle()
                did(nc.vector.reciprocal(v(16), v(16)))
                tt(v(17), v(14), a_re, ALU.mult)
                tt(v(18), v(15), a_im, ALU.mult)
                tt(v(17), v(17), v(18), ALU.add)
                tt(v(17), v(17), v(16), ALU.mult)
                tt(v(18), v(15), a_re, ALU.mult)
                tt(v(19), v(14), a_im, ALU.mult)
                tt(v(18), v(18), v(19), ALU.subtract)
                tt(v(18), v(18), v(16), ALU.mult)
                col = lambda k: s5_v[:, k, :].rearrange("p (t o) -> p t o", o=1).to_broadcast([P, PAIRS, 32])
                m = lambda a: a.rearrange("p (t n) -> p t n", n=32)
                br, bi = b_raw[:, 0, :], b_raw[:, 1, :]
                tt(m(zs[0]), m(br), col(17), ALU.mult)
                tt(m(zs[1]), m(bi), col(18), ALU.mult)
                tt(b_bar[:, 0, :], zs[0], zs[1], ALU.subtract)
                tt(m(zs[0]), m(bi), col(17), ALU.mult)
                tt(m(zs[1]), m(br), col(18), ALU.mult)
                tt(b_bar[:, 1, :], zs[0], zs[1], ALU.add, asks)
                small_pe.past().wait()
                settle()
                did(nc.vector.tensor_copy(std[:, :], xb[:, 0, :]))
                did(nc.vector.tensor_copy(rstd[:, :], xb[:, 1, :]), taken)
                settle()
                did(nc.vector.memset(s5_v[:, 20, :], 0.0), asks)

            def s5():
                s5_scalars()
                with looped_dve(4, {curs: 1, bus: 4, states: 4, pairs: 4, s5ys: 1, own: 4 * (2 + 4 * POW + 13) + 1}, s5ys) as q:
                    curs.past().wait()
                    for j in range(4):
                        sc = lambda k: s5_pow_cur[:, j, k:k + 1]
                        settle()
                        did(nc.vector.memset(rot_c[:, 0:1], 1.0))
                        settle()
                        did(nc.vector.memset(rot_s[:, 0:1], 0.0))
                        for k in range(POW):
                            m = 1 << k
                            ts(wk[0][:, 0:m], rot_s[:, 0:m], sc(9 + k), None, ALU.mult)
                            ts(wk[1][:, 0:m], rot_s[:, 0:m], sc(k), None, ALU.mult)
                            settle()
                            did(nc.vector.scalar_tensor_tensor(rot_s[:, m:2 * m], rot_c[:, 0:m], sc(9 + k), wk[1][:, 0:m],
                                                               ALU.mult, ALU.add))
                            settle()
                            did(nc.vector.scalar_tensor_tensor(rot_c[:, m:2 * m], rot_c[:, 0:m], sc(k), wk[0][:, 0:m],
                                                               ALU.mult, ALU.subtract))
                        bus.past().wait()
                        dr, di = xb[:, 0, :], xb[:, 1, :]
                        tt(wk[0], dr, rot_c, ALU.mult)
                        tt(wk[1], di, rot_s, ALU.mult)
                        tt(wk[0], wk[0], wk[1], ALU.add)
                        tt(wk[1], di, rot_c, ALU.mult)
                        tt(zs[1], dr, rot_s, ALU.mult)
                        tt(wk[1], wk[1], zs[1], ALU.subtract)
                        decay = sc(18).to_broadcast([P, T])
                        for c in range(2):
                            settle()
                            did(nc.vector.tensor_tensor_scan(zs[c], decay, wk[c], 0.0, ALU.mult, ALU.add))
                        dve.wait_ge(pair_used, pairs.n)
                        pairs.past()
                        tt(xs[0], zs[0], rot_c, ALU.mult)
                        tt(wk[0], zs[1], rot_s, ALU.mult)
                        tt(xs[0], xs[0], wk[0], ALU.subtract)
                        tt(wk[1], zs[1], rot_c, ALU.mult)
                        tt(wk[0], zs[0], rot_s, ALU.mult)
                        settle()
                        did(nc.vector.scalar_tensor_tensor(xs[1], wk[0], -1.0, wk[1], ALU.mult, ALU.subtract), states)
                    pairs.wait()
                    settle()
                    did(nc.vector.tensor_copy(s5_d[:, 4:5], s5_d[:, bass.ds(q, 1)]))
                    settle()
                    did(nc.vector.scalar_tensor_tensor(hid[:, q, :], u_cur[:, :], s5_d[:, 4:5], xb[:, 2, :], ALU.mult, ALU.add), s5ys)

            def compress():
                for b, src in enumerate((kc_t, vc_t)):
                    for a in range(2):
                        part = src[:, CMP_STRIDE * a:CMP_STRIDE * (a + CMP)].rearrange("p (c l) -> p l c", l=CMP_STRIDE)
                        pe_ = pe_t[:, b, CMP_STRIDE * a:CMP_STRIDE * (a + 1)].rearrange(
                            "p (l o) -> p l o", o=1).to_broadcast([P, CMP_STRIDE, CMP])
                        tt(blk[b][:, CMP_STRIDE * a:CMP_STRIDE * (a + 1), :], part, pe_, ALU.add, own if a == 0 else blks)
                for b in range(2):
                    small_pe.past().wait()
                    x = cmp_h[:, 0, 0:CMP]
                    settle()
                    did(nc.vector.tensor_copy(x, xb[:, b, 0:CMP]), taken)
                    gelu_before(x, cmp_h[:, 1, 0:CMP], asks)
                    small.past().wait()
                    tt(cmp_h[:, 4 + b, 0:CMP], x, cmp_h[:, 2, 0:CMP], ALU.mult, taken)
                settle()
                did(nc.vector.memset(k_cmp[:, :], 0.0))
                settle()
                did(nc.vector.memset(v_cmp[:, :], 0.0))
                small_pe.past().wait()
                settle()
                did(nc.vector.tensor_copy(k_cmp[:, 0:CMP], xb[:, 2, 0:CMP]), taken)
                small_pe.past().wait()
                did(nc.vector.tensor_copy(v_cmp[0:CMP, :], total[0:CMP, 0:P]), taken)

            def attention_item(n, items, factor):
                if n < len(items):
                    w = items[n][0]
                    scored.past().wait()
                    settle()
                    did(nc.vector.tensor_reduce(stat[:, 2, n:n + 1], scores[n % 2][:, 0:w * P], AX.X, ALU.max))
                    ts(stat[:, 0, n:n + 1], stat[:, 2, n:n + 1], -factor[0], None, ALU.mult, None, maxed)
                if 0 <= n - 1 < len(items):
                    m = n - 1
                    w = items[m][0]
                    exped.past().wait()
                    settle()
                    did(nc.vector.reciprocal(stat[:, 2, m:m + 1], stat[:, 1, m:m + 1]))
                    if factor[1]:
                        ts(probs[:, m % 2, 0:w * P], probs[:, m % 2, 0:w * P], stat[:, 2, m:m + 1], factor[1](m), ALU.mult,
                           ALU.mult, probd)
                    else:
                        ts(probs[:, m % 2, 0:w * P], probs[:, m % 2, 0:w * P], stat[:, 2, m:m + 1], None, ALU.mult, None,
                           probd)

            def nsa():
                for qt in range(TT):
                    g3 = gates[:, qt, :].rearrange("p (h b) -> p h b", b=3)[:, :, 0]
                    ts(g3, g3, row_valid[:, qt:qt + 1], None, ALU.mult)
                items = nsa_items()
                with looped_dve(4, {scored: 24, maxed: 24, exped: 24, probd: 24, own: 48, pvs: 24, os_: 1}, os_) as j:
                    def gate(m):
                        w, half, qt, br = items[m]
                        return gates[:, qt, bass.ds(j * 3 + (12 * half + br), 1)]
                    for n in range(len(items) + 1):
                        attention_item(n, items, (HD ** -0.5, gate))
                    pvs.past(24).wait()
                    settle()
                    did(nc.vector.tensor_copy(hid[:, j + 4, :], banks[:, 2, :]), os_)

            def index():
                small_pe.past().wait()
                ts(idx_w[:, :, :], xb[:, 2, 0:8 * (TT - 1)].rearrange("p (t h) -> p t h", h=8), IDX_HEADS ** -0.5, None,
                   ALU.mult, None, taken)
                root()
                for c in range(2):
                    did(nc.vector.scalar_tensor_tensor(c_kv[c], c_kv[c], kv_gain[:, c:c + 1], rstd[:, :], ALU.mult,
                                                       ALU.mult), own if c == 0 else taken)
                for t in range(TT - 1):
                    w = (2 + t) * P
                    for i in range(IDX_HEADS):
                        n = IDX_HEADS * t + i
                        dve.wait_ge(relu_done, n + 1)
                        settle()
                        if i == 0:
                            used = nc.vector.tensor_scalar(score[:, 0:w], relus[n % 2][:, 0:w], idx_w[:, t, i:i + 1], None,
                                                           ALU.mult)
                        else:
                            used = nc.vector.scalar_tensor_tensor(score[:, 0:w], relus[n % 2][:, 0:w], idx_w[:, t, i:i + 1],
                                                                  score[:, 0:w], ALU.mult, ALU.add)
                        did(used, dots)
                    tt(score[:, w - P:w], score[:, w - P:w], causal_b[:, :], ALU.add)
                    left = sg[:, 0, 0:w]
                    settle()
                    did(nc.vector.tensor_copy(left, score[:, 0:w]))
                    for _ in range(ROUNDS - 1):
                        settle()
                        did(nc.vector.max(top8[:, :], left))
                        settle()
                        did(nc.vector.match_replace(left, top8[:, :], left, LOW))
                    settle()
                    did(nc.vector.max(top8[:, :], left))
                    least = top8[:, 7:8]
                    more, equal, rank = found[:, 0:w], sg[:, 1, 0:w], sg[:, 0, 0:w]
                    ts(more, score[:, 0:w], least, None, ALU.is_gt)
                    settle()
                    did(nc.vector.tensor_reduce(count[:, 0:1], more, AX.X, ALU.add))
                    ts(count[:, 1:2], count[:, 0:1], -1.0, float(TOP), ALU.mult, ALU.add)
                    ts(equal, score[:, 0:w], least, None, ALU.is_equal)
                    settle()
                    did(nc.vector.tensor_tensor_scan(rank, ones[:, 0:1].to_broadcast([P, w]), equal, 0.0, ALU.mult, ALU.add))
                    settle()
                    did(nc.vector.scalar_tensor_tensor(rank, rank, count[:, 1:2], equal, ALU.is_le, ALU.mult))
                    tt(more, more, rank, ALU.add)
                    ts(sel_mask[:, t, 0:w], more, 1.0, -NEG, ALU.subtract, ALU.mult, sels)

            def odd():
                dests = c_kv + [k_rope, k_idx] + q_idx + q_rope
                project(ODD_ROPED, dests)
                index()
                for n in range(8):
                    gemm.past().wait()
                    settle()
                    did(nc.vector.tensor_copy(y_flat[:, n * T:(n + 1) * T], banks[:, (out[0] + n) % BANKS, :]), free)
                out[0] += 8
                items = dsa_items()
                with looped_dve(4, {scored: 16, maxed: 16, exped: 16, probd: 16, own: 32, pvs: 16, os_: 2, gemm: 8,
                                    free: 8}, os_) as it:
                    def query(j, o):
                        gemm.past().wait()
                        settle()
                        did(nc.vector.tensor_copy(q_lat[j % 2][:, o, :], banks[:, o, :]), free)

                    for o in range(2):
                        query(0, o)
                    for n in range(len(items) + 1):
                        attention_item(n, items, (DSA_SCALE, None))
                        if n // 4 + 1 < 4 and n % 2:
                            query(n // 4 + 1, n % 4 // 2)
                        if n in (10, 16):
                            pvs.past(8).wait()
                            settle()
                            did(nc.vector.tensor_copy(hid[:, it * 2 + (0 if n == 10 else 1), :],
                                                      banks[:, 2 if n == 10 else 3, :]), os_)
                out[0] += 2 * HEADS
                take_y(2, plain_y)

            def project(roped_chunks, dests):
                waiting = []

                def end():
                    c = waiting.pop()
                    narrow = roped_chunks is ODD_ROPED and c in NARROW
                    rope_end(roped_chunks.index(c), dests[c], (cos32 if narrow else cos64)[:, :],
                             (sin32 if narrow else sin64)[:, :])

                for c in range(12):
                    gemm.past().wait()
                    bank = (out[0] + c) % BANKS
                    if c in roped_chunks:
                        rope_start(roped_chunks.index(c), bank)
                    else:
                        settle()
                        did(nc.vector.tensor_copy(dests[c], banks[:, bank, :]), free)
                    if waiting:
                        end()
                    if c in roped_chunks:
                        waiting.append(c)
                end()
                out[0] += 12

            def even():
                dests = [hid[:, 8 + c, :] for c in range(4)] + q_t + [kc_t, vc_t, ks_t, kw_t]
                project(EVEN_ROPED, dests)
                for t in range(TT):
                    gemm.past().wait()
                    gated.past().wait()
                    settle()
                    did(nc.vector.tensor_copy(v_tm[:, t, :], banks[:, (out[0] + t) % BANKS, 0:2 * P]), free)
                out[0] += TT
                s5()
                compress()
                nsa()
                for c in range(4):
                    if c >= 1:
                        small.past().wait()
                        tt(hid[:, c - 1, :], hid[:, c - 1, :], sg[:, (c - 1) % 2, :], ALU.mult)
                    gelu_before(hid[:, c, :], s5w[:, c % 2, :], asks)
                small.past().wait()
                tt(hid[:, 3, :], hid[:, 3, :], sg[:, 1, :], ALU.mult, s5ys)
                for c in range(4):
                    gemm.past()
                    small.past().wait()
                    tt(hid[:, 8 + c, :], hid[:, c, :], sg[:, c % 2, :], ALU.mult, free)
                out[0] += 4
                take_y(2, plain_y)

            def ple():
                gate = hid
                for c in range(DC):
                    gemm.past().wait()
                    did(nc.vector.tensor_copy(gate[:, c, :], banks[:, (out[0] + c) % BANKS, :]), free)
                out[0] += DC
                parts.past(DC).wait()
                take_y(2, lambda c, bank: did(nc.vector.tensor_tensor(
                    y[:, c, :], gate[:, c, :], banks[:, bank, :], ALU.mult), free))

            did(nc.vector.memset(eps[:, 0:1], EPS))
            did(nc.vector.memset(eps[:, 1:2], 4 * EPS))
            did(nc.vector.memset(ones[:, :], 1.0), free, BANKS)
            did(nc.vector.memset(ssum[:, :], 0.0), added, 4)
            dve.wait_ge(consts_in, 16 * len(CONSTS))
            did(nc.vector.tensor_copy(causal_b[:, :], sg[:, 0, 0:P]))
            did(nc.vector.tensor_copy(ident_b[:, :], ident[:, :]))
            did(nc.vector.tensor_copy(cmp_mask[:, :, :].rearrange("p t n -> p (t n)"), sg[:, 1, :]))
            for step in plan:
                if step[0] == "norm_in":
                    norm_in(step[1])
                elif step[0] == "norm_out":
                    norm_out(step[1])
                elif step[0] == "ffn":
                    ffn()
                elif step[0] == "even":
                    even()
                elif step[0] == "odd":
                    odd()
                elif step[0] == "odd":
                    odd()
                elif step[0] == "ple":
                    ple()

        @block.gpsimd
        def _(pool):
            scaled, hs, hns = Steps(pool, scaled_done), Steps(pool, h_done), Steps(pool, hn_done)

            for step in plan:
                if step[0] == "norm_out":
                    for c in range(DC):
                        scaled.past().wait()
                        hs.by(nc.gpsimd.tensor_tensor(h[:, c, :], h[:, c, :], tmp[:, c % 2, :], ALU.add))


def tables():
    def rotary(width):
        half = width // 2
        inv = np.float32(10000.0) ** (-np.arange(half, dtype=np.float32) / np.float32(half))
        angle = np.arange(T, dtype=np.float32)[:, None] * inv[None, :].astype(np.float32)
        rows = np.arange(P) % half
        turn = np.zeros((P, P), np.float32)
        for m in range(P):
            low = m % width < half
            turn[m + half if low else m - half, m] = -1.0 if low else 1.0
        return (np.ascontiguousarray(np.cos(angle).T[rows]), np.ascontiguousarray(np.sin(angle).T[rows]), turn)

    cos64, sin64, turn64 = rotary(HD)
    cos32, sin32, turn32 = rotary(32)
    at = np.arange(P)
    causal = np.where(at[None, :] <= at[:, None], 0.0, NEG).astype(np.float32)
    token = np.arange(T).reshape(TT, P).T
    last = at * CMP_STRIDE + CMP_LEN - 1
    seen = (at[None, None, :] < CMP) & (last[None, None, :] <= token[:, :, None])
    return {
        "cos32": cos32, "sin32": sin32, "turn32": turn32, "cos64": cos64, "sin64": sin64, "turn64": turn64, "ident": np.eye(P, dtype=np.float32),
        "causal": causal,
        "cmp_mask": np.where(seen, 0.0, NEG).astype(np.float32).reshape(P, TT * P),
        "row_valid": (token >= CMP_LEN - 1).astype(np.float32),
    }


def lay(inputs):
    def blocks(w, cols):
        k, n = w.shape
        return np.ascontiguousarray(w.reshape(k // P, P, n // cols, cols).transpose(2, 1, 0, 3)).reshape(
            n // cols, P, (k // P) * cols)

    def chunks(t):
        return np.ascontiguousarray(t.T.reshape(t.shape[1] // P, P, t.shape[0]).transpose(1, 0, 2))

    def gate_up(w):
        return np.ascontiguousarray(w.reshape(DC, P, 2, FC, P).transpose(3, 1, 0, 2, 4)).reshape(FC, P, DC * 2 * P)

    ev = inputs["ev_w_in"][0]
    q_cols = ev[:, 512:1024].reshape(D, 2, 4, HD).transpose(0, 2, 1, 3).reshape(D, 512)
    ev_out = inputs["ev_w_out"][0]
    nsa_rows = ev_out[512:].reshape(2, 4, HD, D).transpose(1, 0, 2, 3).reshape(512, D)

    def two(w):
        z = np.zeros(w.shape[:-2] + (P, P), w.dtype)
        z[..., 0:HD, 0:HD] = w
        z[..., HD:, HD:] = w
        return z

    w1s = np.stack([two(inputs[n][0].reshape(CMP_LEN, HD, HD)).transpose(1, 0, 2).reshape(P, CMP_LEN * P)
                    for n in ("nsa_wk1", "nsa_wv1")])
    w2s = np.stack([two(inputs[n][0]) for n in ("nsa_wk2", "nsa_wv2")], axis=1)
    pes = np.stack([np.tile(inputs[n][0].T, (2, 1)) for n in ("nsa_pe_k", "nsa_pe_v")], axis=1)

    def states(t):
        return t.reshape(PAIRS, P).T

    s5_prm = np.stack([states(inputs["s5_a_re"][0]), states(inputs["s5_a_im"][0]),
                       states(np.repeat(inputs["s5_log_dt"][0][:, None], STATES, axis=1))], axis=1)
    s5_b = np.zeros((2, STATES, 2, PAIRS, 2, 16), np.float32)
    s5_c = np.zeros((4, 2, STATES, 2, 4, 8, 16), np.float32)
    for c, part in enumerate(("re", "im")):
        b = inputs[f"s5_b_{part}"][0].reshape(PAIRS, 2, STATES, 16)
        cc = inputs[f"s5_c_{part}"][0].reshape(4, 4, 2, 16, STATES)
        for g in range(2):
            s5_b[g, :, c, :, g, :] = b[:, g].transpose(1, 0, 2)
            for j in range(4):
                s5_c[:, g, :, c, j, 2 * j + g, :] = cc[:, j, g].transpose(0, 2, 1)

    od = inputs["od_w_in"][0]
    k_rope, k_idx = od[:, 4864:4896], od[:, 5408:5472]
    odd_in = np.concatenate([od[:, 4608:4864], k_rope, k_rope, k_rope, k_rope, k_idx, k_idx, od[:, 4896:5408],
                             od[:, 4096:4608]], axis=1)

    order = [(layer, i) for layer in range(2) for i in (1, 2)]
    return {
        "x_t": chunks(inputs["x"][0]),
        "p_t": np.stack([chunks(inputs["p"][layer, 0]) for layer in range(2)]),
        "gains": np.ascontiguousarray(inputs["norm_g"].reshape(16, DC, P).transpose(2, 0, 1)),
        **tables(),
        "even_in": blocks(np.concatenate([ev[:, 0:512], q_cols, ev[:, 1024:1408], ev[:, 1536:1664]], axis=1), 2 * P),
        "even_tm": blocks(np.concatenate([ev[:, 1408:1536], ev[:, 1664:1792], ev[:, 1792:1816]], axis=1), TM),
        "s5_glu": blocks(inputs["s5_w_glu"][0], T),
        "even_out": blocks(np.concatenate([ev_out[0:512], nsa_rows]), 2 * P),
        "w1": w1s, "w2": np.ascontiguousarray(w2s), "pe_t": np.ascontiguousarray(pes),
        "s5_prm": np.ascontiguousarray(s5_prm), "s5_d": np.ascontiguousarray(inputs["s5_d"][0].reshape(4, P).T),
        "s5_b": s5_b.reshape(P, 2, T), "s5_c": s5_c.reshape(4, P, 2, 4, P),
        "odd_in": blocks(odd_in, 2 * P), "q_lat": blocks(od[:, 0:4096], 2 * P),
        "w_uv": blocks(inputs["od_w_uv"][0].transpose(1, 0, 2).reshape(2 * P, D), D),
        "odd_out": blocks(inputs["od_w_out"][0], 2 * P),
        "kv_gain": np.ascontiguousarray(inputs["od_kv_norm"][0].reshape(2, P).T),
        "w_idx": np.ascontiguousarray(od[:, 5472:5480].reshape(DC, P, IDX_HEADS).transpose(1, 0, 2)),
        "ffn_in": np.concatenate([gate_up(inputs[f"ffn{i}_w_in"][layer]) for layer, i in order]),
        "ffn_out": np.concatenate([blocks(inputs[f"ffn{i}_w_out"][layer], P) for layer, i in order]),
        "ple_gate": np.concatenate([blocks(inputs["ple_w_gate"][layer], 2 * P) for layer in range(2)]),
        "ple_proj": np.concatenate([blocks(inputs["ple_w_proj"][layer], D) for layer in range(2)]),
    }


def kernel(**inputs):
    import concourse.bacc as bacc
    from concourse.bass_utils import run_bass_kernel_spmd

    nc = bacc.Bacc("TRN2", target_bir_lowering=False, num_devices=1)
    arrays = lay({k: np.asarray(v) for k, v in inputs.items()})
    ap = {name: nc.dram_tensor("in_" + name, a.shape, mybir.dt.from_np(a.dtype), kind="ExternalInput").ap()
          for name, a in arrays.items()}
    ap["out_t"] = nc.dram_tensor("out_t", (P, DC, T), F32, kind="ExternalOutput").ap()
    trunk(nc, ap)
    got = run_bass_kernel_spmd(nc, [{"in_" + n: a for n, a in arrays.items()}], core_ids=[0]).results[0]["out_t"]
    return np.ascontiguousarray(np.asarray(got).transpose(2, 1, 0).reshape(1, T, D))
```

```python
from contextlib import ExitStack, contextmanager
from functools import partial

import numpy as np

import concourse.bass as bass
from concourse import mybir

F32 = mybir.dt.float32
F32R = mybir.dt.float32r
BF16 = mybir.dt.bfloat16
ALU = mybir.AluOpType
ACT = mybir.ActivationFunctionType
AX = mybir.AxisListType

P = 128
T = 512
D = 1024
DC = D // P
FF = 2816
FC = FF // P
EPS = 1e-6
SLOTS = 4
UNIT = DC * P
FO = 3
BANKS = 4
TT = T // P
NEG = -1e30
HD = 64
STATES = 64
PAIRS = 16
GELU = 2 * (2 / np.pi) ** 0.5
POW = 9
TM = 2 * P + 24
LATENT = 256
HEADS = 16
IDX_HEADS = 8
TOP = T // 4
ROUNDS = TOP // 8
LOW = -3e38
DSA_SCALE = 288 ** -0.5
CMP = 31
CMP_STRIDE = 16
CMP_LEN = 32
OWN_S5 = 4 * 13 + 1
MAGIC = 12582912.0
TWO_PI_HI = 6.28125
TWO_PI_LO = 2 * np.pi - 6.28125
PI_IN = 3.1415925

def plan_of():
    steps = []
    for layer in range(2):
        g = 8 * layer
        steps += [("norm_in", g), ("ffn", 2 * layer), ("norm_out", g + 1, 0.5),
                  ("norm_in", g + 2), ("even", 0) if layer == 0 else ("odd", 0), ("norm_out", g + 3, 1.0),
                  ("norm_in", g + 4), ("ffn", 2 * layer + 1), ("norm_out", g + 5, 0.5),
                  ("norm_in", g + 6), ("ple", layer), ("norm_out", g + 7, 1.0)]
    return steps


class Steps:

    def __init__(self, engine, semaphore, start=0):
        self.engine, self.semaphore, self.n, self.local = engine, semaphore, start, 0

    def by(self, instruction, k=1):
        instruction.then_inc(self.semaphore, k)
        self.n, self.local = self.n + k, self.local + k
        return self

    def past(self, k=1):
        self.n, self.local = self.n + k, self.local + k
        return self

    def wait(self, back=0):
        self.engine.wait_ge(self.semaphore, self.n - back)
        return self


@contextmanager
def looped(engine, trips, per, unit=None, units=0, out=None, outs=0):
    at = {s: s.n for s in per}
    with engine.Fori(0, trips) as i:
        for s, k in per.items():
            s.n, s.local = i * k + s.n, 0
        if unit:
            unit.enter(i, units)
        start = out[0] if out else 0
        yield i
    if unit:
        unit.leave(trips)
    if out:
        assert out[0] - start == outs
        out[0] = start + trips * outs
    for s, k in per.items():
        assert s.local == k, (s.semaphore, s.local, k)
        s.n = at[s] + trips * k


class Feed:

    def __init__(self):
        self.u, self.it, self.per = 0, None, 0

    def slot(self):
        return self.u % SLOTS

    def arrivals(self):
        n = 16 * (self.u // SLOTS + 1)
        return n if self.it is None else self.it * (16 * self.per // SLOTS) + n

    def next(self):
        self.u += 1

    def enter(self, it, per):
        assert per % SLOTS == 0
        self.it, self.per, self.at = it, per, self.u

    def leave(self, trips):
        assert self.u - self.at == self.per
        self.it, self.u = None, self.at + trips * self.per


UNITS = {"ffn": 2 * FC + FO * DC, "even": 12 + 3 + 2 + DC, "odd": 12 + 2 + 2 * 16 + DC, "ple": DC + 2}


def trunk(nc, ap):
    plan = plan_of()
    n_units = sum(UNITS.get(step[0], 0) for step in plan)
    with ExitStack() as ctx:
        def sb(name, shape, dt=F32):
            return ctx.enter_context(nc.sbuf_tensor(name, shape, dt))

        def sem(name):
            return ctx.enter_context(nc.semaphore(name))

        h = sb("h", [P, DC, T])
        raw = sb("raw", [P, SLOTS, UNIT])
        w_hi = sb("w_hi", [P, SLOTS, UNIT], F32R)
        w_lo = sb("w_lo", [P, SLOTS, UNIT], F32R)
        sg = sb("sg", [P, 2, T])
        ssum = sb("ssum", [P, T])
        std = sb("std", [P, T])
        rstd = sb("rstd", [P, T])
        tmp = sb("tmp", [P, 2, T])
        gains = sb("gains", [P, 16, DC])
        ones = sb("ones", [P, P])
        eps = sb("eps", [P, 2])
        warmed = sb("warmed", [P, 1])
        ident = sb("ident", [P, P])
        ident_b = sb("ident_b", [P, P], BF16)
        causal_b = sb("causal_b", [P, P], BF16)
        stat = sb("stat", [P, 3, 24])
        sq = sg

        hn_at = nc.sbuf_base
        sb("hn_region", [P, 2 * DC, T])
        arena_at = nc.sbuf_base
        ARENA = 2 * FC * T * 4
        sb("arena", [P, 2 * FC, T])

        def placed(name, offset, shape, dt=F32, base=None):
            size = 4 * int(np.prod(shape[1:])) if dt is not BF16 else 2 * int(np.prod(shape[1:]))
            assert base is not None or offset + size <= ARENA, name
            return nc.alloc_sbuf_tensor_at(name, shape, dt, offset=(arena_at if base is None else base) + offset)

        KB = 1024
        hn = (placed("hn_hi", 0, [P, DC, T], F32R, hn_at), placed("hn_lo", 16 * KB, [P, DC, T], F32R, hn_at))
        y = placed("y", 0, [P, DC, T], F32, hn_at)
        s5w = placed("s5w", 0, [P, 16, T], F32, hn_at)
        hid = (placed("hid_hi", 0, [P, FC, T], F32R), placed("hid_lo", 44 * KB, [P, FC, T], F32R))
        gate = placed("gate", 0, [P, DC, T])
        p_raw = placed("p_raw", 16 * KB, [P, 2, T])
        p_cut = (placed("p_hi", 20 * KB, [P, 2, T], F32R), placed("p_lo", 24 * KB, [P, 2, T], F32R))
        ev = placed("ev", 0, [P, 14, T])
        w1 = [placed("w1_k", 28 * KB, [P, CMP_LEN, P]), placed("w1_v", 44 * KB, [P, CMP_LEN, P])]
        c_all = placed("c_all", 28 * KB, [P, 4, 2, 4, P])
        z_cut = (placed("z_hi", 28 * KB, [P, 4, T], F32R), placed("z_lo", 36 * KB, [P, 4, T], F32R))
        mixed = (placed("ev_hi", 44 * KB, [P, DC, T], F32R), placed("ev_lo", 60 * KB, [P, DC, T], F32R))
        ev_rot = placed("ev_rot", 60 * KB, [P, 2, T])
        ev_turn = placed("ev_turn", 64 * KB, [P, P])
        small_at = [76 * KB]

        def small_tile(name, shape, dt=F32):
            t = placed(name, small_at[0], shape, dt)
            small_at[0] += -(-4 * int(np.prod(shape[1:])) // 32) * 32
            return t

        cmp_stage = small_tile("cmp_stage", [P, T])
        cmp_mask = small_tile("cmp_mask", [P, TT, P], BF16)
        row_valid = small_tile("row_valid", [P, TT])
        pe_t = small_tile("pe_t", [P, 2, CMP_LEN])
        w2 = small_tile("w2", [P, 2, P])
        gates = small_tile("gates", [P, TT, 24])
        k_cmp = small_tile("k_cmp", [P, P])
        v_cmp = small_tile("v_cmp", [P, P])
        cmp_h = small_tile("cmp_h", [P, 6, 32])
        s5_prm = small_tile("s5_prm", [P, 3, PAIRS])
        s5_d = small_tile("s5_d", [P, 5])
        s5_v = small_tile("s5_v", [P, 21, PAIRS])
        s5_pow = small_tile("s5_pow", [P, PAIRS, 19])
        s5_pow_cur = small_tile("s5_pow_cur", [P, 4, 19])
        b_cur = sb("b_cur", [P, 2, P])

        q_t = [ev[:, 4 + j, :] for j in range(4)]
        kc_t, vc_t, ks_t, kw_t = (ev[:, c, :] for c in (8, 9, 10, 11))
        v_tm = ev[:, 12:14, :].rearrange("p a t -> p (a t)").rearrange("p (t n) -> p t n", t=TT)
        blk = [s5w[:, 2 * b:2 * b + 2, :].rearrange("p a t -> p (a t)")[:, 0:CMP_LEN * CMP].rearrange(
            "p (l c) -> p l c", c=CMP) for b in range(2)]
        rots = [(s5w[:, 0, :], s5w[:, 1, :]), (sg[:, 0, :], sg[:, 1, :])]
        zs = [s5w[:, 2, :], s5w[:, 3, :]]
        xs = [s5w[:, 4, :], s5w[:, 5, :]]
        wk = [s5w[:, 6, :], s5w[:, 7, :]]
        c_cur = s5w[:, 8:10, :].rearrange("p c t -> p (c t)").rearrange("p (c j n) -> p c j n", c=2, j=4)
        b_bar = s5w[:, 4:6, :]
        b_raw = b_t = s5w[:, 14:16, :]
        q_cur, u_cur = ssum, rstd

        q_rope = placed("q_rope", 0, [P, 4, T])
        c_kv_t = placed("c_kv", 8 * KB, [P, 2, T])
        k_rope_t = placed("k_rope", 12 * KB, [P, T])
        k_idx_t = placed("k_idx", 14 * KB, [P, T])
        sel_mask = placed("sel_mask", 16 * KB, [P, TT, T], BF16)
        v_h = placed("v_h", 20 * KB, [P, TT, D])
        q_lat_t = placed("q_lat", 36 * KB, [P, 4, T])
        c_cut = (placed("c_hi", 36 * KB, [P, 2, T], F32R), placed("c_lo", 40 * KB, [P, 2, T], F32R))
        v_cur_t = placed("v_cur", 44 * KB, [P, TT, 4 * HD])
        od_probs = placed("od_probs", 48 * KB, [P, 4, T])
        od_mixed = (placed("od_hi", 56 * KB, [P, DC, T], F32R), placed("od_lo", 72 * KB, [P, DC, T], F32R))
        od_rot = placed("od_rot", 56 * KB, [P, 4, T])
        od_turn = placed("od_turn", 64 * KB, [P, 2, P])
        q_idx_t = placed("q_idx", 72 * KB, [P, 4, T])
        od_work = placed("od_work", 80 * KB, [P, 4, T])
        kv_gain = sb("kv_gain", [P, 2])
        w_idx = sb("w_idx", [P, DC, IDX_HEADS])
        w_idx_cut = (sb("w_idx_hi", [P, DC, IDX_HEADS], F32R), sb("w_idx_lo", [P, DC, IDX_HEADS], F32R))
        idx_w = sb("idx_w", [P, TT - 1, IDX_HEADS])
        top8 = sb("top8", [P, 8])
        count = sb("count", [P, 2])
        c_kv = [c_kv_t[:, c, :] for c in range(2)]
        k_rope, k_idx = k_rope_t[:, :], k_idx_t[:, :]
        q_idx = [q_idx_t[:, c, :] for c in range(4)]
        q_lat = [q_lat_t[:, 0:2, :], q_lat_t[:, 2:4, :]]
        v_cur = v_cur_t[:, :, :]
        score, found = od_work[:, 0, :], od_work[:, 1, :]
        relus = [od_work[:, 2, :], od_work[:, 3, :]]

        banks = ctx.enter_context(nc.psum_tensor("banks", [P, BANKS, T], F32))
        total = ctx.enter_context(nc.psum_tensor("total", [P, T], F32))
        xb = ctx.enter_context(nc.psum_tensor("xb", [P, 3, T], F32))
        scores = [xb[:, 0, :], xb[:, 1, :]]
        flipped = [xb[:, 2, :], total[:, :]]

        consts_in = sem("consts_in")
        x_in = sem("x_in")
        rotary_in = sem("rotary_in")
        stage_in = sem("stage_in")
        s5_in = sem("s5_in")
        p_in = sem("p_in")
        raw_in = [sem(f"raw_in{s}") for s in range(SLOTS)]
        w_hi_done = sem("w_hi_done")
        w_lo_done = sem("w_lo_done")
        unit_done = sem("unit_done")
        bank_free = sem("bank_free")
        val_raw = sem("val_raw")
        val_hi = sem("val_hi")
        val_cut = sem("val_cut")
        hid_hi_done = sem("hid_hi_done")
        hid_done = sem("hid_done")
        h_squared = sem("h_squared")
        y_squared = sem("y_squared")
        y_added = sem("y_added")
        total_step = sem("total_step")
        std_done = sem("std_done")
        scaled_done = sem("scaled_done")
        h_done = sem("h_done")
        act_part = sem("act_part")
        out_stored = sem("out_stored")
        dve_step = sem("dve_step")
        act_step = sem("act_step")
        masks_done = sem("masks_done")
        turned = sem("turned")
        roped = sem("roped")
        gates_done = sem("gates_done")
        blk_done = sem("blk_done")
        pe_step = sem("pe_step")
        small_taken = sem("small_taken")
        small_act = sem("small_act")
        dve_asks = sem("dve_asks")
        cur_done = sem("cur_done")
        bu_done = sem("bu_done")
        states_done = sem("states_done")
        rots_done = sem("rots_done")
        pool_step = sem("pool_step")
        pair_used = sem("pair_used")
        s5_y_taken = sem("s5_y_taken")
        q_done = sem("q_done")
        scores_done = sem("scores_done")
        max_done = sem("max_done")
        exp_done = sem("exp_done")
        probs_done = sem("probs_done")
        flip_done = sem("flip_done")
        flip_taken = sem("flip_taken")
        dots_done = sem("dots_done")
        relu_done = sem("relu_done")
        dots_used = sem("dots_used")
        sel_done = sem("sel_done")
        pv_done = sem("pv_done")
        o_taken = sem("o_taken")
        raised_first = {"pe": (flip_done, pv_done, scores_done, pair_used),
                        "act": (exp_done, flip_taken),
                        "dve": (states_done, states_done, s5_y_taken, o_taken)}

        def raise_first(engine, name):
            for semaphore in raised_first[name]:
                engine.sem_inc(semaphore, 1)

        block = ctx.enter_context(nc.Block())

        ODD_ROPED = [2, 3, 4, 5, 6, 7, 8, 9, 10, 11]
        NARROW = (2, 8, 9, 10, 11)
        EVEN_ROPED = [4, 5, 6, 7, 8, 10, 11]

        def dsa_items():
            return [(qt + 1, j, qt, 0) for j in range(4) for qt in range(TT)]

        def nsa_items():
            return [((1, qt + 1, qt + 1)[br], half, qt, br) for half in range(2) for qt in range(TT) for br in range(3)]

        CONSTS = [(gains[:, :, :], "gains"), (ident[:, :], "ident"), (sg[:, 0, 0:P], "causal"),
                  (kv_gain[:, :], "kv_gain"), (w_idx[:, :, :], "w_idx")]
        EVEN_ROTARY = [(ev_rot[:, 0, :], "cos64"), (ev_rot[:, 1, :], "sin64"), (ev_turn[:, :], "turn64"),
                       (s5_prm[:, :, :], "s5_prm")]
        EVEN_FIRST = [(cmp_stage[:, :], "cmp_mask"), (row_valid[:, :], "row_valid"), (pe_t[:, :, :], "pe_t"),
                      (w2[:, :, :], "w2"), (s5_d[:, 0:4], "s5_d"),
                      (w1[0][:, :, :], "w1_k"), (w1[1][:, :, :], "w1_v")]
        ODD_ROTARY = [(od_rot[:, 0, :], "cos64"), (od_rot[:, 1, :], "sin64"), (od_rot[:, 2, :], "cos32"),
                      (od_rot[:, 3, :], "sin32"), (od_turn[:, 0, :], "turn64"), (od_turn[:, 1, :], "turn32")]

        def cut(pair, *index):
            return pair[0][index], pair[1][index]

        @block.sync
        def _(sp):
            for buf, name in CONSTS:
                sp.dma_start(buf, ap[name]).then_inc(consts_in, 16)
            for c in range(DC):
                sp.dma_start(h[:, c, :], ap["x_t"][:, c, :]).then_inc(x_in, 16)
            for u in range(SLOTS):
                sp.dma_start(raw[:, u, :], ap["weights"][u, :, :]).then_inc(raw_in[u], 16)
            trips = (n_units - SLOTS) // SLOTS
            with sp.Fori(0, trips) as it:
                for k in range(SLOTS):
                    sp.wait_ge(w_lo_done, it * SLOTS + (k + 1))
                    sp.dma_start(raw[:, k, :], ap["weights"][it * SLOTS + (SLOTS + k), :, :]).then_inc(raw_in[k], 16)
            for u in range(SLOTS * (trips + 1), n_units):
                sp.wait_ge(w_lo_done, u - SLOTS + 1)
                sp.dma_start(raw[:, u % SLOTS, :], ap["weights"][u, :, :]).then_inc(raw_in[u % SLOTS], 16)
            ups = sum(DC for s in plan if s[0] == "norm_out")
            for c in range(DC):
                sp.wait_ge(h_done, ups - DC + c + 1)
                sp.dma_start(ap["out_t"][:, c, :], h[:, c, :]).then_inc(out_stored, 16)
            sp.wait_ge(out_stored, 16 * DC)

        @block.tensor
        def _(pe):
            raise_first(pe, "pe")
            free, totals = Steps(pe, bank_free), Steps(pe, total_step)
            done, feed = Steps(pe, unit_done), Steps(pe, w_lo_done)
            h_squares, added = Steps(pe, h_squared), Steps(pe, y_added)
            stds, vals, hids = Steps(pe, std_done), Steps(pe, val_cut), Steps(pe, hid_done)
            added.past(2)
            unit = Feed()
            out = [0]

            def passes(dst, a, b, first, last):
                for n, (s, m) in enumerate(((0, 0), (0, 1), (1, 0))):
                    ins = nc.tensor.matmul(dst, a[s], b[m], start=(first and n == 0), stop=(last and n == 2))
                return ins

            def take_unit():
                feed.past().wait()
                slot = unit.slot()
                unit.next()
                return w_hi[:, slot, :], w_lo[:, slot, :]

            def next_bank():
                free.past().wait()
                out[0] += 1
                return (out[0] - 1) % BANKS

            def columns(w, x, k0=0, kn=DC, bank=None, first=True, last=True, cut_before=None):
                if bank is None:
                    bank = next_bank()
                for k in range(kn):
                    if cut_before is not None:
                        pe.wait_ge(val_cut, cut_before + k + 1)
                    ins = passes(banks[:, bank, :], cut(w, slice(None), slice(k * P, (k + 1) * P)),
                                 cut(x, slice(None), k0 + k, slice(None)), first and k == 0, last and k == kn - 1)
                return ins, bank

            def looped_units(trips, per, outs, steps):
                assert outs % BANKS == 0
                return looped(pe, trips, {feed: per, done: per, free: outs, **steps}, unit, per, out, outs)

            def dense(n, x, cut_before=None):
                for i in range(n):
                    done.by(columns(take_unit(), x, cut_before=cut_before if i == 0 else None)[0])

            def all_taken():
                pe.wait_ge(bank_free, free.n + BANKS)

            def norm_in():
                if totals.n:
                    stds.past().wait()
                for c in range(DC):
                    h_squares.past().wait()
                    totals.by(nc.tensor.matmul(total[:, :], ones[:, :], sq[:, c % 2, :], start=(c == 0),
                                               stop=(c == DC - 1)))

            def norm_out():
                added.past(DC).wait()
                stds.past().wait()
                totals.by(nc.tensor.matmul(total[:, :], ones[:, :], ssum[:, :], start=True, stop=True))

            def ffn():
                before = vals.n
                vals.past(DC)
                with looped_units(FC // 2, 4, 4, {}):
                    dense(4, hn, before)
                before = hids.n
                hids.past(FC)
                with looped_units(2, 12, 4, {}):
                    for _ in range(4):
                        bank = None
                        for part, kn in enumerate((8, 8, 6)):
                            pe.wait_ge(hid_done, before + 8 * part + kn)
                            ins, bank = columns(take_unit(), hid, 8 * part, kn, bank, part == 0, part == 2)
                            done.by(ins)

            def ple():
                vals.past(DC)
                dense(DC, hn, vals.n - DC)
                vals.past(2).wait()
                for _ in range(2):
                    w = take_unit()
                    for o in range(4):
                        bank = next_bank()
                        for k in range(2):
                            ins = passes(banks[:, bank, :], cut(w, slice(None), slice(k * T + o * P, k * T + (o + 1) * P)),
                                         cut(p_cut, slice(None), k, slice(None)), k == 0, k == 1)
                    done.by(ins)

            small, taken = Steps(pe, pe_step), Steps(pe, small_taken)
            turns, ropes = Steps(pe, turned), Steps(pe, roped)
            scored, exped, probd = Steps(pe, scores_done, 1), Steps(pe, exp_done, 1), Steps(pe, probs_done)
            flips, fliptaken, pvs = Steps(pe, flip_done, 1), Steps(pe, flip_taken, 1), Steps(pe, pv_done, 1)
            curs, bus, states, pairs = Steps(pe, cur_done), Steps(pe, bu_done), Steps(pe, states_done, 2), Steps(pe, pair_used, 1)
            s5ys, qs, os_ = Steps(pe, s5_y_taken, 1), Steps(pe, q_done), Steps(pe, o_taken, 1)

            def turn(k, turner):
                ropes_free = ropes.n + k - 1
                if ropes_free >= 1:
                    pe.wait_ge(roped, ropes_free)
                turns.by(nc.tensor.matmul(xb[:, k % 2, :], turner, tmp[:, k % 2, :], start=True, stop=True))

            def s5_inputs():
                pe.wait_ge(dve_asks, 4)
                for c in range(2):
                    for q in range(4):
                        last = nc.tensor.transpose(xb[:, c, q * P:(q + 1) * P], b_bar[:, c, q * P:(q + 1) * P], ident[:, :])
                small.by(last)
                taken.past().wait()

            def s5_drive(j):
                pe.wait_ge(states_done, states.n)
                if j == 0:
                    curs.past().wait()
                rows = slice(32 * j, 32 * j + 32)
                for c in range(2):
                    last = nc.tensor.matmul(banks[:, c, :], b_cur[rows, c, :], u_cur[rows, :], start=True, stop=True,
                                            tile_position=(32 * j, 0))
                bus.by(last)

            def s5_output(j):
                states.past().wait()
                if j == 0:
                    pe.wait_ge(s5_y_taken, s5ys.n)
                for c in range(2):
                    last = nc.tensor.matmul(banks[:, 3, :], c_cur[:, c, j, :], xs[c], start=(j == 0 and c == 0),
                                            stop=(j == 3 and c == 1))
                pairs.by(last)
                if j == 3:
                    s5ys.past()

            def compress():
                pe.wait_ge(stage_in, 16 * len(EVEN_FIRST))
                for b in range(2):
                    pe.wait_ge(blk_done, b + 1)
                    for l in range(CMP_LEN):
                        last = nc.tensor.matmul(xb[:, b, 0:CMP], w1[b][:, l, :], blk[b][:, l, :],
                                                start=(l == 0), stop=(l == CMP_LEN - 1))
                    small.by(last)
                pe.wait_ge(small_taken, 2)
                small.by(nc.tensor.matmul(xb[:, 2, 0:CMP], w2[:, 0, :], cmp_h[:, 4, 0:CMP], start=True, stop=True))
                pe.wait_ge(small_taken, 4)
                small.by(nc.tensor.matmul(total[0:CMP, 0:P], cmp_h[:, 5, 0:CMP], w2[:, 1, :], start=True, stop=True))
                pe.wait_ge(small_taken, 6)
                taken.past(6)

            def scores_of(n, items, score):
                if n < len(items):
                    pe.wait_ge(exp_done, exped.n - 1 if n else exped.n)
                    score(n)
                    exped.past()

            def attention_item(n, items, value, probs):
                if 0 <= n - 1 < len(items):
                    m = n - 1
                    probd.past().wait()
                    pe.wait_ge(flip_taken, fliptaken.n)
                    w = items[m][0]
                    for b in range(w):
                        last = nc.tensor.transpose(flipped[m % 2][:, b * P:(b + 1) * P], probs[:, m % 2, b * P:(b + 1) * P],
                                                   ident[:, :])
                    flips.by(last)
                if 0 <= n - 2 < len(items):
                    m = n - 2
                    fliptaken.past().wait()
                    value(m)

            def nsa_and_s5():
                items = nsa_items()
                with looped(pe, 4, {scored: 24, exped: 24, probd: 24, flips: 24, fliptaken: 24, pvs: 24,
                                    qs: 1, os_: 1, curs: 1, bus: 4, states: 4, pairs: 4, s5ys: 1}) as j:
                    qs.past().wait()

                    def score(n):
                        w, half, qt, br = items[n]
                        rows = slice(HD * half, HD * half + HD)
                        keys = (k_cmp[:, :], ks_t, kw_t)[br]
                        dst = scores[n % 2]
                        nc.tensor.matmul(dst[:, 0:w * P], q_cur[rows, qt * P:(qt + 1) * P], keys[rows, 0:w * P],
                                         start=True, stop=False, tile_position=(HD * half, 0))
                        mask = cmp_mask[:, qt, :] if br == 0 else causal_b[:, :]
                        scored.by(nc.tensor.matmul(dst[:, (w - 1) * P:w * P], ident_b[:, :], mask, start=False, stop=True))

                    def value(m):
                        w, half, qt, br = items[m]
                        cols = slice(HD * half, HD * half + HD)
                        if half == 0 and qt == 0 and br == 0:
                            os_.wait()
                        for b in range(w):
                            v = v_cmp[:, cols] if br == 0 else v_tm[:, b, (br - 1) * P + cols.start:(br - 1) * P + cols.stop]
                            last = nc.tensor.matmul(banks[cols, 2, qt * P:(qt + 1) * P], v,
                                                    s5w[:, 12 + m % 2, b * P:(b + 1) * P], start=(br == 0),
                                                    stop=(br == 2 and b == w - 1), tile_position=(0, HD * half))
                        pvs.by(last)

                    scores_of(0, items, score)
                    for n in range(len(items) + 2):
                        scores_of(n + 1, items, score)
                        if n % 5 == 1 and n < 20:
                            s5_drive(n // 5)
                        attention_item(n, items, value, s5w[:, 10:12, :])
                        if n % 5 == 2 and 5 < n < 24:
                            s5_output(n // 5 - 1)
                    os_.past()
                qs.past()

            def project(roped_chunks, turner_of):
                seen = []
                for c in range(12):
                    dense(1, hn, vals.n - DC if c == 0 else None)
                    if c == roped_chunks[0]:
                        pe.wait_ge(rotary_in, 16 * len(EVEN_ROTARY if roped_chunks is EVEN_ROPED else
                                                       EVEN_ROTARY + ODD_ROTARY))
                    if seen:
                        pe.wait_ge(bank_free, free.n - 1 + BANKS)
                        r = seen.pop()
                        turn(roped_chunks.index(r), turner_of(r))
                    if c in roped_chunks:
                        seen.append(c)
                all_taken()
                r = seen.pop()
                turn(roped_chunks.index(r), turner_of(r))
                ropes.past(len(roped_chunks))

            def even():
                vals.past(DC)
                project(EVEN_ROPED, lambda c: ev_turn[:, :])
                tiles = [next_bank() for _ in range(TT)]
                for part, kn in enumerate((3, 3, 2)):
                    w = take_unit()
                    for t in range(TT):
                        for k in range(kn):
                            ins = passes(banks[:, tiles[t], 0:TM],
                                         cut(hn, slice(None), 3 * part + k, slice(t * P, (t + 1) * P)),
                                         cut(w, slice(None), slice(k * TM, (k + 1) * TM)),
                                         part == 0 and k == 0, part == 2 and k == kn - 1)
                    done.by(ins)
                all_taken()
                ropes.wait()
                compress()
                s5_inputs()
                nsa_and_s5()
                vals.past(8).wait()
                pe.wait_ge(s5_y_taken, s5ys.n)
                for _ in range(2):
                    w = take_unit()
                    for o in range(2):
                        bank = next_bank()
                        for k in range(4):
                            ins = passes(banks[:, bank, :], cut(w, slice(None), slice((2 * k + o) * P, (2 * k + o + 1) * P)),
                                         cut(z_cut, slice(None), k, slice(None)), k == 0, k == 3)
                    done.by(ins)
                vals.past(4).wait()
                dense(DC, mixed)

            def odd():
                vals.past(DC)
                project(ODD_ROPED, lambda c: od_turn[:, 1 if c in NARROW else 0, :])
                vals.past().wait()
                for t in range(TT - 1):
                    for k in range(DC):
                        last = passes(xb[:, 2, 8 * t:8 * t + 8], cut(hn, slice(None), k, slice((1 + t) * P, (2 + t) * P)),
                                      cut(w_idx_cut, slice(None), k, slice(None)), k == 0, k == DC - 1)
                small.by(last)
                stds.past().wait()
                for c in range(2):
                    h_squares.past().wait()
                    totals.by(nc.tensor.matmul(total[:, :], ones[:, :], relus[c], start=(c == 0), stop=(c == 1)))
                ropes.wait()
                for n in range((TT - 1) * IDX_HEADS):
                    qt, i = 1 + n // IDX_HEADS, n % IDX_HEADS
                    rows = slice(HD * (i % 2), HD * (i % 2) + HD)
                    if n >= 2:
                        pe.wait_ge(relu_done, n - 1)
                    nc.tensor.matmul(scores[n % 2][:, 0:(qt + 1) * P], q_idx[i // 2][rows, qt * P:(qt + 1) * P],
                                     k_idx[rows, 0:(qt + 1) * P], start=True, stop=True,
                                     tile_position=(HD * (i % 2), 0)).then_inc(dots_done, 1)
                taken.past().wait()
                vals.past(2).wait()
                for _ in range(2):
                    w = take_unit()
                    for t in range(TT):
                        bank = next_bank()
                        for k in range(2):
                            ins = passes(banks[:, bank, :], cut(c_cut, slice(None), k, slice(t * P, (t + 1) * P)),
                                         cut(w, slice(None), slice(k * T, (k + 1) * T)), k == 0, k == 1)
                    done.by(ins)
                all_taken()
                pe.wait_ge(sel_done, TT - 1)
                dsa()
                all_taken()
                vals.wait()
                dense(DC, od_mixed)

            def dsa():
                items = dsa_items()
                with looped(pe, 4, {scored: 16, exped: 16, probd: 16, flips: 16, fliptaken: 16, pvs: 16,
                                    qs: 1, vals: 2, feed: 8, done: 8, free: 8}, unit, 8, out, 8) as it:
                    ws = {}

                    def project_part(j, part):
                        o, upper = part // 2, part % 2
                        if not upper:
                            ws[o] = take_unit()
                            out[0] += 1
                            free.past()
                            pe.wait_ge(bank_free, free.n + 2)
                        for k in range(4 * upper, 4 * upper + 4):
                            last = passes(banks[:, o, :], cut(ws[o], slice(None), slice(k * P, (k + 1) * P)),
                                          cut(hn, slice(None), k, slice(None)), k == 0, k == DC - 1)
                        if upper:
                            done.by(last)

                    def score_of(n):
                        w, j, qt, _ = items[n]
                        dst = scores[n % 2][:, 0:w * P]
                        if n == 0:
                            all_taken()
                            qs.past().wait()
                        if qt == 0 and j:
                            all_taken()
                        for c in range(2):
                            nc.tensor.matmul(dst, q_lat[j % 2][:, c, qt * P:(qt + 1) * P], c_kv[c][:, 0:w * P],
                                             start=(c == 0), stop=False)
                        rows = slice(32 * j, 32 * j + 32)
                        nc.tensor.matmul(dst, q_cur[rows, qt * P:(qt + 1) * P], k_rope[rows, 0:w * P], start=False,
                                         stop=False, tile_position=(32 * j, 0))
                        if qt == 0:
                            scored.by(nc.tensor.matmul(dst[:, (w - 1) * P:w * P], ident_b[:, :], causal_b[:, :],
                                                       start=False, stop=True))
                        else:
                            scored.by(nc.tensor.matmul(dst, ident_b[:, :], sel_mask[:, qt - 1, 0:w * P],
                                                       start=False, stop=True))

                    def value(m):
                        w, j, qt, _ = items[m]
                        cols = slice(HD * (j % 2), HD * (j % 2) + HD)
                        if qt == 0 and j % 2 == 0:
                            if j:
                                pe.wait_ge(val_cut, vals.n - 1)
                            else:
                                vals.wait()
                            vals.past()
                        for b in range(w):
                            last = nc.tensor.matmul(banks[cols, 2 + j // 2, qt * P:(qt + 1) * P],
                                                    v_cur[:, b, HD * j:HD * j + HD], od_probs[:, 2 + m % 2, b * P:(b + 1) * P],
                                                    start=(b == 0), stop=(b == w - 1), tile_position=(0, HD * (j % 2)))
                        pvs.by(last)

                    for part in range(4):
                        project_part(0, part)
                    scores_of(0, items, score_of)
                    for n in range(len(items) + 2):
                        late = n % 4 == 3
                        if not late:
                            scores_of(n + 1, items, score_of)
                        if late and n // 4 + 1 < 4:
                            project_part(n // 4 + 1, 3)
                        attention_item(n, items, value, od_probs[:, 0:2, :])
                        if not late and n // 4 + 1 < 4:
                            project_part(n // 4 + 1, n % 4)
                        if late:
                            scores_of(n + 1, items, score_of)

            pe.wait_ge(bank_free, BANKS)
            stages = {"norm_in": norm_in, "norm_out": norm_out, "ffn": ffn, "even": even, "odd": odd, "ple": ple}
            for step in plan:
                stages[step[0]]()

        @block.scalar
        def _(act):
            raise_first(act, "act")
            free, done = Steps(act, bank_free), Steps(act, unit_done)
            h_squares, y_squares, added = Steps(act, h_squared), Steps(act, y_squared), Steps(act, y_added)
            totals, stds, hs = Steps(act, total_step), Steps(act, std_done), Steps(act, h_done)
            parts, his, hid_his = Steps(act, act_part), Steps(act, w_hi_done), Steps(act, hid_hi_done)
            raws, val_his = Steps(act, val_raw), Steps(act, val_hi)
            free.past(BANKS)
            unit = Feed()
            out = [0]

            def cut_unit():
                if unit.it is None and unit.u >= n_units:
                    return
                slot = unit.slot()
                act.wait_ge(raw_in[slot], unit.arrivals())
                his.by(nc.scalar.activation(w_hi[:, slot, :], raw[:, slot, :], ACT.Copy))
                unit.next()

            def used(n=1, wait=True):
                for _ in range(n):
                    done.past().wait()
                    cut_unit()

            def cut_value(dst, src):
                val_his.by(nc.scalar.activation(dst, src, ACT.Copy))

            def warm(func):
                own.wait()
                own.by(nc.scalar.activation(warmed[:, :], eps[:, 0:1], func))

            def norm_in():
                for c in range(DC):
                    if h_squares.n < DC:
                        act.wait_ge(x_in, 16 * DC)
                    else:
                        hs.past().wait()
                    if c >= 2:
                        act.wait_ge(total_step, totals.n + c - 1)
                    h_squares.by(nc.scalar.activation(sq[:, c % 2, :], h[:, c, :], ACT.Square))
                totals.past(DC).wait()
                stds.by(nc.scalar.activation(std[:, :], total[:, :], ACT.Sqrt, bias=eps[:, 0:1], scale=1.0 / D))

            def cut_hn():
                for c in range(DC):
                    raws.past().wait()
                    cut_value(hn[0][:, c, :], tmp[:, c % 2, :])

            def norm_out(factor):
                totals.past().wait()
                col = 0 if factor == 1.0 else 1
                stds.by(nc.scalar.activation(std[:, :], total[:, :], ACT.Sqrt, bias=eps[:, col:col + 1],
                                             scale=1.0 / (D * factor * factor)))

            def square_y(c):
                free.past().wait()
                added.past().wait()
                y_squares.by(nc.scalar.activation(sq[:, out[0] % 2, :], y[:, c, :], ACT.Square))
                out[0] += 1

            def ffn():
                bank = out[0]
                with looped(act, FC // 2, {done: 4, free: 4, parts: 2, his: 4, hid_his: 2}, unit, 4) as it:
                    for k in range(2):
                        done.past().wait()
                        free.wait(2)
                        parts.by(nc.scalar.activation(sg[:, k, :], banks[:, (bank + 2 * k) % BANKS, :], ACT.Silu))
                        cut_unit()
                        used()
                        free.past(2).wait()
                        hid_his.by(nc.scalar.activation(hid[0][:, it * 2 + k, :], tmp[:, k, :], ACT.Copy))
                out[0] += 2 * FC
                with looped(act, 2, {done: 12, free: 4, y_squares: 4, added: 4, his: 12}, unit, 12) as it:
                    for k in range(4):
                        used(3)
                        square_y(it * 4 + k)
                out[0] += 4

            def ple(layer):
                for c in range(DC):
                    used()
                    free.past().wait()
                    parts.by(nc.scalar.activation(gate[:, c, :], gate[:, c, :], ACT.Sigmoid))
                act.wait_ge(p_in, 16 * (layer + 1))
                for c in range(2):
                    cut_value(p_cut[0][:, c, :], p_raw[:, c, :])
                out[0] += DC
                for n in range(2):
                    used()
                    for o in range(4):
                        square_y(4 * n + o)

            def bring(kind, layer):
                if kind == "ple":
                    act.dma_start(p_raw[:, :, :], ap["p_t"][layer, :, :, :]).then_inc(p_in, 16)
                for buf, name in {"even": EVEN_ROTARY, "odd": ODD_ROTARY}.get(kind, []):
                    act.dma_start(buf, ap[name]).then_inc(rotary_in, 16)
                if kind == "even":
                    for buf, name in EVEN_FIRST:
                        act.dma_start(buf, ap[name]).then_inc(stage_in, 16)

            small, asks = Steps(act, small_act), Steps(act, dve_asks)
            curs, pairs, qs, pvs = Steps(act, cur_done), Steps(act, pair_used, 1), Steps(act, q_done), Steps(act, pv_done, 1)
            maxed, exped, probd = Steps(act, max_done), Steps(act, exp_done, 1), Steps(act, probs_done)
            flips, fliptaken, own = Steps(act, flip_done, 1), Steps(act, flip_taken, 1), Steps(act, act_step)
            gated, s5ys, scored = Steps(act, gates_done), Steps(act, s5_y_taken, 1), Steps(act, scores_done, 1)

            def attention_item(n, items, scale, probs, probs_t):
                if n < len(items):
                    maxed.past().wait()
                    w = items[n][0]
                    act.wait_ge(flip_done, flips.n)
                    exped.by(nc.scalar.activation(probs[:, n % 2, 0:w * P], scores[n % 2][:, 0:w * P], ACT.Exp,
                                                  bias=stat[:, 0, n:n + 1], scale=scale, accum_out=stat[:, 1, n:n + 1]))
                if 0 <= n - 1 < len(items):
                    m = n - 1
                    w = items[m][0]
                    flips.past().wait()
                    act.wait_ge(pv_done, pvs.n)
                    fliptaken.by(nc.scalar.activation(probs_t[:, m % 2, 0:w * P], flipped[m % 2][:, 0:w * P], ACT.Copy))
                    if m >= 1:
                        pvs.past()

            def odd():
                for c in range(12):
                    used()
                    free.past()
                    if c == 1:
                        free.wait()
                        for k in range(2):
                            h_squares.by(nc.scalar.activation(relus[k], c_kv[k], ACT.Square))
                cut_value(w_idx_cut[0][:, :, :], w_idx[:, :, :])
                totals.past(2).wait()
                stds.by(nc.scalar.activation(std[:, :], total[:, :], ACT.Sqrt, bias=eps[:, 0:1], scale=1.0 / LATENT))
                for c in range(2):
                    raws.past().wait()
                    cut_value(c_cut[0][:, c, :], c_kv[c])
                for n in range((TT - 1) * IDX_HEADS):
                    act.wait_ge(dots_done, n + 1)
                    if n >= 2:
                        act.wait_ge(dots_used, n - 1)
                    nc.scalar.activation(relus[n % 2][:, 0:(2 + n // IDX_HEADS) * P],
                                         scores[n % 2][:, 0:(2 + n // IDX_HEADS) * P], ACT.Relu,
                                         scale=HD ** -0.5).then_inc(relu_done, 1)
                used(2)
                free.past(8).wait()
                act.wait_ge(sel_done, TT - 1)
                items = dsa_items()
                start = scored.n
                with looped(act, 4, {maxed: 16, exped: 16, flips: 16, fliptaken: 16, pvs: 16, qs: 1, own: 1,
                                     done: 8, free: 8, his: 8, raws: 2, val_his: 2}, unit, 8) as it:
                    act.wait_ge(scores_done, it * 16 + start)
                    act.wait_ge(pv_done, pvs.n)
                    own.by(nc.scalar.activation(v_cur, v_h[:, :, bass.ds(it * 256, 256)], ACT.Copy))
                    qs.by(nc.scalar.activation(q_cur[:, :], q_rope[:, it, :], ACT.Copy))
                    used(2)
                    for n in range(len(items) + 1):
                        attention_item(n, items, DSA_SCALE, od_probs[:, 0:2, :], od_probs[:, 2:4, :])
                        if n // 4 + 1 < 4 and n % 2:
                            used()
                        if n in (11, 16):
                            raws.past().wait()
                            cut_value(od_mixed[0][:, it * 2 + (0 if n == 11 else 1), :], tmp[:, 0 if n == 11 else 1, :])
                    pvs.past()
                    free.past(8)
                out[0] += 20 + 2 * HEADS
                for c in range(DC):
                    used()
                    square_y(c)

            def even():
                for c in range(12):
                    used()
                    free.past()
                    if c == 0:
                        act.wait_ge(rotary_in, 16 * len(EVEN_ROTARY))
                        small.by(nc.scalar.activation(s5_v[:, 0, :], s5_prm[:, 2, :], ACT.Exp))
                    if c == 1:
                        asks.past().wait()
                        own.by(nc.scalar.activation(s5_v[:, 3, :], s5_v[:, 1, :], ACT.Exp))
                        own.by(nc.scalar.activation(s5_v[:, 6, :], s5_v[:, 4, :], ACT.Sin))
                        small.by(nc.scalar.activation(s5_v[:, 7, :], s5_v[:, 5, :], ACT.Sin))
                out[0] += 12
                used(3)
                act.dma_start(b_raw, ap["s5_b"]).then_inc(s5_in, 16)
                for t in range(TT):
                    gated.by(nc.scalar.activation(gates[:, t, :], banks[:, (out[0] + t) % BANKS, 2 * P:TM], ACT.Sigmoid))
                    free.past()
                out[0] += TT
                for b in range(2):
                    asks.past().wait()
                    small.by(nc.scalar.activation(cmp_h[:, 2, 0:CMP], cmp_h[:, 1, 0:CMP], ACT.Sigmoid, scale=GELU))
                act.wait_ge(small_taken, 6)
                act.dma_start(c_all[:, :, :, :, :], ap["s5_c"]).then_inc(s5_in, 16)
                asks.past(2).wait()
                act.wait_ge(s5_in, 32)
                items = nsa_items()
                qs.by(nc.scalar.activation(q_cur[:, :], ev[:, 4, :], ACT.Copy))
                with looped(act, 4, {maxed: 24, exped: 24, flips: 24, fliptaken: 24, pvs: 24, qs: 1,
                                     curs: 1, own: 4, s5ys: 1}) as j:
                    for n in range(len(items) + 1):
                        attention_item(n, items, HD ** -0.5, s5w[:, 10:12, :], s5w[:, 12:14, :])
                        if n == 0:
                            s5ys.wait()
                            s5ys.past()
                            own.by(nc.scalar.activation(u_cur[:, :], ev[:, j, :], ACT.Copy))
                            own.by(nc.scalar.activation(b_cur[:, 0, :], b_t[:, 0, bass.ds(j * P, P)], ACT.Copy))
                            own.by(nc.scalar.activation(b_cur[:, 1, :], b_t[:, 1, bass.ds(j * P, P)], ACT.Copy))
                            curs.by(nc.scalar.activation(s5_pow_cur[:, :, :], s5_pow[:, bass.ds(j * 4, 4), :],
                                                         ACT.Copy))
                        if n == 1:
                            own.by(nc.scalar.activation(c_cur, c_all[:, j, :, :, :], ACT.Copy))
                    qs.by(nc.scalar.activation(q_cur[:, :], ev[:, j + 5, :], ACT.Copy))
                    pvs.past()
                scored.past(96)
                for c in range(4):
                    asks.past().wait()
                    small.by(nc.scalar.activation(sg[:, c % 2, :], s5w[:, c % 2, :], ACT.Sigmoid, scale=GELU))
                    cut_value(mixed[0][:, c + 4, :], ev[:, c + 4, :])
                for c in range(4):
                    raws.past().wait()
                    cut_value(z_cut[0][:, c, :], ev[:, c, :])
                for c in range(4):
                    if c % 2 == 0:
                        used()
                    small.by(nc.scalar.activation(sg[:, c % 2, :], banks[:, (out[0] + c) % BANKS, :], ACT.Sigmoid))
                    free.past()
                    raws.past().wait()
                    cut_value(mixed[0][:, c, :], tmp[:, c % 2, :])
                out[0] += 4
                for c in range(DC):
                    used()
                    square_y(c)

            act.wait_ge(bank_free, BANKS)
            act.wait_ge(masks_done, 1)
            own.by(nc.scalar.activation(warmed[:, :], eps[:, 0:1], ACT.Sqrt))
            for _ in range(SLOTS):
                cut_unit()
            for n, step in enumerate(plan):
                if step[0] == "norm_in":
                    norm_in()
                    if plan[n + 1][0] == "ffn":
                        warm(ACT.Silu)
                    cut_hn()
                elif step[0] == "norm_out":
                    warm(ACT.Sqrt)
                    norm_out(step[2])
                elif step[0] == "ffn":
                    ffn()
                    if n + 3 < len(plan):
                        bring(*plan[n + 3][0:2])
                elif step[0] == "even":
                    even()
                elif step[0] == "odd":
                    odd()
                elif step[0] == "ple":
                    ple(step[1])

        @block.vector
        def _(dve):
            raise_first(dve, "dve")
            done, free = Steps(dve, unit_done), Steps(dve, bank_free)
            raws, vals = Steps(dve, val_raw), Steps(dve, val_cut)
            hids, hid_his = Steps(dve, hid_done), Steps(dve, hid_hi_done)
            y_squares, added = Steps(dve, y_squared), Steps(dve, y_added)
            stds, scaled, hs = Steps(dve, std_done), Steps(dve, scaled_done), Steps(dve, h_done)
            parts, own = Steps(dve, act_part), Steps(dve, dve_step)
            out = [0]
            last = [None]

            def did(instruction, steps=own, k=1):
                steps.by(instruction, k)
                last[0] = steps

            def settle():
                last[0].wait()

            def looped_dve(trips, per, tail):
                settle()
                last[0] = tail
                return looped(dve, trips, per)

            def root():
                stds.past().wait()
                settle()
                did(nc.vector.reciprocal(rstd[:, :], std[:, :]))
                settle()

            def norm_in(g):
                root()
                for c in range(DC):
                    if c >= 2:
                        dve.wait_ge(val_cut, vals.n + c - 1)
                    did(nc.vector.scalar_tensor_tensor(tmp[:, c % 2, :], h[:, c, :], gains[:, g, c:c + 1], rstd[:, :],
                                                       ALU.mult, ALU.mult), raws)
                vals.past(DC)

            def norm_out(g):
                root()
                for c in range(DC):
                    if hs.n + c >= 2:
                        dve.wait_ge(h_done, hs.n + c - 1)
                    did(nc.vector.scalar_tensor_tensor(tmp[:, c % 2, :], y[:, c, :], gains[:, g, c:c + 1],
                                                       rstd[:, :], ALU.mult, ALU.mult), scaled)
                hs.past(DC)

            def clear_sum():
                settle()
                did(nc.vector.memset(ssum[:, :], 0.0))

            def plain(c, bank):
                did(nc.vector.tensor_copy(y[:, c, :], banks[:, bank, :]), free)

            def take_y(c, take=plain):
                settle()
                take(c, out[0] % BANKS)
                y_squares.past().wait()
                settle()
                did(nc.vector.tensor_tensor(ssum[:, :], ssum[:, :], sq[:, out[0] % 2, :], ALU.add), added)
                out[0] += 1

            def ffn():
                bank = out[0]
                with looped_dve(FC // 2, {done: 4, free: 4, parts: 2, hids: 2, hid_his: 2}, hids) as it:
                    for k in range(2):
                        done.past(2).wait()
                        parts.past().wait()
                        settle()
                        did(nc.vector.tensor_tensor(tmp[:, k, :], sg[:, k, :],
                                                    banks[:, (bank + 2 * k + 1) % BANKS, :], ALU.mult), free, 2)
                        hid_his.past().wait()
                        settle()
                        did(nc.vector.tensor_tensor(hid[1][:, it * 2 + k, :], tmp[:, k, :],
                                                    hid[0][:, it * 2 + k, :].bitcast(F32), ALU.subtract), hids)
                out[0] += 2 * FC
                clear_sum()
                with looped_dve(2, {done: 12, free: 4, y_squares: 4, added: 4}, added) as it:
                    for k in range(4):
                        done.past(3).wait()
                        take_y(it * 4 + k)
                out[0] += 4

            def ple():
                for c in range(DC):
                    done.past().wait()
                    did(nc.vector.tensor_copy(gate[:, c, :], banks[:, (out[0] + c) % BANKS, :]), free)
                out[0] += DC
                parts.past(DC).wait()
                vals.past(2)
                clear_sum()
                for c in range(DC):
                    if c % 4 == 0:
                        done.past().wait()
                    take_y(c, lambda c, bank: did(nc.vector.tensor_tensor(
                        y[:, c, :], gate[:, c, :], banks[:, bank, :], ALU.mult), free))

            turns, ropes = Steps(dve, turned), Steps(dve, roped)
            gated, blks, small_pe, taken = Steps(dve, gates_done), Steps(dve, blk_done), Steps(dve, pe_step), Steps(dve, small_taken)
            small, asks = Steps(dve, small_act), Steps(dve, dve_asks)
            bus, states, pairs, s5ys, curs = (Steps(dve, bu_done), Steps(dve, states_done, 2), Steps(dve, pair_used, 1),
                                              Steps(dve, s5_y_taken, 1), Steps(dve, cur_done))
            scored, maxed, exped, probd = (Steps(dve, scores_done, 1), Steps(dve, max_done), Steps(dve, exp_done, 1),
                                           Steps(dve, probs_done))
            pvs, os_ = Steps(dve, pv_done, 1), Steps(dve, o_taken, 1)
            turned_by = Steps(dve, rots_done)
            dots, sels, masks = Steps(dve, dots_used), Steps(dve, sel_done), Steps(dve, masks_done)

            def tt(dst, a, b, op, steps=own):
                settle()
                did(nc.vector.tensor_tensor(dst, a, b, op), steps)

            def ts(dst, a, s1, s2, op0, op1=None, steps=own):
                settle()
                if op1 is None:
                    did(nc.vector.tensor_scalar(dst, a, s1, None, op0), steps)
                else:
                    did(nc.vector.tensor_scalar(dst, a, s1, s2, op0, op1), steps)

            def rope_start(k, bank):
                settle()
                did(nc.vector.tensor_copy(tmp[:, k % 2, :], banks[:, bank, :]), free)

            def rope_end(k, dst, cos, sin):
                turns.past().wait()
                tt(sg[:, 0, :], tmp[:, k % 2, :], cos, ALU.mult)
                tt(sg[:, 1, :], xb[:, k % 2, :], sin, ALU.mult)
                tt(dst, sg[:, 0, :], sg[:, 1, :], ALU.add, ropes)

            def gelu_before(x, t, ask):
                tt(t, x, x, ALU.mult)
                ts(t, t, 0.044715, 1.0, ALU.mult, ALU.add)
                tt(t, t, x, ALU.mult, ask)

            v = lambda k: s5_v[:, k, :]
            a_re, a_im = s5_prm[:, 0, :], s5_prm[:, 1, :]

            def s5_angles():
                small.past().wait()
                tt(v(1), a_re, v(0), ALU.mult)
                tt(v(2), a_im, v(0), ALU.mult)
                ts(v(8), v(2), 1 / (2 * np.pi), MAGIC, ALU.mult, ALU.add)
                ts(v(8), v(8), MAGIC, None, ALU.subtract)
                settle()
                did(nc.vector.scalar_tensor_tensor(v(9), v(8), -TWO_PI_HI, v(2), ALU.mult, ALU.add))
                settle()
                did(nc.vector.scalar_tensor_tensor(v(9), v(8), -TWO_PI_LO, v(9), ALU.mult, ALU.add))
                ts(v(4), v(9), PI_IN, -PI_IN, ALU.min, ALU.max)
                ts(v(5), v(4), -1.0, None, ALU.mult)
                tt(v(5), v(5), v(4), ALU.max)
                ts(v(5), v(5), -1.0, np.pi / 2, ALU.mult, ALU.add, asks)

            def s5_power(k):
                if k == 0:
                    small.past().wait()
                for k in (k,):
                    re, im = s5_pow[:, :, k], s5_pow[:, :, 9 + k]
                    if k == 0:
                        cr, ci = v(7), v(6)
                    else:
                        pr, pi = s5_pow[:, :, k - 1], s5_pow[:, :, 8 + k]
                        tt(v(10), pr, pr, ALU.mult)
                        tt(v(11), pi, pi, ALU.mult)
                        tt(v(12), v(10), v(11), ALU.subtract)
                        tt(v(13), pr, pi, ALU.mult)
                        ts(v(13), v(13), 2.0, None, ALU.mult)
                        cr, ci = v(12), v(13)
                    tt(v(10), cr, cr, ALU.mult)
                    tt(v(11), ci, ci, ALU.mult)
                    tt(v(10), v(10), v(11), ALU.add)
                    ts(v(10), v(10), -0.5, 1.5, ALU.mult, ALU.add)
                    tt(re, cr, v(10), ALU.mult)
                    tt(im, ci, v(10), ALU.mult)

            def s5_scalars():
                settle()
                did(nc.vector.tensor_copy(s5_pow[:, :, 18], v(3)))
                tt(v(14), v(3), v(7), ALU.mult)
                ts(v(14), v(14), 1.0, None, ALU.subtract)
                tt(v(15), v(3), v(6), ALU.mult)
                tt(v(16), a_re, a_re, ALU.mult)
                tt(v(17), a_im, a_im, ALU.mult)
                tt(v(16), v(16), v(17), ALU.add)
                settle()
                did(nc.vector.reciprocal(v(16), v(16)))
                tt(v(17), v(14), a_re, ALU.mult)
                tt(v(18), v(15), a_im, ALU.mult)
                tt(v(17), v(17), v(18), ALU.add)
                tt(v(17), v(17), v(16), ALU.mult)
                tt(v(18), v(15), a_re, ALU.mult)
                tt(v(19), v(14), a_im, ALU.mult)
                tt(v(18), v(18), v(19), ALU.subtract)
                tt(v(18), v(18), v(16), ALU.mult)
                col = lambda k: s5_v[:, k, :].rearrange("p (t o) -> p t o", o=1).to_broadcast([P, PAIRS, 32])
                m = lambda a: a.rearrange("p (t n) -> p t n", n=32)
                br, bi = b_raw[:, 0, :], b_raw[:, 1, :]
                dve.wait_ge(s5_in, 32)
                tt(m(zs[0]), m(br), col(17), ALU.mult)
                tt(m(zs[1]), m(bi), col(18), ALU.mult)
                tt(b_bar[:, 0, :], zs[0], zs[1], ALU.subtract)
                tt(m(zs[0]), m(bi), col(17), ALU.mult)
                tt(m(zs[1]), m(br), col(18), ALU.mult)
                tt(b_bar[:, 1, :], zs[0], zs[1], ALU.add, asks)
                small_pe.past().wait()
                settle()
                did(nc.vector.tensor_copy(b_t[:, 0, :], xb[:, 0, :]))
                did(nc.vector.tensor_copy(b_t[:, 1, :], xb[:, 1, :]), taken)
                settle()
                did(nc.vector.memset(s5_v[:, 20, :], 0.0), asks)

            def s5_part(q, j, part):
                sc = lambda k: s5_pow_cur[:, j, k:k + 1]

                rot_c, rot_s = rots[j % 2]
                if part == 1:
                    if j == 0:
                        curs.past().wait()
                    bus.past().wait()
                    turned_by.past().wait()
                    dr, di = banks[:, 0, :], banks[:, 1, :]
                    tt(wk[0], dr, rot_c, ALU.mult)
                    tt(wk[1], di, rot_s, ALU.mult)
                    tt(wk[0], wk[0], wk[1], ALU.add)
                    tt(wk[1], di, rot_c, ALU.mult)
                    tt(zs[1], dr, rot_s, ALU.mult)
                    tt(wk[1], wk[1], zs[1], ALU.subtract)
                elif part == 2:
                    decay = sc(18).to_broadcast([P, T])
                    for c in range(2):
                        settle()
                        did(nc.vector.tensor_tensor_scan(zs[c], decay, wk[c], 0.0, ALU.mult, ALU.add))
                elif part == 3:
                    pairs.wait()
                    pairs.past()
                    tt(xs[0], zs[0], rot_c, ALU.mult)
                    tt(wk[0], zs[1], rot_s, ALU.mult)
                    tt(xs[0], xs[0], wk[0], ALU.subtract)
                else:
                    tt(wk[1], zs[1], rot_c, ALU.mult)
                    tt(wk[0], zs[0], rot_s, ALU.mult)
                    settle()
                    did(nc.vector.scalar_tensor_tensor(xs[1], wk[0], -1.0, wk[1], ALU.mult, ALU.subtract), states)

            def s5_end(q):
                pairs.wait()
                settle()
                did(nc.vector.tensor_copy(s5_d[:, 4:5], s5_d[:, bass.ds(q, 1)]))
                settle()
                did(nc.vector.scalar_tensor_tensor(ev[:, q, :], u_cur[:, :], s5_d[:, 4:5], banks[:, 3, :], ALU.mult,
                                                   ALU.add), s5ys)

            def compress():
                dve.wait_ge(stage_in, 16 * len(EVEN_FIRST))
                settle()
                did(nc.vector.tensor_copy(cmp_mask[:, :, :].rearrange("p t n -> p (t n)"), cmp_stage[:, :]))
                for b, src in enumerate((kc_t, vc_t)):
                    for a in range(2):
                        part = src[:, CMP_STRIDE * a:CMP_STRIDE * (a + CMP)].rearrange("p (c l) -> p l c", l=CMP_STRIDE)
                        pe_ = pe_t[:, b, CMP_STRIDE * a:CMP_STRIDE * (a + 1)].rearrange(
                            "p (l o) -> p l o", o=1).to_broadcast([P, CMP_STRIDE, CMP])
                        tt(blk[b][:, CMP_STRIDE * a:CMP_STRIDE * (a + 1), :], part, pe_, ALU.add, own if a == 0 else blks)
                for b in range(2):
                    small_pe.past().wait()
                    x = cmp_h[:, 0, 0:CMP]
                    settle()
                    did(nc.vector.tensor_copy(x, xb[:, b, 0:CMP]), taken)
                    gelu_before(x, cmp_h[:, 1, 0:CMP], asks)
                    small.past().wait()
                    tt(cmp_h[:, 4 + b, 0:CMP], x, cmp_h[:, 2, 0:CMP], ALU.mult, taken)
                settle()
                did(nc.vector.memset(k_cmp[:, :], 0.0))
                settle()
                did(nc.vector.memset(v_cmp[:, :], 0.0))
                small_pe.past().wait()
                settle()
                did(nc.vector.tensor_copy(k_cmp[:, 0:CMP], xb[:, 2, 0:CMP]), taken)
                small_pe.past().wait()
                did(nc.vector.tensor_copy(v_cmp[0:CMP, :], total[0:CMP, 0:P]), taken)

            def attention_item(n, items, factor, probs):
                if n < len(items):
                    w = items[n][0]
                    scored.past().wait()
                    settle()
                    did(nc.vector.tensor_reduce(stat[:, 2, n:n + 1], scores[n % 2][:, 0:w * P], AX.X, ALU.max))
                    ts(stat[:, 0, n:n + 1], stat[:, 2, n:n + 1], -factor[0], None, ALU.mult, None, maxed)
                if 0 <= n - 1 < len(items):
                    m = n - 1
                    w = items[m][0]
                    exped.past().wait()
                    settle()
                    did(nc.vector.reciprocal(stat[:, 2, m:m + 1], stat[:, 1, m:m + 1]))
                    if factor[1]:
                        ts(probs[:, m % 2, 0:w * P], probs[:, m % 2, 0:w * P], stat[:, 2, m:m + 1], factor[1](m), ALU.mult,
                           ALU.mult, probd)
                    else:
                        ts(probs[:, m % 2, 0:w * P], probs[:, m % 2, 0:w * P], stat[:, 2, m:m + 1], None, ALU.mult, None,
                           probd)

            def nsa_and_s5():
                for qt in range(TT):
                    g3 = gates[:, qt, :].rearrange("p (h b) -> p h b", b=3)[:, :, 0]
                    ts(g3, g3, row_valid[:, qt:qt + 1], None, ALU.mult)
                items = nsa_items()
                with looped_dve(4, {scored: 24, maxed: 24, exped: 24, probd: 24, own: 48 + OWN_S5, pvs: 24, os_: 1,
                                    curs: 1, bus: 4, turned_by: 4, states: 4, pairs: 4, s5ys: 1}, os_) as j:
                    def factor(m):
                        w, half, qt, br = items[m]
                        return gates[:, qt, bass.ds(j * 3 + (12 * half + br), 1)]
                    for n in range(len(items) + 1):
                        attention_item(n, items, (HD ** -0.5, factor), s5w[:, 10:12, :])
                        if 0 < n < 21 and (n - 1) % 5:
                            s5_part(j, (n - 1) // 5, (n - 1) % 5)
                        if n == 23:
                            s5_end(j)
                    pvs.past(24).wait()
                    settle()
                    did(nc.vector.tensor_copy(ev[:, j + 4, :], banks[:, 2, :]), os_)

            def index():
                small_pe.past().wait()
                ts(idx_w[:, :, :], xb[:, 2, 0:8 * (TT - 1)].rearrange("p (t h) -> p t h", h=8), IDX_HEADS ** -0.5, None,
                   ALU.mult, None, taken)
                root()
                for c in range(2):
                    did(nc.vector.scalar_tensor_tensor(c_kv[c], c_kv[c], kv_gain[:, c:c + 1], rstd[:, :], ALU.mult,
                                                       ALU.mult), raws)
                vals.past(3)
                for t in range(TT - 1):
                    w = (2 + t) * P
                    for i in range(IDX_HEADS):
                        n = IDX_HEADS * t + i
                        dve.wait_ge(relu_done, n + 1)
                        settle()
                        if i == 0:
                            used = nc.vector.tensor_scalar(score[:, 0:w], relus[n % 2][:, 0:w], idx_w[:, t, i:i + 1], None,
                                                           ALU.mult)
                        else:
                            used = nc.vector.scalar_tensor_tensor(score[:, 0:w], relus[n % 2][:, 0:w], idx_w[:, t, i:i + 1],
                                                                  score[:, 0:w], ALU.mult, ALU.add)
                        did(used, dots)
                    tt(score[:, w - P:w], score[:, w - P:w], causal_b[:, :], ALU.add)
                    left = sg[:, 0, 0:w]
                    settle()
                    did(nc.vector.tensor_copy(left, score[:, 0:w]))
                    for _ in range(ROUNDS - 1):
                        settle()
                        did(nc.vector.max(top8[:, :], left))
                        settle()
                        did(nc.vector.match_replace(left, top8[:, :], left, LOW))
                    settle()
                    did(nc.vector.max(top8[:, :], left))
                    least = top8[:, 7:8]
                    more, equal, rank = found[:, 0:w], sg[:, 1, 0:w], sg[:, 0, 0:w]
                    ts(more, score[:, 0:w], least, None, ALU.is_gt)
                    settle()
                    did(nc.vector.tensor_reduce(count[:, 0:1], more, AX.X, ALU.add))
                    ts(count[:, 1:2], count[:, 0:1], -1.0, float(TOP), ALU.mult, ALU.add)
                    ts(equal, score[:, 0:w], least, None, ALU.is_equal)
                    settle()
                    did(nc.vector.tensor_tensor_scan(rank, ones[:, 0:1].to_broadcast([P, w]), equal, 0.0, ALU.mult, ALU.add))
                    settle()
                    did(nc.vector.scalar_tensor_tensor(rank, rank, count[:, 1:2], equal, ALU.is_le, ALU.mult))
                    tt(more, more, rank, ALU.add)
                    ts(sel_mask[:, t, 0:w], more, 1.0, -NEG, ALU.subtract, ALU.mult, sels)

            def odd():
                dests = c_kv + [k_rope, k_idx] + q_idx + [q_rope[:, c, :] for c in range(4)]
                project(ODD_ROPED, dests, lambda c: (od_rot[:, 2, :], od_rot[:, 3, :]) if c in NARROW else
                        (od_rot[:, 0, :], od_rot[:, 1, :]))
                index()
                for half in range(2):
                    done.past().wait()
                    for t in range(TT):
                        settle()
                        did(nc.vector.tensor_copy(v_h[:, t, half * T:(half + 1) * T],
                                                  banks[:, (out[0] + 4 * half + t) % BANKS, :]), free)
                out[0] += 8
                items = dsa_items()
                with looped_dve(4, {scored: 16, maxed: 16, exped: 16, probd: 16, own: 32, pvs: 16, raws: 2, vals: 2,
                                    done: 8, free: 8}, raws) as it:
                    def query(j, o):
                        done.past().wait()
                        settle()
                        did(nc.vector.tensor_copy(q_lat[j % 2][:, o, :], banks[:, o, :]), free)

                    for o in range(2):
                        query(0, o)
                    for n in range(len(items) + 1):
                        attention_item(n, items, (DSA_SCALE, None), od_probs[:, 0:2, :])
                        if n // 4 + 1 < 4 and n % 2:
                            query(n // 4 + 1, n % 4 // 2)
                        if n in (10, 16):
                            pvs.past(8).wait()
                            vals.wait()
                            settle()
                            did(nc.vector.tensor_copy(tmp[:, 0 if n == 10 else 1, :],
                                                      banks[:, 2 if n == 10 else 3, :]), raws)
                            vals.past()
                out[0] += 2 * HEADS
                clear_sum()
                for c in range(DC):
                    done.past().wait()
                    take_y(c)

            def project(roped_chunks, dests, rotary_of, between={}):
                waiting = []
                vals.wait()
                dve.wait_ge(rotary_in, 16 * len(EVEN_ROTARY if roped_chunks is EVEN_ROPED else
                                                EVEN_ROTARY + ODD_ROTARY))

                def end():
                    c = waiting.pop()
                    rope_end(roped_chunks.index(c), dests[c], *rotary_of(c))

                for c in range(12):
                    done.past().wait()
                    bank = (out[0] + c) % BANKS
                    if c in roped_chunks:
                        rope_start(roped_chunks.index(c), bank)
                    else:
                        settle()
                        did(nc.vector.tensor_copy(dests[c], banks[:, bank, :]), free)
                    if waiting:
                        end()
                    if c in roped_chunks:
                        waiting.append(c)
                    if c in between:
                        between[c]()
                end()
                out[0] += 12

            def even():
                dests = [ev[:, c, :] for c in range(4)] + q_t + [kc_t, vc_t, ks_t, kw_t]
                between = {0: s5_angles, **{3 + k: partial(s5_power, k) for k in range(POW)}}
                project(EVEN_ROPED, dests, lambda c: (ev_rot[:, 0, :], ev_rot[:, 1, :]), between)
                done.past(3).wait()
                for t in range(TT):
                    gated.past().wait()
                    settle()
                    did(nc.vector.tensor_copy(v_tm[:, t, :], banks[:, (out[0] + t) % BANKS, 0:2 * P]), free)
                out[0] += TT
                compress()
                s5_scalars()
                nsa_and_s5()
                for c in range(4):
                    if c >= 1:
                        small.past().wait()
                        tt(ev[:, c - 1, :], ev[:, c - 1, :], sg[:, (c - 1) % 2, :], ALU.mult, raws)
                    gelu_before(ev[:, c, :], s5w[:, c % 2, :], asks)
                small.past().wait()
                tt(ev[:, 3, :], ev[:, 3, :], sg[:, 1, :], ALU.mult, raws)
                vals.past(8)
                for c in range(4):
                    if c % 2 == 0:
                        done.past()
                    small.past().wait()
                    if c >= 2:
                        dve.wait_ge(val_cut, vals.n + c - 1)
                    settle()
                    did(nc.vector.tensor_tensor(tmp[:, c % 2, :], ev[:, c, :], sg[:, c % 2, :], ALU.mult), raws)
                    settle()
                    did(nc.vector.memset(stat[:, 0, 0:1], 0.0), free)
                vals.past(4)
                out[0] += 4
                clear_sum()
                for c in range(DC):
                    done.past().wait()
                    take_y(c)

            did(nc.vector.memset(eps[:, 0:1], EPS))
            did(nc.vector.memset(eps[:, 1:2], 4 * EPS))
            did(nc.vector.memset(ones[:, :], 1.0), free, BANKS)
            did(nc.vector.memset(ssum[:, :], 0.0), added, 2)
            dve.wait_ge(consts_in, 16 * len(CONSTS))
            did(nc.vector.tensor_copy(causal_b[:, :], sg[:, 0, 0:P]))
            did(nc.vector.tensor_copy(ident_b[:, :], ident[:, :]), masks)
            for step in plan:
                if step[0] == "norm_in":
                    norm_in(step[1])
                elif step[0] == "norm_out":
                    norm_out(step[1])
                elif step[0] == "ffn":
                    ffn()
                elif step[0] == "even":
                    even()
                elif step[0] == "odd":
                    odd()
                elif step[0] == "odd":
                    odd()
                elif step[0] == "ple":
                    ple()

        @block.gpsimd
        def _(pool):
            scaled, hs = Steps(pool, scaled_done), Steps(pool, h_done)
            his, los = Steps(pool, w_hi_done), Steps(pool, w_lo_done)
            val_his, vals = Steps(pool, val_hi), Steps(pool, val_cut)
            unit = Feed()

            def cut_unit(n=1):
                for _ in range(n):
                    if unit.it is None and unit.u >= n_units:
                        return
                    his.past().wait()
                    slot = unit.slot()
                    los.by(nc.gpsimd.tensor_tensor(w_lo[:, slot, :], raw[:, slot, :], w_hi[:, slot, :].bitcast(F32),
                                                   ALU.subtract))
                    unit.next()

            def cut_value(pair, src, *index):
                val_his.past().wait()
                hi, lo = cut(pair, *index)
                vals.by(nc.gpsimd.tensor_tensor(lo, src, hi.bitcast(F32), ALU.subtract))

            every = slice(None)
            rotated, states, own = (Steps(pool, rots_done), Steps(pool, states_done, 2),
                                          Steps(pool, pool_step))

            def rotation(trip, q):
                both = (s5w[:, 0:2, :], sg[:, 0:2, :])[q % 2]
                c, s = both[:, 0, :], both[:, 1, :]
                halves = lambda a: a.rearrange("p (c t) -> p c t", c=2)
                by_cos, by_sin = halves(std[:, :]), halves(tmp[:, 1, :])

                def step(dst, a, b, op):
                    own.by(nc.gpsimd.tensor_tensor(dst, a, b, op))

                one = ones[:, 0:1]
                step(c[:, 0:1], one, one, ALU.mult)
                step(s[:, 0:1], one, one, ALU.subtract)
                for k in range(POW):
                    m = 1 << k
                    power = lambda at: s5_pow[:, bass.ds(trip * 4 + q, 1), at:at + 1].to_broadcast([P, 2, m])
                    own.wait()
                    step(by_cos[:, :, 0:m], both[:, :, 0:m], power(k), ALU.mult)
                    step(by_sin[:, :, 0:m], both[:, :, 0:m], power(9 + k), ALU.mult)
                    own.wait()
                    step(s[:, m:2 * m], by_cos[:, 1, 0:m], by_sin[:, 0, 0:m], ALU.add)
                    rotated_by = nc.gpsimd.tensor_tensor(c[:, m:2 * m], by_cos[:, 0, 0:m], by_sin[:, 1, 0:m],
                                                         ALU.subtract)
                    if k < POW - 1:
                        own.by(rotated_by)
                rotated.by(rotated_by)

            def norm_in():
                for c in range(DC):
                    cut_value(hn, tmp[:, c % 2, :], every, c, every)

            def norm_out():
                for c in range(DC):
                    scaled.past().wait()
                    hs.by(nc.gpsimd.tensor_tensor(h[:, c, :], h[:, c, :], tmp[:, c % 2, :], ALU.add))

            def ffn():
                with looped(pool, FC // 2, {his: 4, los: 4}, unit, 4):
                    cut_unit(4)
                with looped(pool, 2, {his: 12, los: 12}, unit, 12):
                    cut_unit(12)

            def ple():
                cut_unit(DC)
                for c in range(2):
                    cut_value(p_cut, p_raw[:, c, :], every, c, every)
                cut_unit(2)

            def even():
                cut_unit(15)
                pool.wait_ge(dve_asks, 5)
                with looped(pool, 4, {rotated: 4, states: 4, own: 4 * (4 * POW + 1)}) as j:
                    for q in range(4):
                        pool.wait_ge(states_done, states.n - 1)
                        rotation(j, q)
                        states.past()
                for c in range(4):
                    cut_value(mixed, ev[:, c + 4, :], every, c + 4, every)
                for c in range(4):
                    cut_value(z_cut, ev[:, c, :], every, c, every)
                for c in range(4):
                    if c % 2 == 0:
                        cut_unit()
                    cut_value(mixed, tmp[:, c % 2, :], every, c, every)
                cut_unit(DC)

            def odd():
                cut_unit(12)
                cut_value(w_idx_cut, w_idx[:, :, :], every, every, every)
                for c in range(2):
                    cut_value(c_cut, c_kv[c], every, c, every)
                cut_unit(2)
                with looped(pool, 4, {his: 8, los: 8, val_his: 2, vals: 2}, unit, 8) as it:
                    cut_unit(2)
                    for n in range(17):
                        if n // 4 + 1 < 4 and n % 2:
                            cut_unit()
                        if n in (11, 16):
                            cut_value(od_mixed, tmp[:, 0 if n == 11 else 1, :], every, it * 2 + (0 if n == 11 else 1), every)
                cut_unit(DC)

            cut_unit(SLOTS)
            stages = {"norm_in": norm_in, "norm_out": norm_out, "ffn": ffn, "even": even, "odd": odd, "ple": ple}
            for step in plan:
                stages[step[0]]()


def tables():
    def rotary(width):
        half = width // 2
        inv = np.float32(10000.0) ** (-np.arange(half, dtype=np.float32) / np.float32(half))
        angle = np.arange(T, dtype=np.float32)[:, None] * inv[None, :].astype(np.float32)
        rows = np.arange(P) % half
        turn = np.zeros((P, P), np.float32)
        for m in range(P):
            low = m % width < half
            turn[m + half if low else m - half, m] = -1.0 if low else 1.0
        return (np.ascontiguousarray(np.cos(angle).T[rows]), np.ascontiguousarray(np.sin(angle).T[rows]), turn)

    cos64, sin64, turn64 = rotary(HD)
    cos32, sin32, turn32 = rotary(32)
    at = np.arange(P)
    causal = np.where(at[None, :] <= at[:, None], 0.0, NEG).astype(np.float32)
    token = np.arange(T).reshape(TT, P).T
    last = at * CMP_STRIDE + CMP_LEN - 1
    seen = (at[None, None, :] < CMP) & (last[None, None, :] <= token[:, :, None])
    return {
        "cos32": cos32, "sin32": sin32, "turn32": turn32, "cos64": cos64, "sin64": sin64, "turn64": turn64, "ident": np.eye(P, dtype=np.float32),
        "causal": causal,
        "cmp_mask": np.where(seen, 0.0, NEG).astype(np.float32).reshape(P, TT * P),
        "row_valid": (token >= CMP_LEN - 1).astype(np.float32),
    }


def lay(inputs):
    def blocks(w, cols):
        k, n = w.shape
        units = w.reshape(k // P, P, n // cols, cols).transpose(2, 1, 0, 3).reshape(n // cols, P, (k // P) * cols)
        return np.pad(units, ((0, 0), (0, 0), (0, UNIT - units.shape[2])))

    def chunks(t):
        return np.ascontiguousarray(t.T.reshape(t.shape[1] // P, P, t.shape[0]).transpose(1, 0, 2))

    def gate_up(w):
        return blocks(w.reshape(D, 2, FC, P).transpose(0, 2, 1, 3).reshape(D, 2 * FF), P)

    def rows(w, n, cols):
        k, width = w.shape
        whole = np.pad(w, ((0, -k % (n * P)), (0, 0)))
        parts = np.stack([blocks(part, cols) for part in np.split(whole, whole.shape[0] // (n * P))], axis=1)
        return parts.reshape(-1, P, UNIT)

    ev = inputs["ev_w_in"][0]
    q_cols = ev[:, 512:1024].reshape(D, 2, 4, HD).transpose(0, 2, 1, 3).reshape(D, 512)
    ev_out = inputs["ev_w_out"][0]
    nsa_rows = ev_out[512:].reshape(2, 4, HD, D).transpose(1, 0, 2, 3).reshape(512, D)

    def two(w):
        z = np.zeros(w.shape[:-2] + (P, P), w.dtype)
        z[..., 0:HD, 0:HD] = w
        z[..., HD:, HD:] = w
        return z

    w1s = np.stack([two(inputs[n][0].reshape(CMP_LEN, HD, HD)).transpose(1, 0, 2).reshape(P, CMP_LEN * P)
                    for n in ("nsa_wk1", "nsa_wv1")])
    w2s = np.stack([two(inputs[n][0]) for n in ("nsa_wk2", "nsa_wv2")], axis=1)
    pes = np.stack([np.tile(inputs[n][0].T, (2, 1)) for n in ("nsa_pe_k", "nsa_pe_v")], axis=1)

    def states(t):
        return t.reshape(PAIRS, P).T

    s5_prm = np.stack([states(inputs["s5_a_re"][0]), states(inputs["s5_a_im"][0]),
                       states(np.repeat(inputs["s5_log_dt"][0][:, None], STATES, axis=1))], axis=1)
    s5_b = np.zeros((2, STATES, 2, PAIRS, 2, 16), np.float32)
    s5_c = np.zeros((4, 2, STATES, 2, 4, 8, 16), np.float32)
    for c, part in enumerate(("re", "im")):
        b = inputs[f"s5_b_{part}"][0].reshape(PAIRS, 2, STATES, 16)
        cc = inputs[f"s5_c_{part}"][0].reshape(4, 4, 2, 16, STATES)
        for g in range(2):
            s5_b[g, :, c, :, g, :] = b[:, g].transpose(1, 0, 2)
            for j in range(4):
                s5_c[:, g, :, c, j, 2 * j + g, :] = cc[:, j, g].transpose(0, 2, 1)

    od = inputs["od_w_in"][0]
    k_rope, k_idx = od[:, 4864:4896], od[:, 5408:5472]
    odd_in = np.concatenate([od[:, 4608:4864], k_rope, k_rope, k_rope, k_rope, k_idx, k_idx, od[:, 4896:5408],
                             od[:, 4096:4608]], axis=1)

    even = [blocks(np.concatenate([ev[:, 0:512], q_cols, ev[:, 1024:1408], ev[:, 1536:1664]], axis=1), P),
            rows(np.concatenate([ev[:, 1408:1536], ev[:, 1664:1792], ev[:, 1792:1816]], axis=1), 3, TM),
            blocks(inputs["s5_w_glu"][0], 2 * P), blocks(np.concatenate([ev_out[0:512], nsa_rows]), P)]
    odd = [blocks(odd_in, P), blocks(inputs["od_w_uv"][0].transpose(1, 0, 2).reshape(2 * P, D), T),
           blocks(od[:, 0:4096], P), blocks(inputs["od_w_out"][0], P)]
    units = []
    for layer, mixer in enumerate((even, odd)):
        units += [gate_up(inputs["ffn1_w_in"][layer]), rows(inputs["ffn1_w_out"][layer], DC, P), *mixer,
                  gate_up(inputs["ffn2_w_in"][layer]), rows(inputs["ffn2_w_out"][layer], DC, P),
                  blocks(inputs["ple_w_gate"][layer], P), blocks(inputs["ple_w_proj"][layer], T)]
    return {
        "x_t": chunks(inputs["x"][0]),
        "p_t": np.stack([chunks(inputs["p"][layer, 0]) for layer in range(2)]),
        "gains": np.ascontiguousarray(inputs["norm_g"].reshape(16, DC, P).transpose(2, 0, 1)),
        **tables(),
        "weights": np.concatenate(units),
        "w1_k": w1s[0].reshape(P, CMP_LEN, P), "w1_v": w1s[1].reshape(P, CMP_LEN, P),
        "w2": np.ascontiguousarray(w2s), "pe_t": np.ascontiguousarray(pes),
        "s5_prm": np.ascontiguousarray(s5_prm), "s5_d": np.ascontiguousarray(inputs["s5_d"][0].reshape(4, P).T),
        "s5_b": s5_b.reshape(P, 2, T),
        "s5_c": np.ascontiguousarray(s5_c.reshape(4, P, 2, 4, P).transpose(1, 0, 2, 3, 4)),
        "kv_gain": np.ascontiguousarray(inputs["od_kv_norm"][0].reshape(2, P).T),
        "w_idx": np.ascontiguousarray(od[:, 5472:5480].reshape(DC, P, IDX_HEADS).transpose(1, 0, 2)),
    }


def kernel(**inputs):
    import concourse.bacc as bacc
    from concourse.bass_utils import run_bass_kernel_spmd

    nc = bacc.Bacc("TRN2", target_bir_lowering=False, num_devices=1)
    arrays = lay({k: np.asarray(v) for k, v in inputs.items()})
    ap = {name: nc.dram_tensor("in_" + name, a.shape, mybir.dt.from_np(a.dtype), kind="ExternalInput").ap()
          for name, a in arrays.items()}
    ap["out_t"] = nc.dram_tensor("out_t", (P, DC, T), F32, kind="ExternalOutput").ap()
    trunk(nc, ap)
    got = run_bass_kernel_spmd(nc, [{"in_" + n: a for n, a in arrays.items()}], core_ids=[0]).results[0]["out_t"]
    return np.ascontiguousarray(np.asarray(got).transpose(2, 1, 0).reshape(1, T, D))
```

```python
from contextlib import ExitStack, contextmanager
from functools import partial

import numpy as np

import concourse.bass as bass
from concourse import mybir

F32 = mybir.dt.float32
F32R = mybir.dt.float32r
BF16 = mybir.dt.bfloat16
ALU = mybir.AluOpType
ACT = mybir.ActivationFunctionType
AX = mybir.AxisListType

P = 128
T = 512
D = 1024
DC = D // P
FF = 2816
FC = FF // P
EPS = 1e-6
SLOTS = 4
UNIT = DC * P
FO = 3
BANKS = 4
TT = T // P
NEG = -1e30
HD = 64
STATES = 64
PAIRS = 16
GELU = 2 * (2 / np.pi) ** 0.5
POW = 9
TM = 2 * P + 24
LATENT = 256
HEADS = 16
IDX_HEADS = 8
TOP = T // 4
ROUNDS = TOP // 8
LOW = -3e38
DSA_SCALE = 288 ** -0.5
CMP = 31
CMP_STRIDE = 16
CMP_LEN = 32
OWN_S5 = 4 * 11 + 1
MAGIC = 12582912.0
TWO_PI_HI = 6.28125
TWO_PI_LO = 2 * np.pi - 6.28125
PI_IN = 3.1415925

BY_DVE = (2, 5, 7)
LATE = ("ffn", "ple")
BY_POOL = tuple(c for c in range(DC) if c not in BY_DVE)

def plan_of():
    steps = []
    for layer in range(2):
        g = 8 * layer
        steps += [("norm_in", g), ("ffn", 2 * layer), ("norm_out", g + 1, 0.5),
                  ("norm_in", g + 2), ("even", 0) if layer == 0 else ("odd", 0), ("norm_out", g + 3, 1.0),
                  ("norm_in", g + 4), ("ffn", 2 * layer + 1), ("norm_out", g + 5, 0.5),
                  ("norm_in", g + 6), ("ple", layer), ("norm_out", g + 7, 1.0)]
    return steps


class Steps:

    def __init__(self, engine, semaphore, start=0):
        self.engine, self.semaphore, self.n, self.local = engine, semaphore, start, 0

    def by(self, instruction, k=1):
        instruction.then_inc(self.semaphore, k)
        self.n, self.local = self.n + k, self.local + k
        return self

    def past(self, k=1):
        self.n, self.local = self.n + k, self.local + k
        return self

    def wait(self, back=0):
        self.engine.wait_ge(self.semaphore, self.n - back)
        return self


@contextmanager
def looped(engine, trips, per, unit=None, units=0, out=None, outs=0):
    at = {s: s.n for s in per}
    with engine.Fori(0, trips) as i:
        for s, k in per.items():
            s.n, s.local = i * k + s.n, 0
        if unit:
            unit.enter(i, units)
        start = out[0] if out else 0
        yield i
    if unit:
        unit.leave(trips)
    if out:
        assert out[0] - start == outs
        out[0] = start + trips * outs
    for s, k in per.items():
        assert s.local == k, (s.semaphore, s.local, k)
        s.n = at[s] + trips * k


class Feed:

    def __init__(self):
        self.u, self.it, self.per = 0, None, 0

    def slot(self):
        return self.u % SLOTS

    def arrivals(self):
        n = 16 * (self.u // SLOTS + 1)
        return n if self.it is None else self.it * (16 * self.per // SLOTS) + n

    def next(self):
        self.u += 1

    def enter(self, it, per):
        assert per % SLOTS == 0
        self.it, self.per, self.at = it, per, self.u

    def leave(self, trips):
        assert self.u - self.at == self.per
        self.it, self.u = None, self.at + trips * self.per


UNITS = {"ffn": 2 * FC + FO * DC, "even": 12 + 3 + 2 + DC, "odd": 12 + 2 + 2 * 16 + DC, "ple": DC + 2}


def trunk(nc, ap):
    plan = plan_of()
    n_units = sum(UNITS.get(step[0], 0) for step in plan)
    with ExitStack() as ctx:
        def sb(name, shape, dt=F32):
            return ctx.enter_context(nc.sbuf_tensor(name, shape, dt))

        def sem(name):
            return ctx.enter_context(nc.semaphore(name))

        h = sb("h", [P, DC, T])
        raw = sb("raw", [P, SLOTS, UNIT])
        w_hi = sb("w_hi", [P, SLOTS, UNIT], F32R)
        w_lo = sb("w_lo", [P, SLOTS, UNIT], F32R)
        sg = sb("sg", [P, 2, T])
        ssum = sb("ssum", [P, T])
        std = sb("std", [P, T])
        rstd = sb("rstd", [P, T])
        tmp = sb("tmp", [P, 2, T])
        gains = sb("gains", [P, 16, DC])
        ones = sb("ones", [P, P])
        eps = sb("eps", [P, 2])
        warmed = sb("warmed", [P, 1])
        ident = sb("ident", [P, P])
        ident_b = sb("ident_b", [P, P], BF16)
        causal_b = sb("causal_b", [P, P], BF16)
        stat = sb("stat", [P, 3, 24])
        sq = [sg[:, 0, :], sg[:, 1, :], tmp[:, 0, :], tmp[:, 1, :]]

        hn_at = nc.sbuf_base
        sb("hn_region", [P, 2 * DC, T])
        arena_at = nc.sbuf_base
        ARENA = 2 * FC * T * 4
        sb("arena", [P, 2 * FC, T])

        def placed(name, offset, shape, dt=F32, base=None):
            size = 4 * int(np.prod(shape[1:])) if dt is not BF16 else 2 * int(np.prod(shape[1:]))
            assert base is not None or offset + size <= ARENA, name
            return nc.alloc_sbuf_tensor_at(name, shape, dt, offset=(arena_at if base is None else base) + offset)

        KB = 1024
        hn = (placed("hn_hi", 0, [P, DC, T], F32R, hn_at), placed("hn_lo", 16 * KB, [P, DC, T], F32R, hn_at))
        hn_raw = placed("hn_raw", 16 * KB, [P, DC, T], F32, hn_at)
        y = placed("y", 0, [P, DC, T], F32, hn_at)
        s5w = placed("s5w", 0, [P, 16, T], F32, hn_at)
        hid = (placed("hid_hi", 0, [P, FC, T], F32R), placed("hid_lo", 44 * KB, [P, FC, T], F32R))
        gate = placed("gate", 0, [P, DC, T])
        p_raw = placed("p_raw", 16 * KB, [P, 2, T])
        p_cut = (placed("p_hi", 20 * KB, [P, 2, T], F32R), placed("p_lo", 24 * KB, [P, 2, T], F32R))
        ev = placed("ev", 0, [P, 14, T])
        w1 = [placed("w1_k", 28 * KB, [P, CMP_LEN, P]), placed("w1_v", 44 * KB, [P, CMP_LEN, P])]
        c_all = placed("c_all", 28 * KB, [P, 4, 2, 4, P])
        z_cut = (placed("z_hi", 28 * KB, [P, 4, T], F32R), placed("z_lo", 36 * KB, [P, 4, T], F32R))
        mixed = (placed("ev_hi", 44 * KB, [P, DC, T], F32R), placed("ev_lo", 60 * KB, [P, DC, T], F32R))
        turned_back_t = placed("turned_back", 44 * KB, [P, 4, T])
        ev_rot = placed("ev_rot", 60 * KB, [P, 2, T])
        ev_turn = placed("ev_turn", 64 * KB, [P, P])
        small_at = [76 * KB]

        def small_tile(name, shape, dt=F32):
            t = placed(name, small_at[0], shape, dt)
            small_at[0] += -(-4 * int(np.prod(shape[1:])) // 32) * 32
            return t

        cmp_stage = small_tile("cmp_stage", [P, T])
        cmp_mask = small_tile("cmp_mask", [P, TT, P], BF16)
        row_valid = small_tile("row_valid", [P, TT])
        pe_t = small_tile("pe_t", [P, 2, CMP_LEN])
        w2 = small_tile("w2", [P, 2, P])
        gates = small_tile("gates", [P, TT, 24])
        k_cmp = small_tile("k_cmp", [P, P])
        v_cmp = small_tile("v_cmp", [P, P])
        cmp_h = small_tile("cmp_h", [P, 6, 32])
        s5_prm = small_tile("s5_prm", [P, 3, PAIRS])
        s5_d = small_tile("s5_d", [P, 5])
        s5_v = small_tile("s5_v", [P, 21, PAIRS])
        s5_pow = small_tile("s5_pow", [P, PAIRS, 19])
        s5_pow_cur = small_tile("s5_pow_cur", [P, 4, 19])
        b_cur = sb("b_cur", [P, 2, P])

        q_t = [ev[:, 4 + j, :] for j in range(4)]
        kc_t, vc_t, ks_t, kw_t = (ev[:, c, :] for c in (8, 9, 10, 11))
        v_tm = ev[:, 12:14, :].rearrange("p a t -> p (a t)").rearrange("p (t n) -> p t n", t=TT)
        blk = [s5w[:, 2 * b:2 * b + 2, :].rearrange("p a t -> p (a t)")[:, 0:CMP_LEN * CMP].rearrange(
            "p (l c) -> p l c", c=CMP) for b in range(2)]
        rots = [(s5w[:, 0, :], s5w[:, 1, :]), (sg[:, 0, :], sg[:, 1, :])]
        zs = [s5w[:, 2, :], s5w[:, 3, :]]
        wk = [s5w[:, 4, :], s5w[:, 5, :]]
        turned_back = [turned_back_t[:, k, :] for k in range(4)]
        c_cur = s5w[:, 8:10, :].rearrange("p c t -> p (c t)").rearrange("p (c j n) -> p c j n", c=2, j=4)
        b_bar, b_parts = s5w[:, 8:10, :], [s5w[:, 6, :], s5w[:, 7, :]]
        b_raw = b_t = s5w[:, 14:16, :]
        q_cur, u_cur = ssum, rstd

        q_rope = placed("q_rope", 0, [P, 4, T])
        c_kv_t = placed("c_kv", 8 * KB, [P, 2, T])
        k_rope_t = placed("k_rope", 12 * KB, [P, T])
        k_idx_t = placed("k_idx", 14 * KB, [P, T])
        sel_mask = placed("sel_mask", 16 * KB, [P, TT, T], BF16)
        v_h = placed("v_h", 20 * KB, [P, TT, D])
        q_lat_t = placed("q_lat", 36 * KB, [P, 4, T])
        c_cut = (placed("c_hi", 36 * KB, [P, 2, T], F32R), placed("c_lo", 40 * KB, [P, 2, T], F32R))
        v_cur_t = placed("v_cur", 44 * KB, [P, TT, 4 * HD])
        od_probs = placed("od_probs", 48 * KB, [P, 4, T])
        od_mixed = (placed("od_hi", 56 * KB, [P, DC, T], F32R), placed("od_lo", 72 * KB, [P, DC, T], F32R))
        od_rot = placed("od_rot", 56 * KB, [P, 4, T])
        od_turn = placed("od_turn", 64 * KB, [P, 2, P])
        q_idx_t = placed("q_idx", 72 * KB, [P, 4, T])
        od_work = placed("od_work", 80 * KB, [P, 4, T])
        kv_gain = sb("kv_gain", [P, 2])
        w_idx = sb("w_idx", [P, DC, IDX_HEADS])
        w_idx_cut = (sb("w_idx_hi", [P, DC, IDX_HEADS], F32R), sb("w_idx_lo", [P, DC, IDX_HEADS], F32R))
        idx_w = sb("idx_w", [P, TT - 1, IDX_HEADS])
        top8 = sb("top8", [P, 8])
        count = sb("count", [P, 2])
        c_kv = [c_kv_t[:, c, :] for c in range(2)]
        k_rope, k_idx = k_rope_t[:, :], k_idx_t[:, :]
        q_idx = [q_idx_t[:, c, :] for c in range(4)]
        q_lat = [q_lat_t[:, 0:2, :], q_lat_t[:, 2:4, :]]
        v_cur = v_cur_t[:, :, :]
        score, found = od_work[:, 0, :], od_work[:, 1, :]
        relus = [od_work[:, 2, :], od_work[:, 3, :]]

        banks = ctx.enter_context(nc.psum_tensor("banks", [P, BANKS, T], F32))
        total = ctx.enter_context(nc.psum_tensor("total", [P, T], F32))
        xb = ctx.enter_context(nc.psum_tensor("xb", [P, 3, T], F32))
        scores = [xb[:, 0, :], xb[:, 1, :]]
        flipped = [xb[:, 2, :], total[:, :]]
        turned_apart = [xb[:, 2, :], total[:, :]]
        sums = xb[:, 2, 0:TT]

        consts_in = sem("consts_in")
        x_in = [sem(f"x_in{half}") for half in range(2)]
        rotary_in = sem("rotary_in")
        stage_in = sem("stage_in")
        s5_b_in = sem("s5_b_in")
        s5_c_in = sem("s5_c_in")
        p_in = sem("p_in")
        raw_in = [sem(f"raw_in{s}") for s in range(SLOTS)]
        w_hi_done = sem("w_hi_done")
        w_lo_done = sem("w_lo_done")
        unit_done = sem("unit_done")
        bank_free = sem("bank_free")
        val_raw = sem("val_raw")
        val_hi = sem("val_hi")
        val_cut = sem("val_cut")
        hid_raw = sem("hid_raw")
        hid_hi_done = sem("hid_hi_done")
        hid_done = sem("hid_done")
        h_squared = sem("h_squared")
        y_squared = sem("y_squared")
        y_added = sem("y_added")
        total_step = sem("total_step")
        std_done = sem("std_done")
        diag_done = sem("diag_done")
        scaled_done = sem("scaled_done")
        h_done = sem("h_done")
        h_done_dve = sem("h_done_dve")
        hn_cut_dve = sem("hn_cut_dve")
        act_part = sem("act_part")
        out_stored = sem("out_stored")
        dve_step = sem("dve_step")
        act_step = sem("act_step")
        turned = sem("turned")
        roped = sem("roped")
        gates_done = sem("gates_done")
        blk_done = sem("blk_done")
        pe_step = sem("pe_step")
        small_taken = sem("small_taken")
        small_act = sem("small_act")
        dve_asks = sem("dve_asks")
        cur_done = sem("cur_done")
        bu_done = sem("bu_done")
        states_done = sem("states_done")
        rots_done = sem("rots_done")
        pool_step = sem("pool_step")
        pair_used = sem("pair_used")
        s5_y_taken = sem("s5_y_taken")
        q_done = sem("q_done")
        scores_done = sem("scores_done")
        max_done = sem("max_done")
        exp_done = sem("exp_done")
        probs_done = sem("probs_done")
        flip_done = sem("flip_done")
        flip_taken = sem("flip_taken")
        dots_done = sem("dots_done")
        relu_done = sem("relu_done")
        dots_used = sem("dots_used")
        sel_done = sem("sel_done")
        pv_done = sem("pv_done")
        o_taken = sem("o_taken")
        raised_first = {"pe": (flip_done, pv_done, scores_done, pair_used),
                        "act": (exp_done, flip_taken),
                        "dve": (states_done, states_done, s5_y_taken, o_taken)}

        def raise_first(engine, name):
            for semaphore in raised_first[name]:
                engine.sem_inc(semaphore, 1)

        block = ctx.enter_context(nc.Block())

        ODD_ROPED = [2, 3, 4, 5, 6, 7, 8, 9, 10, 11]
        NARROW = (2, 8, 9, 10, 11)
        EVEN_ROPED = [4, 5, 6, 7, 8, 10, 11]

        def dsa_items():
            return [(qt + 1, j, qt, 0) for j in range(4) for qt in range(TT)]

        def nsa_items():
            return [((1, qt + 1, qt + 1)[br], half, qt, br) for half in range(2) for qt in range(TT) for br in range(3)]

        CONSTS = [(gains[:, :, :], "gains"), (ident[:, :], "ident"), (rstd[:, 0:P], "causal"),
                  (kv_gain[:, :], "kv_gain"), (w_idx[:, :, :], "w_idx")]
        EVEN_ROTARY = [(ev_rot[:, 0, :], "cos64"), (ev_rot[:, 1, :], "sin64"), (ev_turn[:, :], "turn64"),
                       (s5_prm[:, :, :], "s5_prm")]
        EVEN_FIRST = [(cmp_stage[:, :], "cmp_mask"), (row_valid[:, :], "row_valid"), (pe_t[:, :, :], "pe_t"),
                      (w2[:, :, :], "w2"), (s5_d[:, 0:4], "s5_d"),
                      (w1[0][:, :, :], "w1_k"), (w1[1][:, :, :], "w1_v")]
        ODD_ROTARY = [(od_rot[:, 0, :], "cos64"), (od_rot[:, 1, :], "sin64"), (od_rot[:, 2, :], "cos32"),
                      (od_rot[:, 3, :], "sin32"), (od_turn[:, 0, :], "turn64"), (od_turn[:, 1, :], "turn32")]

        def cut(pair, *index):
            return pair[0][index], pair[1][index]

        @block.sync
        def _(sp):
            for half in range(2):
                chunks = slice(half * DC // 2, (half + 1) * DC // 2)
                sp.dma_start(h[:, chunks, :], ap["x_t"][:, chunks, :]).then_inc(x_in[half], 16)
            for u in range(SLOTS):
                sp.dma_start(raw[:, u, :], ap["weights"][u, :, :]).then_inc(raw_in[u], 16)
            trips = (n_units - SLOTS) // SLOTS
            with sp.Fori(0, trips) as it:
                for k in range(SLOTS):
                    sp.wait_ge(w_lo_done, it * SLOTS + (k + 1))
                    sp.dma_start(raw[:, k, :], ap["weights"][it * SLOTS + (SLOTS + k), :, :]).then_inc(raw_in[k], 16)
            for u in range(SLOTS * (trips + 1), n_units):
                sp.wait_ge(w_lo_done, u - SLOTS + 1)
                sp.dma_start(raw[:, u % SLOTS, :], ap["weights"][u, :, :]).then_inc(raw_in[u % SLOTS], 16)
            ups = sum(1 for s in plan if s[0] == "norm_out") - 1
            for c in range(DC):
                if c in BY_DVE:
                    sp.wait_ge(h_done_dve, ups * len(BY_DVE) + BY_DVE.index(c) + 1)
                else:
                    sp.wait_ge(h_done, ups * len(BY_POOL) + BY_POOL.index(c) + 1)
                sp.dma_start(ap["out_t"][:, c, :], h[:, c, :]).then_inc(out_stored, 16)
            sp.wait_ge(out_stored, 16 * DC)

        @block.tensor
        def _(pe):
            raise_first(pe, "pe")
            free, totals = Steps(pe, bank_free), Steps(pe, total_step)
            done, feed = Steps(pe, unit_done), Steps(pe, w_lo_done)
            h_squares, added = Steps(pe, h_squared), Steps(pe, y_added)
            stds, vals, hids = Steps(pe, std_done), Steps(pe, val_cut), Steps(pe, hid_done)
            diags, hn_dve = Steps(pe, diag_done), Steps(pe, hn_cut_dve)
            added.past(2)
            unit = Feed()
            out = [0]

            def passes(dst, a, b, first, last):
                for n, (s, m) in enumerate(((0, 0), (0, 1), (1, 0))):
                    ins = nc.tensor.matmul(dst, a[s], b[m], start=(first and n == 0), stop=(last and n == 2))
                return ins

            def take_unit():
                feed.past().wait()
                slot = unit.slot()
                unit.next()
                return w_hi[:, slot, :], w_lo[:, slot, :]

            def next_bank():
                free.past().wait()
                out[0] += 1
                return (out[0] - 1) % BANKS

            def columns(w, x, k0=0, kn=DC, bank=None, first=True, last=True, arriving=None):
                if bank is None:
                    bank = next_bank()
                for n, (k, semaphore, count) in enumerate(arriving or [(k, None, 0) for k in range(kn)]):
                    if semaphore is not None:
                        pe.wait_ge(semaphore, count)
                    ins = passes(banks[:, bank, :], cut(w, slice(None), slice(k * P, (k + 1) * P)),
                                 cut(x, slice(None), k0 + k, slice(None)), first and n == 0, last and n == kn - 1)
                return ins, bank

            def hn_arriving():
                by_pool, by_dve = vals.n, hn_dve.n
                vals.past(len(BY_POOL))
                hn_dve.past(len(BY_DVE))
                return [(c, hn_cut_dve, by_dve + BY_DVE.index(c) + 1) if c in BY_DVE else
                        (c, val_cut, by_pool + BY_POOL.index(c) + 1) for c in range(DC)]

            def looped_units(trips, per, outs, steps):
                assert outs % BANKS == 0
                return looped(pe, trips, {feed: per, done: per, free: outs, **steps}, unit, per, out, outs)

            def dense(n, x, arriving=None):
                for i in range(n):
                    done.by(columns(take_unit(), x, arriving=arriving if i == 0 else None)[0])

            def all_taken():
                pe.wait_ge(bank_free, free.n + BANKS)

            def sum_up(bank, squares, first, last):
                totals.by(nc.tensor.matmul(bank, ones[:, :], squares, start=first, stop=last))

            def norm_in():
                if totals.n:
                    stds.past().wait()
                for c in range(DC):
                    h_squares.past().wait()
                    sum_up(xb[:, 2, :], sq[c % 4], c == 0, c == DC - 1)

            def norm_out():
                added.past(DC).wait()
                stds.past().wait()
                for t in range(TT):
                    ins = nc.tensor.matmul(sums[:, t:t + 1], ssum[:, t * P:(t + 1) * P], ones[:, 0:1], start=(t == 0),
                                           stop=(t == TT - 1))
                totals.by(ins)
                diags.past().wait()
                totals.by(nc.tensor.matmul(total[:, :], ones[:, :], rstd[:, :], start=True, stop=True))

            def ffn():
                arriving = hn_arriving()
                with looped_units(FC // 2, 4, 4, {}):
                    dense(4, hn, arriving)
                before = hids.n
                hids.past(FC)
                with looped_units(2, 12, 4, {}):
                    for _ in range(4):
                        bank = None
                        for part, kn in enumerate((8, 8, 6)):
                            pe.wait_ge(hid_done, before + 8 * part + kn)
                            ins, bank = columns(take_unit(), hid, 8 * part, kn, bank, part == 0, part == 2)
                            done.by(ins)

            def ple():
                dense(DC, hn, hn_arriving())
                vals.past(2).wait()
                for _ in range(2):
                    w = take_unit()
                    for o in range(4):
                        bank = next_bank()
                        for k in range(2):
                            ins = passes(banks[:, bank, :], cut(w, slice(None), slice(k * T + o * P, k * T + (o + 1) * P)),
                                         cut(p_cut, slice(None), k, slice(None)), k == 0, k == 1)
                    done.by(ins)

            small, taken = Steps(pe, pe_step), Steps(pe, small_taken)
            turns, ropes = Steps(pe, turned), Steps(pe, roped)
            scored, exped, probd = Steps(pe, scores_done, 1), Steps(pe, exp_done, 1), Steps(pe, probs_done)
            flips, fliptaken, pvs = Steps(pe, flip_done, 1), Steps(pe, flip_taken, 1), Steps(pe, pv_done, 1)
            curs, bus, states, pairs = Steps(pe, cur_done), Steps(pe, bu_done), Steps(pe, states_done, 2), Steps(pe, pair_used, 1)
            s5ys, qs, os_ = Steps(pe, s5_y_taken, 1), Steps(pe, q_done), Steps(pe, o_taken, 1)

            def turn(k, turner):
                ropes_free = ropes.n + k - 1
                if ropes_free >= 1:
                    pe.wait_ge(roped, ropes_free)
                turns.by(nc.tensor.matmul(xb[:, k % 2, :], turner, tmp[:, k % 2, :], start=True, stop=True))

            def turn_apart(k, turner):
                if k >= 8:
                    pe.wait_ge(roped, ropes.n + k - 7)
                turns.by(nc.tensor.matmul(turned_apart[k % 2], turner, tmp[:, k % 2, :], start=True, stop=True))

            def s5_inputs():
                pe.wait_ge(dve_asks, 2)
                for c in range(2):
                    for q in range(4):
                        last = nc.tensor.transpose(xb[:, c, q * P:(q + 1) * P], b_bar[:, c, q * P:(q + 1) * P], ident[:, :])
                small.by(last)
                taken.past().wait()

            def s5_drive(j):
                pe.wait_ge(states_done, states.n)
                if j == 0:
                    curs.past().wait()
                rows = slice(32 * j, 32 * j + 32)
                for c in range(2):
                    last = nc.tensor.matmul(banks[:, c, :], b_cur[rows, c, :], u_cur[rows, :], start=True, stop=True,
                                            tile_position=(32 * j, 0))
                bus.by(last)

            def s5_output(j):
                states.past().wait()
                if j == 0:
                    pe.wait_ge(s5_y_taken, s5ys.n)
                for k in range(4):
                    last = nc.tensor.matmul(banks[:, 3, :], c_cur[:, k // 2, j, :], turned_back[k],
                                            start=(j == 0 and k == 0), stop=(j == 3 and k == 3))
                pairs.by(last)
                if j == 3:
                    s5ys.past()

            def compress():
                pe.wait_ge(stage_in, 16 * len(EVEN_FIRST))
                for b in range(2):
                    pe.wait_ge(blk_done, b + 1)
                    for l in range(CMP_LEN):
                        last = nc.tensor.matmul(xb[:, b, 0:CMP], w1[b][:, l, :], blk[b][:, l, :],
                                                start=(l == 0), stop=(l == CMP_LEN - 1))
                    small.by(last)
                pe.wait_ge(small_taken, 2)
                small.by(nc.tensor.matmul(xb[:, 2, 0:CMP], w2[:, 0, :], cmp_h[:, 4, 0:CMP], start=True, stop=True))
                pe.wait_ge(small_taken, 4)
                small.by(nc.tensor.matmul(total[0:CMP, 0:P], cmp_h[:, 5, 0:CMP], w2[:, 1, :], start=True, stop=True))
                pe.wait_ge(small_taken, 6)
                taken.past(6)

            def scores_of(n, items, score):
                if n < len(items):
                    pe.wait_ge(exp_done, exped.n - 1 if n else exped.n)
                    score(n)
                    exped.past()

            def attention_item(n, items, value, probs):
                if 0 <= n - 1 < len(items):
                    m = n - 1
                    probd.past().wait()
                    pe.wait_ge(flip_taken, fliptaken.n)
                    w = items[m][0]
                    for b in range(w):
                        last = nc.tensor.transpose(flipped[m % 2][:, b * P:(b + 1) * P], probs[:, m % 2, b * P:(b + 1) * P],
                                                   ident[:, :])
                    flips.by(last)
                if 0 <= n - 2 < len(items):
                    m = n - 2
                    fliptaken.past().wait()
                    value(m)

            def nsa_and_s5():
                items = nsa_items()
                with looped(pe, 4, {scored: 24, exped: 24, probd: 24, flips: 24, fliptaken: 24, pvs: 24,
                                    qs: 1, os_: 1, curs: 1, bus: 4, states: 4, pairs: 4, s5ys: 1}) as j:
                    qs.past().wait()

                    def score(n):
                        w, half, qt, br = items[n]
                        rows = slice(HD * half, HD * half + HD)
                        keys = (k_cmp[:, :], ks_t, kw_t)[br]
                        dst = scores[n % 2]
                        nc.tensor.matmul(dst[:, 0:w * P], q_cur[rows, qt * P:(qt + 1) * P], keys[rows, 0:w * P],
                                         start=True, stop=False, tile_position=(HD * half, 0))
                        mask = cmp_mask[:, qt, :] if br == 0 else causal_b[:, :]
                        scored.by(nc.tensor.matmul(dst[:, (w - 1) * P:w * P], ident_b[:, :], mask, start=False, stop=True))

                    def value(m):
                        w, half, qt, br = items[m]
                        cols = slice(HD * half, HD * half + HD)
                        if half == 0 and qt == 0 and br == 0:
                            os_.wait()
                        for b in range(w):
                            v = v_cmp[:, cols] if br == 0 else v_tm[:, b, (br - 1) * P + cols.start:(br - 1) * P + cols.stop]
                            last = nc.tensor.matmul(banks[cols, 2, qt * P:(qt + 1) * P], v,
                                                    s5w[:, 12 + m % 2, b * P:(b + 1) * P], start=(br == 0),
                                                    stop=(br == 2 and b == w - 1), tile_position=(0, HD * half))
                        pvs.by(last)

                    scores_of(0, items, score)
                    for n in range(len(items) + 2):
                        scores_of(n + 1, items, score)
                        if n % 5 == 1 and n < 20:
                            s5_drive(n // 5)
                        attention_item(n, items, value, s5w[:, 10:12, :])
                        if n % 5 == 3 and 5 < n < 24:
                            s5_output(n // 5 - 1)
                    os_.past()
                qs.past()

            def project(units, roped_chunks, turner_of):
                seen = []
                arriving = hn_arriving()
                for c in range(units):
                    dense(1, hn, arriving if c == 0 else None)
                    if c == roped_chunks[0]:
                        pe.wait_ge(rotary_in, 16 * len(EVEN_ROTARY if roped_chunks is EVEN_ROPED else
                                                       EVEN_ROTARY + ODD_ROTARY))
                    if seen:
                        pe.wait_ge(bank_free, free.n - 1 + BANKS)
                        r = seen.pop()
                        turn(roped_chunks.index(r), turner_of(r))
                    if c in roped_chunks:
                        seen.append(c)
                all_taken()
                r = seen.pop()
                turn(roped_chunks.index(r), turner_of(r))
                ropes.past(sum(c < units for c in roped_chunks))

            def even():
                project(12, EVEN_ROPED, lambda c: ev_turn[:, :])
                tiles = [next_bank() for _ in range(TT)]
                for part, kn in enumerate((3, 3, 2)):
                    w = take_unit()
                    for t in range(TT):
                        for k in range(kn):
                            ins = passes(banks[:, tiles[t], 0:TM],
                                         cut(hn, slice(None), 3 * part + k, slice(t * P, (t + 1) * P)),
                                         cut(w, slice(None), slice(k * TM, (k + 1) * TM)),
                                         part == 0 and k == 0, part == 2 and k == kn - 1)
                    done.by(ins)
                all_taken()
                ropes.wait()
                compress()
                s5_inputs()
                nsa_and_s5()
                pe.wait_ge(s5_y_taken, s5ys.n)
                before = vals.n
                vals.past(12)
                w = [take_unit() for _ in range(2)]
                outs = [next_bank() for _ in range(4)]
                for k in range(4):
                    pe.wait_ge(val_cut, before + 2 * (k + 1))
                    for o in range(4):
                        at = (2 * k + o % 2) * P
                        ins = passes(banks[:, outs[o], :], cut(w[o // 2], slice(None), slice(at, at + P)),
                                     cut(z_cut, slice(None), k, slice(None)), k == 0, k == 3)
                        if k == 3 and o % 2:
                            done.by(ins)
                dense(DC, mixed, [(k, None, 0) for k in range(4, DC)] + [(k, val_cut, before + 9 + k) for k in range(4)])

            def odd():
                project(8, ODD_ROPED, lambda c: od_turn[:, 1 if c in NARROW else 0, :])
                vals.past().wait()
                for t in range(TT - 1):
                    for k in range(DC):
                        last = passes(xb[:, 2, 8 * t:8 * t + 8], cut(hn, slice(None), k, slice((1 + t) * P, (2 + t) * P)),
                                      cut(w_idx_cut, slice(None), k, slice(None)), k == 0, k == DC - 1)
                small.by(last)
                stds.past().wait()
                for c in range(2):
                    h_squares.past().wait()
                    sum_up(total[:, :], relus[c], c == 0, c == 1)
                ropes.wait()
                taken.past()
                for t in range(TT - 1):
                    for i in range(IDX_HEADS):
                        n, qt = IDX_HEADS * t + i, 1 + t
                        rows = slice(HD * (i % 2), HD * (i % 2) + HD)
                        if n >= 2:
                            pe.wait_ge(relu_done, n - 1)
                        nc.tensor.matmul(scores[n % 2][:, 0:(qt + 1) * P], q_idx[i // 2][rows, qt * P:(qt + 1) * P],
                                         k_idx[rows, 0:(qt + 1) * P], start=True, stop=True,
                                         tile_position=(HD * (i % 2), 0)).then_inc(dots_done, 1)
                    if t == 0:
                        dense(4, hn)
                        taken.wait()
                        pe.wait_ge(std_done, stds.n + 1)
                        for c in range(8, 12):
                            pe.wait_ge(bank_free, free.n - 11 + c + BANKS)
                            turn_apart(ODD_ROPED.index(c), od_turn[:, 1, :])
                        ropes.past(4)
                        vals.past(2).wait()
                    else:
                        values_from_latent()
                all_taken()
                pe.wait_ge(sel_done, TT - 1)
                dsa()
                all_taken()
                vals.wait()
                dense(DC, od_mixed)

            def values_from_latent():
                w = take_unit()
                for t in range(TT):
                    bank = next_bank()
                    for k in range(2):
                        ins = passes(banks[:, bank, :], cut(c_cut, slice(None), k, slice(t * P, (t + 1) * P)),
                                     cut(w, slice(None), slice(k * T, (k + 1) * T)), k == 0, k == 1)
                done.by(ins)

            def dsa():
                items = dsa_items()
                with looped(pe, 4, {scored: 16, exped: 16, probd: 16, flips: 16, fliptaken: 16, pvs: 16,
                                    qs: 1, vals: 2, feed: 8, done: 8, free: 8}, unit, 8, out, 8) as it:
                    ws = {}

                    def project_part(j, part):
                        o, upper = part // 2, part % 2
                        if not upper:
                            ws[o] = take_unit()
                            out[0] += 1
                            free.past()
                            pe.wait_ge(bank_free, free.n + 2)
                        for k in range(4 * upper, 4 * upper + 4):
                            last = passes(banks[:, o, :], cut(ws[o], slice(None), slice(k * P, (k + 1) * P)),
                                          cut(hn, slice(None), k, slice(None)), k == 0, k == DC - 1)
                        if upper:
                            done.by(last)

                    def score_of(n):
                        w, j, qt, _ = items[n]
                        dst = scores[n % 2][:, 0:w * P]
                        if n == 0:
                            all_taken()
                            qs.past().wait()
                        if qt == 0 and j:
                            all_taken()
                        for c in range(2):
                            nc.tensor.matmul(dst, q_lat[j % 2][:, c, qt * P:(qt + 1) * P], c_kv[c][:, 0:w * P],
                                             start=(c == 0), stop=False)
                        rows = slice(32 * j, 32 * j + 32)
                        nc.tensor.matmul(dst, q_cur[rows, qt * P:(qt + 1) * P], k_rope[rows, 0:w * P], start=False,
                                         stop=False, tile_position=(32 * j, 0))
                        if qt == 0:
                            scored.by(nc.tensor.matmul(dst[:, (w - 1) * P:w * P], ident_b[:, :], causal_b[:, :],
                                                       start=False, stop=True))
                        else:
                            scored.by(nc.tensor.matmul(dst, ident_b[:, :], sel_mask[:, qt - 1, 0:w * P],
                                                       start=False, stop=True))

                    def value(m):
                        w, j, qt, _ = items[m]
                        cols = slice(HD * (j % 2), HD * (j % 2) + HD)
                        if qt == 0 and j % 2 == 0:
                            if j:
                                pe.wait_ge(val_cut, vals.n - 1)
                            else:
                                vals.wait()
                            vals.past()
                        for b in range(w):
                            last = nc.tensor.matmul(banks[cols, 2 + j // 2, qt * P:(qt + 1) * P],
                                                    v_cur[:, b, HD * j:HD * j + HD], od_probs[:, 2 + m % 2, b * P:(b + 1) * P],
                                                    start=(b == 0), stop=(b == w - 1), tile_position=(0, HD * (j % 2)))
                        pvs.by(last)

                    for part in range(4):
                        project_part(0, part)
                    scores_of(0, items, score_of)
                    for n in range(len(items) + 2):
                        late = n % 4 == 3
                        if not late:
                            scores_of(n + 1, items, score_of)
                        if late and n // 4 + 1 < 4:
                            project_part(n // 4 + 1, 3)
                        attention_item(n, items, value, od_probs[:, 0:2, :])
                        if not late and n // 4 + 1 < 4:
                            project_part(n // 4 + 1, n % 4)
                        if late:
                            scores_of(n + 1, items, score_of)

            pe.wait_ge(bank_free, BANKS)
            stages = {"norm_in": norm_in, "norm_out": norm_out, "ffn": ffn, "even": even, "odd": odd, "ple": ple}
            for step in plan:
                stages[step[0]]()

        @block.scalar
        def _(act):
            raise_first(act, "act")
            free, done = Steps(act, bank_free), Steps(act, unit_done)
            h_squares, y_squares, added = Steps(act, h_squared), Steps(act, y_squared), Steps(act, y_added)
            totals, stds, hs = Steps(act, total_step), Steps(act, std_done), Steps(act, h_done)
            hs_dve = Steps(act, h_done_dve)
            parts, his, hid_his = Steps(act, act_part), Steps(act, w_hi_done), Steps(act, hid_hi_done)
            raws, val_his, hid_raws = Steps(act, val_raw), Steps(act, val_hi), Steps(act, hid_raw)
            free.past(BANKS)
            unit = Feed()
            out = [0]

            def cut_unit():
                if unit.it is None and unit.u >= n_units:
                    return
                slot = unit.slot()
                act.wait_ge(raw_in[slot], unit.arrivals())
                his.by(nc.scalar.activation(w_hi[:, slot, :], raw[:, slot, :], ACT.Copy))
                unit.next()

            def used(n=1):
                for _ in range(n):
                    done.past().wait()
                    cut_unit()

            def cut_value(dst, src):
                val_his.by(nc.scalar.activation(dst, src, ACT.Copy))

            def warm(func):
                own.wait()
                own.by(nc.scalar.activation(warmed[:, :], eps[:, 0:1], func))

            def norm_in():
                for c in range(DC):
                    if h_squares.n < DC:
                        act.wait_ge(x_in[c // (DC // 2)], 16)
                    else:
                        (hs_dve if c in BY_DVE else hs).past().wait()
                    if c >= 4:
                        act.wait_ge(total_step, totals.n + c - 3)
                    h_squares.by(nc.scalar.activation(sq[c % 4], h[:, c, :], ACT.Square))

            def cut_hn(late):
                for c in range(DC):
                    if c == (5 if late else 0):
                        totals.past(DC).wait()
                        stds.by(nc.scalar.activation(std[:, :], xb[:, 2, :], ACT.Sqrt, bias=eps[:, 0:1],
                                                     scale=1.0 / D))
                    raws.past().wait()
                    cut_value(hn[0][:, c, :], hn_raw[:, c, :])

            def norm_out(factor):
                totals.past().wait()
                col = 0 if factor == 1.0 else 1
                stds.by(nc.scalar.activation(std[:, 0:TT], sums, ACT.Sqrt, bias=eps[:, col:col + 1],
                                             scale=1.0 / (D * factor * factor)))
                totals.past()

            def square_y(c):
                free.past().wait()
                added.past().wait()
                y_squares.by(nc.scalar.activation(sq[out[0] % 2], y[:, c, :], ACT.Square))
                out[0] += 1

            def ffn():
                with looped(act, FC // 2, {done: 4, free: 4, parts: 2, his: 4, hid_raws: 2, hid_his: 2}, unit, 4) as it:
                    for k in range(2):
                        used()
                        free.past().wait()
                        parts.by(nc.scalar.activation(sg[:, k, :], sg[:, k, :], ACT.Silu))
                        used()
                        free.past()
                        hid_raws.past().wait()
                        hid_his.by(nc.scalar.activation(hid[0][:, it * 2 + k, :], tmp[:, k, :], ACT.Copy))
                out[0] += 2 * FC
                with looped(act, 2, {done: 12, free: 4, y_squares: 4, added: 4, his: 12}, unit, 12) as it:
                    for k in range(4):
                        used(3)
                        square_y(it * 4 + k)
                out[0] += 4

            def ple(layer):
                for c in range(DC):
                    used()
                    free.past().wait()
                    parts.by(nc.scalar.activation(gate[:, c, :], gate[:, c, :], ACT.Sigmoid))
                act.wait_ge(p_in, 16 * (layer + 1))
                for c in range(2):
                    cut_value(p_cut[0][:, c, :], p_raw[:, c, :])
                out[0] += DC
                for n in range(2):
                    used()
                    for o in range(4):
                        square_y(4 * n + o)

            def bring(kind, layer):
                if kind == "ple":
                    act.dma_start(p_raw[:, :, :], ap["p_t"][layer, :, :, :]).then_inc(p_in, 16)
                for buf, name in {"even": EVEN_ROTARY, "odd": ODD_ROTARY}.get(kind, []):
                    act.dma_start(buf, ap[name]).then_inc(rotary_in, 16)
                if kind == "even":
                    for buf, name in EVEN_FIRST:
                        act.dma_start(buf, ap[name]).then_inc(stage_in, 16)

            small, asks = Steps(act, small_act), Steps(act, dve_asks)
            curs, pairs, qs, pvs = Steps(act, cur_done), Steps(act, pair_used, 1), Steps(act, q_done), Steps(act, pv_done, 1)
            maxed, exped, probd = Steps(act, max_done), Steps(act, exp_done, 1), Steps(act, probs_done)
            flips, fliptaken, own = Steps(act, flip_done, 1), Steps(act, flip_taken, 1), Steps(act, act_step)
            gated, s5ys, scored = Steps(act, gates_done), Steps(act, s5_y_taken, 1), Steps(act, scores_done, 1)

            def attention_item(n, items, scale, probs, probs_t):
                if n < len(items):
                    maxed.past().wait()
                    w = items[n][0]
                    act.wait_ge(flip_done, flips.n)
                    exped.by(nc.scalar.activation(probs[:, n % 2, 0:w * P], scores[n % 2][:, 0:w * P], ACT.Exp,
                                                  bias=stat[:, 0, n:n + 1], scale=scale, accum_out=stat[:, 1, n:n + 1]))
                if 0 <= n - 1 < len(items):
                    m = n - 1
                    w = items[m][0]
                    flips.past().wait()
                    act.wait_ge(pv_done, pvs.n)
                    fliptaken.by(nc.scalar.activation(probs_t[:, m % 2, 0:w * P], flipped[m % 2][:, 0:w * P], ACT.Copy))
                    if m >= 1:
                        pvs.past()

            def odd():
                for c in range(8):
                    used()
                    free.past()
                    if c == 1:
                        free.wait()
                        for k in range(2):
                            h_squares.by(nc.scalar.activation(relus[k], c_kv[k], ACT.Square))
                cut_value(w_idx_cut[0][:, :, :], w_idx[:, :, :])
                totals.past(2).wait()
                stds.by(nc.scalar.activation(std[:, :], total[:, :], ACT.Sqrt, bias=eps[:, 0:1], scale=1.0 / LATENT))
                for c in range(2):
                    raws.past().wait()
                    cut_value(c_cut[0][:, c, :], c_kv[c])
                for t in range(TT - 1):
                    for n in range(IDX_HEADS * t, IDX_HEADS * (t + 1)):
                        act.wait_ge(dots_done, n + 1)
                        if n >= 2:
                            act.wait_ge(dots_used, n - 1)
                        nc.scalar.activation(relus[n % 2][:, 0:(2 + t) * P], scores[n % 2][:, 0:(2 + t) * P], ACT.Relu,
                                             scale=HD ** -0.5).then_inc(relu_done, 1)
                    used(4 if t == 0 else 1)
                free.past(12).wait()
                act.wait_ge(sel_done, TT - 1)
                items = dsa_items()
                start = scored.n
                with looped(act, 4, {maxed: 16, exped: 16, flips: 16, fliptaken: 16, pvs: 16, qs: 1, own: 1,
                                     done: 8, free: 8, his: 8, raws: 2, val_his: 2}, unit, 8) as it:
                    act.wait_ge(scores_done, it * 16 + start)
                    act.wait_ge(pv_done, pvs.n)
                    own.by(nc.scalar.activation(v_cur, v_h[:, :, bass.ds(it * 256, 256)], ACT.Copy))
                    qs.by(nc.scalar.activation(q_cur[:, :], q_rope[:, it, :], ACT.Copy))
                    used(2)
                    for n in range(len(items) + 1):
                        attention_item(n, items, DSA_SCALE, od_probs[:, 0:2, :], od_probs[:, 2:4, :])
                        if n // 4 + 1 < 4 and n % 2:
                            used()
                        if n in (11, 16):
                            raws.past().wait()
                            cut_value(od_mixed[0][:, it * 2 + (0 if n == 11 else 1), :], tmp[:, 0 if n == 11 else 1, :])
                    pvs.past()
                    free.past(8)
                out[0] += 20 + 2 * HEADS
                for c in range(DC):
                    used()
                    square_y(c)

            def even():
                for c in range(12):
                    used()
                    free.past()
                    if c == 0:
                        act.wait_ge(rotary_in, 16 * len(EVEN_ROTARY))
                        small.by(nc.scalar.activation(s5_v[:, 0, :], s5_prm[:, 2, :], ACT.Exp))
                    if c == 1:
                        asks.past().wait()
                        own.by(nc.scalar.activation(s5_v[:, 3, :], s5_v[:, 1, :], ACT.Exp))
                        own.by(nc.scalar.activation(s5_v[:, 6, :], s5_v[:, 4, :], ACT.Sin))
                        small.by(nc.scalar.activation(s5_v[:, 7, :], s5_v[:, 5, :], ACT.Sin))
                out[0] += 12
                used(3)
                act.dma_start(b_raw, ap["s5_b"]).then_inc(s5_b_in, 16)
                for t in range(TT):
                    gated.by(nc.scalar.activation(gates[:, t, :], banks[:, (out[0] + t) % BANKS, 2 * P:TM], ACT.Sigmoid))
                    free.past()
                out[0] += TT
                asks.past()
                for b in range(2):
                    asks.past().wait()
                    small.by(nc.scalar.activation(cmp_h[:, 2, 0:CMP], cmp_h[:, 1, 0:CMP], ACT.Sigmoid, scale=GELU))
                act.wait_ge(small_taken, 6)
                act.dma_start(c_all[:, :, :, :, :], ap["s5_c"]).then_inc(s5_c_in, 16)
                asks.past().wait()
                act.wait_ge(s5_c_in, 16)
                items = nsa_items()
                qs.by(nc.scalar.activation(q_cur[:, :], ev[:, 4, :], ACT.Copy, scale=HD ** -0.5))
                with looped(act, 4, {maxed: 24, exped: 24, flips: 24, fliptaken: 24, pvs: 24, qs: 1,
                                     curs: 1, own: 4, s5ys: 1}) as j:
                    for n in range(len(items) + 1):
                        attention_item(n, items, 1.0, s5w[:, 10:12, :], s5w[:, 12:14, :])
                        if n == 0:
                            s5ys.wait()
                            s5ys.past()
                            own.by(nc.scalar.activation(u_cur[:, :], ev[:, j, :], ACT.Copy))
                            own.by(nc.scalar.activation(b_cur[:, 0, :], b_t[:, 0, bass.ds(j * P, P)], ACT.Copy))
                            own.by(nc.scalar.activation(b_cur[:, 1, :], b_t[:, 1, bass.ds(j * P, P)], ACT.Copy))
                            curs.by(nc.scalar.activation(s5_pow_cur[:, :, :], s5_pow[:, bass.ds(j * 4, 4), :],
                                                         ACT.Copy))
                        if n == 1:
                            own.by(nc.scalar.activation(c_cur, c_all[:, j, :, :, :], ACT.Copy))
                    qs.by(nc.scalar.activation(q_cur[:, :], ev[:, j + 5, :], ACT.Copy, scale=HD ** -0.5))
                    pvs.past()
                scored.past(96)
                for c in range(4):
                    asks.past().wait()
                    small.by(nc.scalar.activation(sg[:, c % 2, :], s5w[:, c % 2, :], ACT.Sigmoid, scale=GELU))
                    if c >= 1:
                        raws.past().wait()
                        cut_value(z_cut[0][:, c - 1, :], ev[:, c - 1, :])
                    cut_value(mixed[0][:, c + 4, :], ev[:, c + 4, :])
                raws.past().wait()
                cut_value(z_cut[0][:, 3, :], ev[:, 3, :])
                for c in range(4):
                    if c % 2 == 0:
                        used()
                    small.by(nc.scalar.activation(sg[:, c % 2, :], banks[:, (out[0] + c) % BANKS, :], ACT.Sigmoid))
                    free.past()
                    raws.past().wait()
                    cut_value(mixed[0][:, c, :], tmp[:, c % 2, :])
                out[0] += 4
                for c in range(DC):
                    used()
                    square_y(c)

            for buf, name in CONSTS:
                act.dma_start(buf, ap[name]).then_inc(consts_in, 16)
            act.wait_ge(bank_free, BANKS)
            own.by(nc.scalar.activation(warmed[:, :], eps[:, 0:1], ACT.Sqrt))
            for n, step in enumerate(plan):
                if step[0] == "norm_in":
                    norm_in()
                    if n == 0:
                        cut_unit()
                    cut_hn(plan[n + 1][0] in LATE)
                    if plan[n + 1][0] == "ffn":
                        warm(ACT.Silu)
                    for _ in range(SLOTS - 1 if n == 0 else 0):
                        cut_unit()
                elif step[0] == "norm_out":
                    warm(ACT.Sqrt)
                    norm_out(step[2])
                    if plan[n - 1][0] == "ffn" and n + 2 < len(plan):
                        bring(*plan[n + 2][0:2])
                elif step[0] == "ffn":
                    ffn()
                elif step[0] == "even":
                    even()
                elif step[0] == "odd":
                    odd()
                elif step[0] == "ple":
                    ple(step[1])

        @block.vector
        def _(dve):
            raise_first(dve, "dve")
            done, free = Steps(dve, unit_done), Steps(dve, bank_free)
            raws, vals = Steps(dve, val_raw), Steps(dve, val_cut)
            hids, hid_his = Steps(dve, hid_done), Steps(dve, hid_hi_done)
            y_squares, added = Steps(dve, y_squared), Steps(dve, y_added)
            stds, scaled, hs = Steps(dve, std_done), Steps(dve, scaled_done), Steps(dve, h_done_dve)
            totals, diags = Steps(dve, total_step), Steps(dve, diag_done)
            cuts, val_his, hs_pool = Steps(dve, hn_cut_dve), Steps(dve, val_hi), Steps(dve, h_done)
            hid_raws = Steps(dve, hid_raw)
            parts, own = Steps(dve, act_part), Steps(dve, dve_step)
            out = [0]
            last = [None]

            def did(instruction, steps=own, k=1):
                steps.by(instruction, k)
                last[0] = steps

            def settle():
                last[0].wait()

            def looped_dve(trips, per, tail):
                settle()
                last[0] = tail
                return looped(dve, trips, per)

            def root():
                stds.past().wait()
                settle()
                did(nc.vector.reciprocal(rstd[:, :], std[:, :]))
                settle()

            def root_by_token():
                stds.past().wait()
                settle()
                did(nc.vector.reciprocal(std[:, TT:2 * TT], std[:, 0:TT]))
                settle()
                did(nc.vector.tensor_tensor(
                    rstd[:, :].rearrange("p (t q) -> p t q", t=TT),
                    ident[:, :].rearrange("p (t q) -> p t q", t=1).to_broadcast([P, TT, P]),
                    std[:, TT:2 * TT].rearrange("p (t q) -> p t q", q=1).to_broadcast([P, TT, P]), ALU.mult), diags)
                totals.past(2).wait()

            def norm_in(g, late):
                totals.past(DC)
                if not late:
                    root()
                hn_his = val_his.n

                def cut_chunk(c):
                    dve.wait_ge(val_hi, hn_his + c + 1)
                    did(nc.vector.tensor_tensor(hn[1][:, c, :], hn_raw[:, c, :], hn[0][:, c, :].bitcast(F32),
                                                ALU.subtract), cuts)

                for c in range(DC):
                    if late:
                        if g == 0:
                            dve.wait_ge(x_in[c // (DC // 2)], 16)
                        elif c in BY_POOL:
                            dve.wait_ge(h_done, hs_pool.n - len(BY_POOL) + BY_POOL.index(c) + 1)
                        did(nc.vector.tensor_scalar(hn_raw[:, c, :], h[:, c, :], gains[:, g, c:c + 1], None, ALU.mult),
                            raws)
                    else:
                        did(nc.vector.scalar_tensor_tensor(hn_raw[:, c, :], h[:, c, :], gains[:, g, c:c + 1],
                                                           rstd[:, :], ALU.mult, ALU.mult), raws)
                    if c - 1 in BY_DVE:
                        cut_chunk(c - 1)
                cut_chunk(DC - 1)
                val_his.past(DC)
                vals.past(len(BY_POOL))
                if late:
                    root()

            def norm_out(g):
                root_by_token()
                for c in range(DC):
                    if c in BY_DVE:
                        did(nc.vector.scalar_tensor_tensor(y[:, c, :], y[:, c, :], gains[:, g, c:c + 1], total[:, :],
                                                           ALU.mult, ALU.mult))
                        settle()
                        did(nc.vector.tensor_tensor(h[:, c, :], h[:, c, :], y[:, c, :], ALU.add), hs)
                    else:
                        did(nc.vector.scalar_tensor_tensor(y[:, c, :], y[:, c, :], gains[:, g, c:c + 1], total[:, :],
                                                           ALU.mult, ALU.mult), scaled)
                hs_pool.past(len(BY_POOL))
                settle()

            def clear_sum():
                settle()
                did(nc.vector.memset(ssum[:, :], 0.0))

            def plain(c, bank):
                did(nc.vector.tensor_copy(y[:, c, :], banks[:, bank, :]), free)

            def take_y(c, take=plain):
                settle()
                take(c, out[0] % BANKS)
                y_squares.past().wait()
                settle()
                did(nc.vector.tensor_tensor(ssum[:, :], ssum[:, :], sq[out[0] % 2], ALU.add), added)
                out[0] += 1

            def ffn():
                bank = out[0]
                with looped_dve(FC // 2, {done: 4, free: 4, parts: 2, hid_raws: 2, hids: 2, hid_his: 2}, hids) as it:
                    for k in range(2):
                        gate_bank, up_bank = ((bank + 2 * k + i) % BANKS for i in range(2))
                        done.past().wait()
                        settle()
                        did(nc.vector.tensor_tensor(sg[:, k, :], banks[:, gate_bank, :], rstd[:, :], ALU.mult), free)
                        done.past().wait()
                        did(nc.vector.tensor_tensor(tmp[:, k, :], banks[:, up_bank, :], rstd[:, :], ALU.mult), free)
                        parts.past().wait()
                        settle()
                        did(nc.vector.tensor_tensor(tmp[:, k, :], tmp[:, k, :], sg[:, k, :], ALU.mult), hid_raws)
                        hid_his.past().wait()
                        settle()
                        did(nc.vector.tensor_tensor(hid[1][:, it * 2 + k, :], tmp[:, k, :],
                                                    hid[0][:, it * 2 + k, :].bitcast(F32), ALU.subtract), hids)
                out[0] += 2 * FC
                clear_sum()
                with looped_dve(2, {done: 12, free: 4, y_squares: 4, added: 4}, added) as it:
                    for k in range(4):
                        done.past(3).wait()
                        take_y(it * 4 + k)
                out[0] += 4

            def ple():
                for c in range(DC):
                    done.past().wait()
                    did(nc.vector.tensor_tensor(gate[:, c, :], banks[:, (out[0] + c) % BANKS, :], rstd[:, :], ALU.mult),
                        free)
                out[0] += DC
                parts.past(DC).wait()
                vals.past(2)
                val_his.past(2)
                clear_sum()
                for c in range(DC):
                    if c % 4 == 0:
                        done.past().wait()
                    take_y(c, lambda c, bank: did(nc.vector.tensor_tensor(
                        y[:, c, :], gate[:, c, :], banks[:, bank, :], ALU.mult), free))

            turns, ropes = Steps(dve, turned), Steps(dve, roped)
            gated, blks, small_pe, taken = Steps(dve, gates_done), Steps(dve, blk_done), Steps(dve, pe_step), Steps(dve, small_taken)
            small, asks = Steps(dve, small_act), Steps(dve, dve_asks)
            bus, states, pairs, s5ys, curs = (Steps(dve, bu_done), Steps(dve, states_done, 2), Steps(dve, pair_used, 1),
                                              Steps(dve, s5_y_taken, 1), Steps(dve, cur_done))
            scored, maxed, exped, probd = (Steps(dve, scores_done, 1), Steps(dve, max_done), Steps(dve, exp_done, 1),
                                           Steps(dve, probs_done))
            pvs, os_ = Steps(dve, pv_done, 1), Steps(dve, o_taken, 1)
            turned_by = Steps(dve, rots_done)
            dots, sels = Steps(dve, dots_used), Steps(dve, sel_done)

            def tt(dst, a, b, op, steps=own, apart=False):
                if not apart:
                    settle()
                did(nc.vector.tensor_tensor(dst, a, b, op), steps)

            def ts(dst, a, s1, s2, op0, op1=None, steps=own):
                settle()
                if op1 is None:
                    did(nc.vector.tensor_scalar(dst, a, s1, None, op0), steps)
                else:
                    did(nc.vector.tensor_scalar(dst, a, s1, s2, op0, op1), steps)

            def rope_start(k, bank):
                settle()
                did(nc.vector.tensor_copy(tmp[:, k % 2, :], banks[:, bank, :]), free)

            def rope_end(k, dst, cos, sin, banks_of=(xb[:, 0, :], xb[:, 1, :])):
                turns.past().wait()
                tt(sg[:, 0, :], tmp[:, k % 2, :], cos, ALU.mult)
                tt(sg[:, 1, :], banks_of[k % 2], sin, ALU.mult)
                tt(dst, sg[:, 0, :], sg[:, 1, :], ALU.add, ropes)

            def gelu_before(x, t, ask):
                tt(t, x, x, ALU.mult)
                ts(t, t, 0.044715, 1.0, ALU.mult, ALU.add)
                tt(t, t, x, ALU.mult, ask)

            v = lambda k: s5_v[:, k, :]
            a_re, a_im = s5_prm[:, 0, :], s5_prm[:, 1, :]

            def s5_angles():
                small.past().wait()
                tt(v(1), a_re, v(0), ALU.mult)
                tt(v(2), a_im, v(0), ALU.mult)
                ts(v(8), v(2), 1 / (2 * np.pi), MAGIC, ALU.mult, ALU.add)
                ts(v(8), v(8), MAGIC, None, ALU.subtract)
                settle()
                did(nc.vector.scalar_tensor_tensor(v(9), v(8), -TWO_PI_HI, v(2), ALU.mult, ALU.add))
                settle()
                did(nc.vector.scalar_tensor_tensor(v(9), v(8), -TWO_PI_LO, v(9), ALU.mult, ALU.add))
                ts(v(4), v(9), PI_IN, -PI_IN, ALU.min, ALU.max)
                ts(v(5), v(4), -1.0, None, ALU.mult)
                tt(v(5), v(5), v(4), ALU.max)
                ts(v(5), v(5), -1.0, np.pi / 2, ALU.mult, ALU.add, asks)

            def s5_power(k):
                if k == 0:
                    small.past().wait()
                re, im = s5_pow[:, :, k], s5_pow[:, :, 9 + k]
                if k == 0:
                    cr, ci = v(7), v(6)
                else:
                    pr, pi = s5_pow[:, :, k - 1], s5_pow[:, :, 8 + k]
                    tt(v(10), pr, pr, ALU.mult)
                    tt(v(11), pi, pi, ALU.mult)
                    tt(v(12), v(10), v(11), ALU.subtract)
                    tt(v(13), pr, pi, ALU.mult)
                    ts(v(13), v(13), 2.0, None, ALU.mult)
                    cr, ci = v(12), v(13)
                tt(v(10), cr, cr, ALU.mult)
                tt(v(11), ci, ci, ALU.mult)
                tt(v(10), v(10), v(11), ALU.add)
                ts(v(10), v(10), -0.5, 1.5, ALU.mult, ALU.add)
                tt(re, cr, v(10), ALU.mult)
                tt(im, ci, v(10), ALU.mult)

            def s5_scalars():
                settle()
                did(nc.vector.tensor_copy(s5_pow[:, :, 18], v(3)))
                tt(v(14), v(3), v(7), ALU.mult)
                ts(v(14), v(14), 1.0, None, ALU.subtract)
                tt(v(15), v(3), v(6), ALU.mult)
                tt(v(16), a_re, a_re, ALU.mult)
                tt(v(17), a_im, a_im, ALU.mult)
                tt(v(16), v(16), v(17), ALU.add)
                settle()
                did(nc.vector.reciprocal(v(16), v(16)))
                tt(v(17), v(14), a_re, ALU.mult)
                tt(v(18), v(15), a_im, ALU.mult)
                tt(v(17), v(17), v(18), ALU.add)
                tt(v(17), v(17), v(16), ALU.mult)
                tt(v(18), v(15), a_re, ALU.mult)
                tt(v(19), v(14), a_im, ALU.mult)
                tt(v(18), v(18), v(19), ALU.subtract)
                tt(v(18), v(18), v(16), ALU.mult)
                col = lambda k: s5_v[:, k, :].rearrange("p (t o) -> p t o", o=1).to_broadcast([P, PAIRS, 32])
                m = lambda a: a.rearrange("p (t n) -> p t n", n=32)
                br, bi = b_raw[:, 0, :], b_raw[:, 1, :]
                dve.wait_ge(s5_b_in, 16)
                tt(m(b_parts[0]), m(br), col(17), ALU.mult)
                tt(m(b_parts[1]), m(bi), col(18), ALU.mult)
                tt(b_bar[:, 0, :], b_parts[0], b_parts[1], ALU.subtract)
                tt(m(b_parts[0]), m(bi), col(17), ALU.mult)
                tt(m(b_parts[1]), m(br), col(18), ALU.mult)
                tt(b_bar[:, 1, :], b_parts[0], b_parts[1], ALU.add, asks)

            def s5_inputs():
                small_pe.past().wait()
                settle()
                did(nc.vector.tensor_copy(b_t[:, 0, :], xb[:, 0, :]))
                did(nc.vector.tensor_copy(b_t[:, 1, :], xb[:, 1, :]), taken)
                settle()
                did(nc.vector.memset(s5_v[:, 20, :], 0.0), asks)

            def s5_part(q, j, part):
                sc = lambda k: s5_pow_cur[:, j, k:k + 1]

                rot_c, rot_s = rots[j % 2]
                dr, di = banks[:, 0, :], banks[:, 1, :]
                if part == 0:
                    if j == 0:
                        curs.past().wait()
                    bus.past().wait()
                    turned_by.past().wait()
                    tt(wk[0], dr, rot_c, ALU.mult, apart=True)
                    tt(wk[1], di, rot_s, ALU.mult, apart=True)
                    tt(wk[0], wk[0], wk[1], ALU.add)
                elif part == 1:
                    tt(wk[1], di, rot_c, ALU.mult, apart=True)
                    tt(zs[1], dr, rot_s, ALU.mult, apart=True)
                    tt(wk[1], wk[1], zs[1], ALU.subtract)
                elif part == 2:
                    decay = sc(18).to_broadcast([P, T])
                    for c in range(2):
                        did(nc.vector.tensor_tensor_scan(zs[c], decay, wk[c], 0.0, ALU.mult, ALU.add))
                else:
                    if part == 3:
                        pairs.wait()
                        pairs.past()
                        products = ((0, zs[0], rot_c, 1.0), (1, zs[1], rot_s, -1.0))
                    else:
                        products = ((2, zs[0], rot_s, -1.0), (3, zs[1], rot_c, -1.0))
                    for k, z, rot, sign in products:
                        did(nc.vector.scalar_tensor_tensor(turned_back[k], z, sign, rot, ALU.mult, ALU.mult),
                            states if k == 3 else own)

            def s5_end(q):
                pairs.wait()
                settle()
                did(nc.vector.tensor_copy(s5_d[:, 4:5], s5_d[:, bass.ds(q, 1)]))
                settle()
                did(nc.vector.scalar_tensor_tensor(ev[:, q, :], u_cur[:, :], s5_d[:, 4:5], banks[:, 3, :], ALU.mult,
                                                   ALU.add), s5ys)

            def compress():
                dve.wait_ge(stage_in, 16 * len(EVEN_FIRST))
                settle()
                did(nc.vector.tensor_copy(cmp_mask[:, :, :].rearrange("p t n -> p (t n)"), cmp_stage[:, :]))
                for b, src in enumerate((kc_t, vc_t)):
                    for a in range(2):
                        part = src[:, CMP_STRIDE * a:CMP_STRIDE * (a + CMP)].rearrange("p (c l) -> p l c", l=CMP_STRIDE)
                        pe_ = pe_t[:, b, CMP_STRIDE * a:CMP_STRIDE * (a + 1)].rearrange(
                            "p (l o) -> p l o", o=1).to_broadcast([P, CMP_STRIDE, CMP])
                        tt(blk[b][:, CMP_STRIDE * a:CMP_STRIDE * (a + 1), :], part, pe_, ALU.add, own if a == 0 else blks)
                s5_scalars()
                for b in range(2):
                    small_pe.past().wait()
                    x = cmp_h[:, 0, 0:CMP]
                    settle()
                    did(nc.vector.tensor_copy(x, xb[:, b, 0:CMP]), taken)
                    gelu_before(x, cmp_h[:, 1, 0:CMP], asks)
                    small.past().wait()
                    tt(cmp_h[:, 4 + b, 0:CMP], x, cmp_h[:, 2, 0:CMP], ALU.mult, taken)
                settle()
                did(nc.vector.memset(k_cmp[:, :], 0.0))
                settle()
                did(nc.vector.memset(v_cmp[:, :], 0.0))
                small_pe.past().wait()
                settle()
                did(nc.vector.tensor_copy(k_cmp[:, 0:CMP], xb[:, 2, 0:CMP]), taken)
                small_pe.past().wait()
                did(nc.vector.tensor_copy(v_cmp[0:CMP, :], total[0:CMP, 0:P]), taken)

            def attention_item(n, items, factor, probs):
                if n < len(items):
                    w = items[n][0]
                    scored.past().wait()
                    if factor[0] == 1.0:
                        did(nc.vector.tensor_reduce(stat[:, 0, n:n + 1], scores[n % 2][:, 0:w * P], AX.X, ALU.max,
                                                    negate=True), maxed)
                    else:
                        did(nc.vector.tensor_reduce(stat[:, 2, n:n + 1], scores[n % 2][:, 0:w * P], AX.X, ALU.max))
                        ts(stat[:, 0, n:n + 1], stat[:, 2, n:n + 1], -factor[0], None, ALU.mult, None, maxed)
                if 0 <= n - 1 < len(items):
                    m = n - 1
                    w = items[m][0]
                    exped.past().wait()
                    did(nc.vector.reciprocal(stat[:, 2, m:m + 1], stat[:, 1, m:m + 1]))
                    if factor[1]:
                        ts(probs[:, m % 2, 0:w * P], probs[:, m % 2, 0:w * P], stat[:, 2, m:m + 1], factor[1](m), ALU.mult,
                           ALU.mult, probd)
                    else:
                        ts(probs[:, m % 2, 0:w * P], probs[:, m % 2, 0:w * P], stat[:, 2, m:m + 1], None, ALU.mult, None,
                           probd)

            def nsa_and_s5():
                for qt in range(TT):
                    g3 = gates[:, qt, :].rearrange("p (h b) -> p h b", b=3)[:, :, 0]
                    ts(g3, g3, row_valid[:, qt:qt + 1], None, ALU.mult)
                items = nsa_items()
                with looped_dve(4, {scored: 24, maxed: 24, exped: 24, probd: 24, own: 24 + OWN_S5, pvs: 24, os_: 1,
                                    curs: 1, bus: 4, turned_by: 4, states: 4, pairs: 4, s5ys: 1}, os_) as j:
                    def factor(m):
                        w, half, qt, br = items[m]
                        return gates[:, qt, bass.ds(j * 3 + (12 * half + br), 1)]
                    for n in range(len(items) + 1):
                        attention_item(n, items, (1.0, factor), s5w[:, 10:12, :])
                        if 2 <= n < 22:
                            s5_part(j, (n - 2) // 5, (n - 2) % 5)
                        if n == 24:
                            s5_end(j)
                    pvs.past(24).wait()
                    settle()
                    did(nc.vector.tensor_copy(ev[:, j + 4, :], banks[:, 2, :]), os_)

            def index(beside):
                small_pe.past().wait()
                ts(idx_w[:, :, :], xb[:, 2, 0:8 * (TT - 1)].rearrange("p (t h) -> p t h", h=8), IDX_HEADS ** -0.5, None,
                   ALU.mult, None, taken)
                root()
                totals.past(2)
                for c in range(2):
                    did(nc.vector.scalar_tensor_tensor(c_kv[c], c_kv[c], kv_gain[:, c:c + 1], rstd[:, :], ALU.mult,
                                                       ALU.mult), raws)
                vals.past(3)
                val_his.past(3)
                for t in range(TT - 1):
                    w = (2 + t) * P
                    for i in range(IDX_HEADS):
                        n = IDX_HEADS * t + i
                        dve.wait_ge(relu_done, n + 1)
                        settle()
                        if i == 0:
                            used = nc.vector.tensor_scalar(score[:, 0:w], relus[n % 2][:, 0:w], idx_w[:, t, i:i + 1], None,
                                                           ALU.mult)
                        else:
                            used = nc.vector.scalar_tensor_tensor(score[:, 0:w], relus[n % 2][:, 0:w], idx_w[:, t, i:i + 1],
                                                                  score[:, 0:w], ALU.mult, ALU.add)
                        did(used, dots)
                    tt(score[:, w - P:w], score[:, w - P:w], causal_b[:, :], ALU.add)
                    left = sg[:, 0, 0:w]
                    settle()
                    did(nc.vector.tensor_copy(left, score[:, 0:w]))
                    for _ in range(ROUNDS - 1):
                        settle()
                        did(nc.vector.max(top8[:, :], left))
                        settle()
                        did(nc.vector.match_replace(left, top8[:, :], left, LOW))
                    settle()
                    did(nc.vector.max(top8[:, :], left))
                    least = top8[:, 7:8]
                    more, equal, rank = found[:, 0:w], sg[:, 1, 0:w], sg[:, 0, 0:w]
                    ts(more, score[:, 0:w], least, None, ALU.is_gt)
                    settle()
                    did(nc.vector.tensor_reduce(count[:, 0:1], more, AX.X, ALU.add))
                    ts(count[:, 1:2], count[:, 0:1], -1.0, float(TOP), ALU.mult, ALU.add)
                    ts(equal, score[:, 0:w], least, None, ALU.is_equal)
                    settle()
                    did(nc.vector.tensor_tensor_scan(rank, ones[:, 0:1].to_broadcast([P, w]), equal, 0.0, ALU.mult, ALU.add))
                    settle()
                    did(nc.vector.scalar_tensor_tensor(rank, rank, count[:, 1:2], equal, ALU.is_le, ALU.mult))
                    tt(more, more, rank, ALU.add)
                    ts(sel_mask[:, t, 0:w], more, 1.0, -NEG, ALU.subtract, ALU.mult, sels)
                    beside(t)

            def odd():
                dests = c_kv + [k_rope, k_idx] + q_idx + [q_rope[:, c, :] for c in range(4)]
                rotary = lambda c: (od_rot[:, 2, :], od_rot[:, 3, :]) if c in NARROW else (od_rot[:, 0, :], od_rot[:, 1, :])
                project(8, ODD_ROPED, dests, rotary)

                def beside(t):
                    if t == 0:
                        for c in range(8, 12):
                            done.past().wait()
                            k = ODD_ROPED.index(c)
                            rope_start(k, (out[0] + c - 8) % BANKS)
                            if c > 8:
                                rope_end(k - 1, dests[c - 1], *rotary(c - 1), banks_of=turned_apart)
                        rope_end(k, dests[c], *rotary(c), banks_of=turned_apart)
                        out[0] += 4
                        return
                    done.past().wait()
                    for tile in range(TT):
                        settle()
                        did(nc.vector.tensor_copy(v_h[:, tile, (t - 1) * T:t * T], banks[:, (out[0] + tile) % BANKS, :]),
                            free)
                    out[0] += TT

                index(beside)
                items = dsa_items()
                with looped_dve(4, {scored: 16, maxed: 16, exped: 16, probd: 16, own: 32, pvs: 16, raws: 2, vals: 2,
                                    done: 8, free: 8}, raws) as it:
                    def query(j, o):
                        done.past().wait()
                        settle()
                        did(nc.vector.tensor_copy(q_lat[j % 2][:, o, :], banks[:, o, :]), free)

                    for o in range(2):
                        query(0, o)
                    for n in range(len(items) + 1):
                        attention_item(n, items, (DSA_SCALE, None), od_probs[:, 0:2, :])
                        if n // 4 + 1 < 4 and n % 2:
                            query(n // 4 + 1, n % 4 // 2)
                        if n in (10, 16):
                            pvs.past(8).wait()
                            vals.wait()
                            settle()
                            did(nc.vector.tensor_copy(tmp[:, 0 if n == 10 else 1, :],
                                                      banks[:, 2 if n == 10 else 3, :]), raws)
                            vals.past()
                out[0] += 2 * HEADS
                val_his.past(8)
                clear_sum()
                for c in range(DC):
                    done.past().wait()
                    take_y(c)

            def project(units, roped_chunks, dests, rotary_of, between={}):
                waiting = []
                vals.wait()
                dve.wait_ge(rotary_in, 16 * len(EVEN_ROTARY if roped_chunks is EVEN_ROPED else
                                                EVEN_ROTARY + ODD_ROTARY))

                def end():
                    c = waiting.pop()
                    rope_end(roped_chunks.index(c), dests[c], *rotary_of(c))

                for c in range(units):
                    done.past().wait()
                    bank = (out[0] + c) % BANKS
                    if c in roped_chunks:
                        rope_start(roped_chunks.index(c), bank)
                    else:
                        settle()
                        did(nc.vector.tensor_copy(dests[c], banks[:, bank, :]), free)
                    if waiting:
                        end()
                    if c in roped_chunks:
                        waiting.append(c)
                    if c in between:
                        between[c]()
                end()
                out[0] += units

            def even():
                dests = [ev[:, c, :] for c in range(4)] + q_t + [kc_t, vc_t, ks_t, kw_t]
                between = {0: s5_angles, **{3 + k: partial(s5_power, k) for k in range(POW)}}
                project(12, EVEN_ROPED, dests, lambda c: (ev_rot[:, 0, :], ev_rot[:, 1, :]), between)
                done.past(3).wait()
                for t in range(TT):
                    gated.past().wait()
                    settle()
                    did(nc.vector.tensor_copy(v_tm[:, t, :], banks[:, (out[0] + t) % BANKS, 0:2 * P]), free)
                out[0] += TT
                compress()
                s5_inputs()
                nsa_and_s5()
                for c in range(4):
                    if c >= 1:
                        small.past().wait()
                        tt(ev[:, c - 1, :], ev[:, c - 1, :], sg[:, (c - 1) % 2, :], ALU.mult, raws)
                    gelu_before(ev[:, c, :], s5w[:, c % 2, :], asks)
                small.past().wait()
                tt(ev[:, 3, :], ev[:, 3, :], sg[:, 1, :], ALU.mult, raws)
                vals.past(8)
                val_his.past(12)
                for c in range(4):
                    if c % 2 == 0:
                        done.past()
                    small.past().wait()
                    if c >= 2:
                        dve.wait_ge(val_cut, vals.n + c - 1)
                    settle()
                    did(nc.vector.tensor_tensor(tmp[:, c % 2, :], ev[:, c, :], sg[:, c % 2, :], ALU.mult), raws)
                    settle()
                    did(nc.vector.memset(stat[:, 0, 0:1], 0.0), free)
                vals.past(4)
                out[0] += 4
                clear_sum()
                for c in range(DC):
                    done.past().wait()
                    take_y(c)

            did(nc.vector.memset(eps[:, 0:1], EPS))
            did(nc.vector.memset(eps[:, 1:2], 4 * EPS))
            did(nc.vector.memset(ones[:, :], 1.0), free, BANKS)
            did(nc.vector.memset(ssum[:, :], 0.0), added, 2)
            dve.wait_ge(consts_in, 16 * len(CONSTS))
            did(nc.vector.tensor_copy(causal_b[:, :], rstd[:, 0:P]))
            did(nc.vector.tensor_copy(ident_b[:, :], ident[:, :]))
            for n, step in enumerate(plan):
                if step[0] == "norm_in":
                    norm_in(step[1], plan[n + 1][0] in LATE)
                elif step[0] == "norm_out":
                    norm_out(step[1])
                elif step[0] == "ffn":
                    ffn()
                elif step[0] == "even":
                    even()
                elif step[0] == "odd":
                    odd()
                elif step[0] == "ple":
                    ple()

        @block.gpsimd
        def _(pool):
            scaled, hs = Steps(pool, scaled_done), Steps(pool, h_done)
            his, los = Steps(pool, w_hi_done), Steps(pool, w_lo_done)
            val_his, vals = Steps(pool, val_hi), Steps(pool, val_cut)
            unit = Feed()

            def cut_unit(n=1):
                for _ in range(n):
                    if unit.it is None and unit.u >= n_units:
                        return
                    his.past().wait()
                    slot = unit.slot()
                    los.by(nc.gpsimd.tensor_tensor(w_lo[:, slot, :], raw[:, slot, :], w_hi[:, slot, :].bitcast(F32),
                                                   ALU.subtract))
                    unit.next()

            def cut_value(pair, src, *index):
                val_his.past().wait()
                hi, lo = cut(pair, *index)
                vals.by(nc.gpsimd.tensor_tensor(lo, src, hi.bitcast(F32), ALU.subtract))

            every = slice(None)
            rotated, states, own = (Steps(pool, rots_done), Steps(pool, states_done, 2),
                                          Steps(pool, pool_step))

            def rotation(trip, q):
                both = (s5w[:, 0:2, :], sg[:, 0:2, :])[q % 2]
                c, s = both[:, 0, :], both[:, 1, :]
                halves = lambda a: a.rearrange("p (c t) -> p c t", c=2)
                by_cos, by_sin = halves(std[:, :]), halves(tmp[:, 1, :])

                def step(dst, a, b, op):
                    own.by(nc.gpsimd.tensor_tensor(dst, a, b, op))

                one = ones[:, 0:1]
                step(c[:, 0:1], one, one, ALU.mult)
                step(s[:, 0:1], one, one, ALU.subtract)
                for k in range(POW):
                    m = 1 << k
                    power = lambda at: s5_pow[:, bass.ds(trip * 4 + q, 1), at:at + 1].to_broadcast([P, 2, m])
                    own.wait()
                    step(by_cos[:, :, 0:m], both[:, :, 0:m], power(k), ALU.mult)
                    step(by_sin[:, :, 0:m], both[:, :, 0:m], power(9 + k), ALU.mult)
                    own.wait()
                    step(s[:, m:2 * m], by_cos[:, 1, 0:m], by_sin[:, 0, 0:m], ALU.add)
                    rotated_by = nc.gpsimd.tensor_tensor(c[:, m:2 * m], by_cos[:, 0, 0:m], by_sin[:, 1, 0:m],
                                                         ALU.subtract)
                    if k < POW - 1:
                        own.by(rotated_by)
                rotated.by(rotated_by)

            def norm_in():
                for c in range(DC):
                    if c in BY_DVE:
                        val_his.past()
                    else:
                        cut_value(hn, hn_raw[:, c, :], every, c, every)

            def norm_out():
                for c in BY_POOL:
                    scaled.past().wait()
                    hs.by(nc.gpsimd.tensor_tensor(h[:, c, :], h[:, c, :], y[:, c, :], ALU.add))

            def ffn():
                with looped(pool, FC // 2, {his: 4, los: 4}, unit, 4):
                    cut_unit(4)
                with looped(pool, 2, {his: 12, los: 12}, unit, 12):
                    cut_unit(12)

            def ple():
                cut_unit(DC)
                for c in range(2):
                    cut_value(p_cut, p_raw[:, c, :], every, c, every)
                cut_unit(2)

            def even():
                cut_unit(15)
                pool.wait_ge(dve_asks, 5)
                with looped(pool, 4, {rotated: 4, states: 4, own: 4 * (4 * POW + 1)}) as j:
                    for q in range(4):
                        pool.wait_ge(states_done, states.n - 1)
                        rotation(j, q)
                        states.past()
                for c in range(4):
                    if c >= 1:
                        cut_value(z_cut, ev[:, c - 1, :], every, c - 1, every)
                    cut_value(mixed, ev[:, c + 4, :], every, c + 4, every)
                cut_value(z_cut, ev[:, 3, :], every, 3, every)
                for c in range(4):
                    if c % 2 == 0:
                        cut_unit()
                    cut_value(mixed, tmp[:, c % 2, :], every, c, every)
                cut_unit(DC)

            def odd():
                cut_unit(8)
                cut_value(w_idx_cut, w_idx[:, :, :], every, every, every)
                for c in range(2):
                    cut_value(c_cut, c_kv[c], every, c, every)
                cut_unit(6)
                with looped(pool, 4, {his: 8, los: 8, val_his: 2, vals: 2}, unit, 8) as it:
                    cut_unit(2)
                    for n in range(17):
                        if n // 4 + 1 < 4 and n % 2:
                            cut_unit()
                        if n in (11, 16):
                            cut_value(od_mixed, tmp[:, 0 if n == 11 else 1, :], every, it * 2 + (0 if n == 11 else 1), every)
                cut_unit(DC)

            cut_unit()
            norm_in()
            cut_unit(SLOTS - 1)
            stages = {"norm_in": norm_in, "norm_out": norm_out, "ffn": ffn, "even": even, "odd": odd, "ple": ple}
            for step in plan[1:]:
                stages[step[0]]()


def tables():
    def rotary(width):
        half = width // 2
        inv = np.float32(10000.0) ** (-np.arange(half, dtype=np.float32) / np.float32(half))
        angle = np.arange(T, dtype=np.float32)[:, None] * inv[None, :].astype(np.float32)
        rows = np.arange(P) % half
        turn = np.zeros((P, P), np.float32)
        for m in range(P):
            low = m % width < half
            turn[m + half if low else m - half, m] = -1.0 if low else 1.0
        return (np.ascontiguousarray(np.cos(angle).T[rows]), np.ascontiguousarray(np.sin(angle).T[rows]), turn)

    cos64, sin64, turn64 = rotary(HD)
    cos32, sin32, turn32 = rotary(32)
    at = np.arange(P)
    causal = np.where(at[None, :] <= at[:, None], 0.0, NEG).astype(np.float32)
    token = np.arange(T).reshape(TT, P).T
    last = at * CMP_STRIDE + CMP_LEN - 1
    seen = (at[None, None, :] < CMP) & (last[None, None, :] <= token[:, :, None])
    return {
        "cos32": cos32, "sin32": sin32, "turn32": turn32, "cos64": cos64, "sin64": sin64, "turn64": turn64, "ident": np.eye(P, dtype=np.float32),
        "causal": causal,
        "cmp_mask": np.where(seen, 0.0, NEG).astype(np.float32).reshape(P, TT * P),
        "row_valid": (token >= CMP_LEN - 1).astype(np.float32),
    }


def lay(inputs):
    def blocks(w, cols):
        k, n = w.shape
        units = w.reshape(k // P, P, n // cols, cols).transpose(2, 1, 0, 3).reshape(n // cols, P, (k // P) * cols)
        return np.pad(units, ((0, 0), (0, 0), (0, UNIT - units.shape[2])))

    def chunks(t):
        return np.ascontiguousarray(t.T.reshape(t.shape[1] // P, P, t.shape[0]).transpose(1, 0, 2))

    def gate_up(w):
        return blocks(w.reshape(D, 2, FC, P).transpose(0, 2, 1, 3).reshape(D, 2 * FF), P)

    def rows(w, n, cols):
        k, width = w.shape
        whole = np.pad(w, ((0, -k % (n * P)), (0, 0)))
        parts = np.stack([blocks(part, cols) for part in np.split(whole, whole.shape[0] // (n * P))], axis=1)
        return parts.reshape(-1, P, UNIT)

    ev = inputs["ev_w_in"][0]
    q_cols = ev[:, 512:1024].reshape(D, 2, 4, HD).transpose(0, 2, 1, 3).reshape(D, 512)
    ev_out = inputs["ev_w_out"][0]
    nsa_rows = ev_out[512:].reshape(2, 4, HD, D).transpose(1, 0, 2, 3).reshape(512, D)

    def two(w):
        z = np.zeros(w.shape[:-2] + (P, P), w.dtype)
        z[..., 0:HD, 0:HD] = w
        z[..., HD:, HD:] = w
        return z

    w1s = np.stack([two(inputs[n][0].reshape(CMP_LEN, HD, HD)).transpose(1, 0, 2).reshape(P, CMP_LEN * P)
                    for n in ("nsa_wk1", "nsa_wv1")])
    w2s = np.stack([two(inputs[n][0]) for n in ("nsa_wk2", "nsa_wv2")], axis=1)
    pes = np.stack([np.tile(inputs[n][0].T, (2, 1)) for n in ("nsa_pe_k", "nsa_pe_v")], axis=1)

    def states(t):
        return t.reshape(PAIRS, P).T

    s5_prm = np.stack([states(inputs["s5_a_re"][0]), states(inputs["s5_a_im"][0]),
                       states(np.repeat(inputs["s5_log_dt"][0][:, None], STATES, axis=1))], axis=1)
    s5_b = np.zeros((2, STATES, 2, PAIRS, 2, 16), np.float32)
    s5_c = np.zeros((4, 2, STATES, 2, 4, 8, 16), np.float32)
    for c, part in enumerate(("re", "im")):
        b = inputs[f"s5_b_{part}"][0].reshape(PAIRS, 2, STATES, 16)
        cc = inputs[f"s5_c_{part}"][0].reshape(4, 4, 2, 16, STATES)
        for g in range(2):
            s5_b[g, :, c, :, g, :] = b[:, g].transpose(1, 0, 2)
            for j in range(4):
                s5_c[:, g, :, c, j, 2 * j + g, :] = cc[:, j, g].transpose(0, 2, 1)

    od = inputs["od_w_in"][0]
    k_rope, k_idx = od[:, 4864:4896], od[:, 5408:5472]
    odd_in = np.concatenate([od[:, 4608:4864], k_rope, k_rope, k_rope, k_rope, k_idx, k_idx, od[:, 4896:5408],
                             od[:, 4096:4608]], axis=1)

    even = [blocks(np.concatenate([ev[:, 0:512], q_cols, ev[:, 1024:1408], ev[:, 1536:1664]], axis=1), P),
            rows(np.concatenate([ev[:, 1408:1536], ev[:, 1664:1792], ev[:, 1792:1816]], axis=1), 3, TM),
            blocks(inputs["s5_w_glu"][0], 2 * P), blocks(np.concatenate([ev_out[0:512], nsa_rows]), P)]
    odd = [blocks(odd_in, P), blocks(inputs["od_w_uv"][0].transpose(1, 0, 2).reshape(2 * P, D), T),
           blocks(od[:, 0:4096], P), blocks(inputs["od_w_out"][0], P)]
    units = []
    for layer, mixer in enumerate((even, odd)):
        units += [gate_up(inputs["ffn1_w_in"][layer]), rows(inputs["ffn1_w_out"][layer], DC, P), *mixer,
                  gate_up(inputs["ffn2_w_in"][layer]), rows(inputs["ffn2_w_out"][layer], DC, P),
                  blocks(inputs["ple_w_gate"][layer], P), blocks(inputs["ple_w_proj"][layer], T)]
    return {
        "x_t": chunks(inputs["x"][0]),
        "p_t": np.stack([chunks(inputs["p"][layer, 0]) for layer in range(2)]),
        "gains": np.ascontiguousarray(inputs["norm_g"].reshape(16, DC, P).transpose(2, 0, 1)),
        **tables(),
        "weights": np.concatenate(units),
        "w1_k": w1s[0].reshape(P, CMP_LEN, P), "w1_v": w1s[1].reshape(P, CMP_LEN, P),
        "w2": np.ascontiguousarray(w2s), "pe_t": np.ascontiguousarray(pes),
        "s5_prm": np.ascontiguousarray(s5_prm), "s5_d": np.ascontiguousarray(inputs["s5_d"][0].reshape(4, P).T),
        "s5_b": s5_b.reshape(P, 2, T),
        "s5_c": np.ascontiguousarray(s5_c.reshape(4, P, 2, 4, P).transpose(1, 0, 2, 3, 4)),
        "kv_gain": np.ascontiguousarray(inputs["od_kv_norm"][0].reshape(2, P).T),
        "w_idx": np.ascontiguousarray(od[:, 5472:5480].reshape(DC, P, IDX_HEADS).transpose(1, 0, 2)),
    }


def kernel(**inputs):
    import concourse.bacc as bacc
    from concourse.bass_utils import run_bass_kernel_spmd

    nc = bacc.Bacc("TRN2", target_bir_lowering=False, num_devices=1)
    arrays = lay({k: np.asarray(v) for k, v in inputs.items()})
    ap = {name: nc.dram_tensor("in_" + name, a.shape, mybir.dt.from_np(a.dtype), kind="ExternalInput").ap()
          for name, a in arrays.items()}
    ap["out_t"] = nc.dram_tensor("out_t", (P, DC, T), F32, kind="ExternalOutput").ap()
    trunk(nc, ap)
    got = run_bass_kernel_spmd(nc, [{"in_" + n: a for n, a in arrays.items()}], core_ids=[0]).results[0]["out_t"]
    return np.ascontiguousarray(np.asarray(got).transpose(2, 1, 0).reshape(1, T, D))
```
